# Optimizing a Trainium2 kernel written in Bass

```python
import math
import jax, jax.numpy as jnp
from jax import lax
import numpy as np

D_MODEL = 1024
BATCH = 1
SEQ = 1024
DEPTH = 1

MIX_WIDTH = D_MODEL
GDN_WIDTH = MIX_WIDTH // 2
GDN_HEAD_DIM = 64
GDN_HEADS = GDN_WIDTH // GDN_HEAD_DIM
GDN_CHUNK = 64
CONV_K = 5
SGU_WIDTH = MIX_WIDTH - GDN_WIDTH
SGU_GROUPS = 4
SGU_GROUP_DIM = SGU_WIDTH // SGU_GROUPS
SGU_CHUNK = 128
FF_DIM = 4 * D_MODEL
EPS = 1e-6

SPLIT_SIZES = (GDN_WIDTH, GDN_WIDTH, GDN_WIDTH, GDN_WIDTH,
               GDN_HEADS, GDN_HEADS, GDN_HEADS, GDN_HEADS,
               SGU_WIDTH, SGU_WIDTH)
SPLIT_POINTS = tuple(int(s) for s in np.cumsum(SPLIT_SIZES)[:-1])
IN_COLS = sum(SPLIT_SIZES)


def rms_norm(x, gain):
    xf = x.astype(jnp.float32)
    y = xf * lax.rsqrt(jnp.mean(xf * xf, axis=-1, keepdims=True) + EPS)
    return (y * gain.astype(jnp.float32)).astype(x.dtype)

def l2_normalize(x):
    return x * lax.rsqrt(jnp.sum(x * x, axis=-1, keepdims=True) + EPS)

def short_conv(x, w):
    c = x.shape[-1]
    return lax.conv_general_dilated(
        x, w[:, None, :].astype(x.dtype), window_strides=(1,),
        padding=[(CONV_K // 2, CONV_K // 2)],
        dimension_numbers=("NWC", "WIO", "NWC"), feature_group_count=c)

def gated_delta_rule_chunked(q, k, v, g, beta):
    bsz, nh, s, dk = q.shape
    dv = v.shape[-1]
    n = s // GDN_CHUNK
    q = q * (dk ** -0.5)

    def chunks(t):
        return t.reshape(bsz, nh, n, GDN_CHUNK, *t.shape[3:])

    q, k, v, g, beta = chunks(q), chunks(k), chunks(v), chunks(g), chunks(beta)
    g = jnp.cumsum(g, axis=-1)
    tri_incl = jnp.tril(jnp.ones((GDN_CHUNK, GDN_CHUNK), dtype=bool))
    tri_strict = jnp.tril(jnp.ones((GDN_CHUNK, GDN_CHUNK), dtype=bool), -1)
    diff = g[..., :, None] - g[..., None, :]
    decay = jnp.exp(jnp.where(tri_incl, diff, -jnp.inf))

    k_beta = k * beta[..., None]
    v_beta = v * beta[..., None]
    lower = jnp.where(tri_strict, jnp.einsum("bhnid,bhnjd->bhnij", k_beta, k) * decay, 0.0)
    a_mat = jnp.eye(GDN_CHUNK, dtype=jnp.float32) + lower
    rhs = jnp.concatenate([v_beta, k_beta * jnp.exp(g)[..., None]], axis=-1)
    sol = lax.linalg.triangular_solve(a_mat, rhs, left_side=True, lower=True, unit_diagonal=True)
    u_c, w_c = sol[..., :dv], sol[..., dv:]

    attn_intra = jnp.einsum("bhnid,bhnjd->bhnij", q, k) * decay
    q_dec = q * jnp.exp(g)[..., None]
    k_dec = k * jnp.exp(g[..., -1:] - g)[..., None]
    g_last = jnp.exp(g[..., -1])

    def step(state, inp):
        u_i, w_i, q_i, k_i, a_i, gl = inp
        v_new = u_i - jnp.einsum("bhid,bhde->bhie", w_i, state)
        o_i = jnp.einsum("bhid,bhde->bhie", q_i, state) + jnp.einsum("bhij,bhje->bhie", a_i, v_new)
        state = state * gl[..., None, None] + jnp.einsum("bhid,bhie->bhde", k_i, v_new)
        return state, o_i

    xs = tuple(jnp.moveaxis(t, 2, 0) for t in (u_c, w_c, q_dec, k_dec, attn_intra, g_last))
    state0 = jnp.zeros((bsz, nh, dk, dv), jnp.float32)
    _, o = lax.scan(step, state0, xs)
    return jnp.moveaxis(o, 0, 2).reshape(bsz, nh, s, dv)

def bidir_gated_deltanet(qkv, z, b_f, b_b, a_f, a_b, a_log_f, dt_bias_f, a_log_b, dt_bias_b, norm_gain):
    bsz, s, _ = qkv.shape
    q, k, v = jnp.split(qkv.astype(jnp.float32), 3, axis=-1)

    def heads(t):
        return t.reshape(bsz, s, GDN_HEADS, GDN_HEAD_DIM).transpose(0, 2, 1, 3)

    q, k, v = l2_normalize(heads(q)), l2_normalize(heads(k)), heads(v)

    def gates(b, a, a_log, dt_bias):
        beta = jax.nn.sigmoid(b.astype(jnp.float32)).transpose(0, 2, 1)
        g = -jnp.exp(a_log.astype(jnp.float32)) * jax.nn.softplus(
            a.astype(jnp.float32) + dt_bias.astype(jnp.float32))
        return g.transpose(0, 2, 1), beta

    g_f, beta_f = gates(b_f, a_f, a_log_f, dt_bias_f)
    g_b, beta_b = gates(b_b, a_b, a_log_b, dt_bias_b)
    o_fwd = gated_delta_rule_chunked(q, k, v, g_f, beta_f)
    flip = lambda t: jnp.flip(t, axis=2)
    o_bwd = flip(gated_delta_rule_chunked(flip(q), flip(k), flip(v), flip(g_b), flip(beta_b)))
    o = (o_fwd + o_bwd).transpose(0, 2, 1, 3)
    zf = z.astype(jnp.float32).reshape(bsz, s, GDN_HEADS, GDN_HEAD_DIM)
    o = rms_norm(o, norm_gain) * jax.nn.silu(zf)
    return o.reshape(bsz, s, GDN_WIDTH).astype(z.dtype)

def spatial_gating(u, v, v_gain, w_s, b_s, out_gain):
    bsz, s, _ = u.shape
    u = jax.nn.gelu(u, approximate=False).reshape(bsz, s, SGU_GROUPS, SGU_GROUP_DIM)
    v = jax.nn.gelu(v, approximate=False).reshape(bsz, s, SGU_GROUPS, SGU_GROUP_DIM)
    v = rms_norm(v, v_gain).reshape(bsz, s // SGU_CHUNK, SGU_CHUNK, SGU_GROUPS, SGU_GROUP_DIM)
    mixed = jnp.einsum("gts,bnsgc->bntgc", w_s, v) + b_s.T[:, :, None]
    gated = u * mixed.reshape(bsz, s, SGU_GROUPS, SGU_GROUP_DIM)
    return rms_norm(gated, out_gain).reshape(bsz, s, SGU_WIDTH)

def first_inputs(seed: int = 0) -> dict:
    key = jax.random.key(seed)
    ks = jax.random.split(key, 20)
    f32 = jnp.float32
    L = DEPTH
    x = jax.random.normal(ks[0], (BATCH, SEQ, D_MODEL), f32)
    norm_mix = 1.0 + 0.02 * jax.random.normal(ks[1], (L, D_MODEL), f32)
    w_in = jax.random.normal(ks[2], (L, D_MODEL, IN_COLS), f32) * D_MODEL ** -0.5
    conv_w = jax.random.normal(ks[3], (L, CONV_K, 3 * GDN_WIDTH), f32) * CONV_K ** -0.5

    def decay_params(k_a, k_dt):
        a_log = jnp.log(jax.random.uniform(k_a, (L, GDN_HEADS), f32, 1.0, 16.0))
        dt = jnp.exp(jax.random.uniform(k_dt, (L, GDN_HEADS), f32, math.log(1e-3), math.log(1e-1)))
        dt_bias = dt + jnp.log(-jnp.expm1(-dt))
        return a_log, dt_bias

    a_log_fwd, dt_bias_fwd = decay_params(ks[4], ks[5])
    a_log_bwd, dt_bias_bwd = decay_params(ks[6], ks[7])
    gdn_norm = 1.0 + 0.02 * jax.random.normal(ks[8], (L, GDN_HEAD_DIM), f32)
    sgu_v_norm = 1.0 + 0.02 * jax.random.normal(ks[9], (L, SGU_GROUPS, SGU_GROUP_DIM), f32)
    sgu_w = jax.random.normal(ks[10], (L, SGU_GROUPS, SGU_CHUNK, SGU_CHUNK), f32) * SGU_CHUNK ** -0.5
    sgu_b = 1.0 + 0.02 * jax.random.normal(ks[11], (L, SGU_GROUPS, SGU_CHUNK), f32)
    sgu_out_norm = 1.0 + 0.02 * jax.random.normal(ks[12], (L, SGU_GROUPS, SGU_GROUP_DIM), f32)
    w_out = jax.random.normal(ks[13], (L, MIX_WIDTH, D_MODEL), f32) * MIX_WIDTH ** -0.5
    norm_ffn = 1.0 + 0.02 * jax.random.normal(ks[14], (L, D_MODEL), f32)
    w_ff1 = jax.random.normal(ks[15], (L, D_MODEL, FF_DIM), f32) * D_MODEL ** -0.5
    w_ff2 = jax.random.normal(ks[16], (L, FF_DIM, D_MODEL), f32) * FF_DIM ** -0.5
    norm_final = 1.0 + 0.02 * jax.random.normal(ks[17], (D_MODEL,), f32)
    return {"x": x, "norm_mix": norm_mix, "w_in": w_in, "conv_w": conv_w,
            "a_log_fwd": a_log_fwd, "dt_bias_fwd": dt_bias_fwd,
            "a_log_bwd": a_log_bwd, "dt_bias_bwd": dt_bias_bwd,
            "gdn_norm": gdn_norm, "sgu_v_norm": sgu_v_norm, "sgu_w": sgu_w, "sgu_b": sgu_b,
            "sgu_out_norm": sgu_out_norm, "w_out": w_out, "norm_ffn": norm_ffn,
            "w_ff1": w_ff1, "w_ff2": w_ff2, "norm_final": norm_final}

def first_block(x, norm_mix, w_in, conv_w, a_log_fwd, dt_bias_fwd, a_log_bwd, dt_bias_bwd,
              gdn_norm, sgu_v_norm, sgu_w, sgu_b, sgu_out_norm, w_out, norm_ffn,
              w_ff1, w_ff2, norm_final):
    for l in range(DEPTH):
        h = rms_norm(x, norm_mix[l])
        proj = jnp.einsum("bsd,dc->bsc", h, w_in[l])
        q, k, v, z, b_f, b_b, a_f, a_b, su, sv = jnp.split(proj, SPLIT_POINTS, axis=-1)
        qkv = jax.nn.silu(short_conv(jnp.concatenate([q, k, v], axis=-1), conv_w[l]))
        o_a = bidir_gated_deltanet(qkv, z, b_f, b_b, a_f, a_b, a_log_fwd[l], dt_bias_fwd[l],
                                   a_log_bwd[l], dt_bias_bwd[l], gdn_norm[l])
        o_b = spatial_gating(su, sv, sgu_v_norm[l], sgu_w[l], sgu_b[l], sgu_out_norm[l])
        mix = jnp.concatenate([o_a, o_b], axis=-1)
        x = x + jnp.einsum("bsc,cd->bsd", mix, w_out[l])
        h = rms_norm(x, norm_ffn[l])
        ff = jnp.square(jax.nn.relu(jnp.einsum("bsd,df->bsf", h, w_ff1[l])))
        x = x + jnp.einsum("bsf,fd->bsd", ff, w_ff2[l])
    return rms_norm(x, norm_final)


_first_inputs = first_inputs


def first_inputs(seed=0):
    import zlib

    import numpy as np

    out = dict(_first_inputs(seed))
    spreads = {}
    factors = {'gdn_norm': 8.0,
     'sgu_v_norm': 6.292,
     'sgu_b': 7.79,
     'sgu_out_norm': 4.892,
     'norm_ffn': 3.634,
     'norm_final': 2.865}
    for name, (base, spread) in spreads.items():
        noise = np.random.default_rng([zlib.crc32(name.encode()), seed]).standard_normal(out[name].shape)
        drawn = base * np.exp(spread * noise) if base else spread * noise
        out[name] = __import__('jax').numpy.asarray(drawn.astype(out[name].dtype))
    for name, factor in factors.items():
        out[name] = (out[name] * factor).astype(out[name].dtype)
    return out


_narrow_inputs = first_inputs


def first_inputs(seed=0):

    out = dict(_narrow_inputs(seed))
    wider = {'gdn_norm': 4.4,
     'sgu_v_norm': 5.69,
     'sgu_b': 6.55,
     'sgu_out_norm': 4.03,
     'norm_final': 3.2}
    for name, times in wider.items():
        mean = out[name].mean()
        out[name] = (mean + times * (out[name] - mean)).astype(out[name].dtype)
    return out


CHUNK = 64
SSM_WIDTH = D_MODEL // 2
SSM_GROUP = 16
SSM_GROUPS = SSM_WIDTH // SSM_GROUP
SSM_STATE = 64
CONV_WIDTH = D_MODEL // 2
CONV_K_2 = 3
FFN_HIDDEN = ((8 * D_MODEL // 3 + 255) // 256) * 256
IN_COLS_2 = SSM_WIDTH + 3 * CONV_WIDTH + 2 * D_MODEL
ALPHA = (2.0 * DEPTH) ** 0.25
BETA = (8.0 * DEPTH) ** -0.25
DT_MIN = 0.001
DT_MAX = 0.1
LN_EPS = 1e-5


def layer_norm(x, g, b):
    xf = x.astype(jnp.float32)
    mu = jnp.mean(xf, axis=-1, keepdims=True)
    var = jnp.mean(jnp.square(xf - mu), axis=-1, keepdims=True)
    y = (xf - mu) * lax.rsqrt(var + LN_EPS) * g.astype(jnp.float32) + b.astype(jnp.float32)
    return y.astype(x.dtype)

def _complex_affine_combine(earlier, later):
    ar_i, ai_i, br_i, bi_i = earlier
    ar_j, ai_j, br_j, bi_j = later
    ar = ar_j * ar_i - ai_j * ai_i
    ai = ar_j * ai_i + ai_j * ar_i
    br = ar_j * br_i - ai_j * bi_i + br_j
    bi = ar_j * bi_i + ai_j * br_i + bi_j
    return (ar, ai, br, bi)

def s5_ssm(u, lam_re, lam_im, log_dt, b_re, b_im, c_re, c_im, d_skip):
    f32 = jnp.float32
    bsz, slen, _ = u.shape
    uf = u.astype(f32).reshape(bsz, slen, SSM_GROUPS, SSM_GROUP).transpose(1, 0, 2, 3)
    lr = lam_re.astype(f32)
    li = lam_im.astype(f32)
    dt = jnp.exp(log_dt.astype(f32))[:, None]
    mag = jnp.exp(lr * dt)
    lb_re = mag * jnp.cos(li * dt)
    lb_im = mag * jnp.sin(li * dt)
    den = lr * lr + li * li
    num_re = lb_re - 1.0
    fr = (num_re * lr + lb_im * li) / den
    fi = (lb_im * lr - num_re * li) / den
    br = b_re.astype(f32)
    bi = b_im.astype(f32)
    bb_re = fr[..., None] * br - fi[..., None] * bi
    bb_im = fr[..., None] * bi + fi[..., None] * br
    bu_re = jnp.einsum('sbgc,gpc->sbgp', uf, bb_re)
    bu_im = jnp.einsum('sbgc,gpc->sbgp', uf, bb_im)
    a_re = jnp.broadcast_to(lb_re[None, None], (slen, 1, SSM_GROUPS, SSM_STATE))
    a_im = jnp.broadcast_to(lb_im[None, None], (slen, 1, SSM_GROUPS, SSM_STATE))
    _, _, xs_re, xs_im = lax.associative_scan(
        _complex_affine_combine, (a_re, a_im, bu_re, bu_im), axis=0)
    y = (jnp.einsum('sbgp,gcp->sbgc', xs_re, c_re.astype(f32))
         - jnp.einsum('sbgp,gcp->sbgc', xs_im, c_im.astype(f32))
         + d_skip.astype(f32).reshape(SSM_GROUPS, SSM_GROUP) * uf)
    y = y.transpose(1, 0, 2, 3).reshape(bsz, slen, SSM_WIDTH)
    return y.astype(u.dtype)

def causal_depthwise_conv(z, w):
    return lax.conv_general_dilated(
        z, w[:, None, :].astype(z.dtype), window_strides=(1,), padding=[(CONV_K_2 - 1, 0)],
        dimension_numbers=('NWC', 'WIO', 'NWC'), feature_group_count=CONV_WIDTH)

def hybrid_layer(x, w_in, b_in, ssm_lambda_re, ssm_lambda_im, ssm_log_dt, ssm_b_re, ssm_b_im,
                 ssm_c_re, ssm_c_im, ssm_d, glu_w, glu_b, w_ssm_out, conv_w, w_conv_out, w_o,
                 ln1_g, ln1_b, w_gate, w_up, w_down, ln2_g, ln2_b):
    proj = jnp.einsum('bsd,dn->bsn', x, w_in) + b_in
    o1 = SSM_WIDTH
    o2 = o1 + CONV_WIDTH
    o3 = o2 + CONV_WIDTH
    o4 = o3 + CONV_WIDTH
    o5 = o4 + D_MODEL
    u, h, c_gate, b_gate, gate_a, gate_b = jnp.split(proj, [o1, o2, o3, o4, o5], axis=-1)

    y_a = s5_ssm(u, ssm_lambda_re, ssm_lambda_im, ssm_log_dt, ssm_b_re, ssm_b_im,
                 ssm_c_re, ssm_c_im, ssm_d)
    g = jax.nn.gelu(y_a)
    y_a = g * jax.nn.sigmoid(jnp.einsum('bsc,ce->bse', g, glu_w) + glu_b)
    y_a = jnp.einsum('bsc,cd->bsd', y_a, w_ssm_out)

    z = causal_depthwise_conv(c_gate * h, conv_w)
    y_b = jnp.einsum('bsc,cd->bsd', b_gate * z, w_conv_out)

    merged = jax.nn.sigmoid(gate_a) * y_a + jax.nn.sigmoid(gate_b) * y_b
    mix = jnp.einsum('bsd,de->bse', merged, w_o)
    x = layer_norm(ALPHA * x + mix, ln1_g, ln1_b)

    hid = jax.nn.silu(jnp.einsum('bsd,df->bsf', x, w_gate)) * jnp.einsum('bsd,df->bsf', x, w_up)
    ffn = jnp.einsum('bsf,fd->bsd', hid, w_down)
    x = layer_norm(ALPHA * x + ffn, ln2_g, ln2_b)
    return x

def second_inputs(seed: int = 0) -> dict:
    key = jax.random.key(seed)
    ks = jax.random.split(key, 24)
    L = DEPTH
    f32 = jnp.float32
    nrm = lambda k, shape, s: jax.random.normal(k, shape, f32) * s
    x = jax.random.normal(ks[0], (BATCH, SEQ, D_MODEL), f32)
    w_in = nrm(ks[1], (L, D_MODEL, IN_COLS_2), D_MODEL ** -0.5)
    b_in = nrm(ks[2], (L, IN_COLS_2), 0.01)
    n_idx = jnp.arange(SSM_STATE, dtype=f32)
    ssm_lambda_re = -0.5 + nrm(ks[3], (L, SSM_GROUPS, SSM_STATE), 0.01)
    ssm_lambda_im = math.pi * n_idx[None, None, :] + nrm(ks[4], (L, SSM_GROUPS, SSM_STATE), 0.01)
    ssm_log_dt = jax.random.uniform(ks[5], (L, SSM_GROUPS), f32,
                                    minval=math.log(DT_MIN), maxval=math.log(DT_MAX))
    ssm_b_re = nrm(ks[6], (L, SSM_GROUPS, SSM_STATE, SSM_GROUP), (2.0 * SSM_GROUP) ** -0.5)
    ssm_b_im = nrm(ks[7], (L, SSM_GROUPS, SSM_STATE, SSM_GROUP), (2.0 * SSM_GROUP) ** -0.5)
    ssm_c_re = nrm(ks[8], (L, SSM_GROUPS, SSM_GROUP, SSM_STATE), SSM_STATE ** -0.5)
    ssm_c_im = nrm(ks[9], (L, SSM_GROUPS, SSM_GROUP, SSM_STATE), SSM_STATE ** -0.5)
    ssm_d = nrm(ks[10], (L, SSM_WIDTH), 1.0)
    glu_w = nrm(ks[11], (L, SSM_WIDTH, SSM_WIDTH), SSM_WIDTH ** -0.5)
    glu_b = nrm(ks[12], (L, SSM_WIDTH), 0.01)
    w_ssm_out = nrm(ks[13], (L, SSM_WIDTH, D_MODEL), BETA * SSM_WIDTH ** -0.5)
    conv_w = nrm(ks[14], (L, CONV_K_2, CONV_WIDTH), CONV_K_2 ** -0.5)
    w_conv_out = nrm(ks[15], (L, CONV_WIDTH, D_MODEL), BETA * CONV_WIDTH ** -0.5)
    w_o = nrm(ks[16], (L, D_MODEL, D_MODEL), BETA * D_MODEL ** -0.5)
    ln1_g = 1.0 + nrm(ks[17], (L, D_MODEL), 0.01)
    ln1_b = nrm(ks[18], (L, D_MODEL), 0.01)
    w_gate = nrm(ks[19], (L, D_MODEL, FFN_HIDDEN), D_MODEL ** -0.5)
    w_up = nrm(ks[20], (L, D_MODEL, FFN_HIDDEN), D_MODEL ** -0.5)
    w_down = nrm(ks[21], (L, FFN_HIDDEN, D_MODEL), BETA * FFN_HIDDEN ** -0.5)
    ln2_g = 1.0 + nrm(ks[22], (L, D_MODEL), 0.01)
    ln2_b = nrm(ks[23], (L, D_MODEL), 0.01)
    return {"x": x, "w_in": w_in, "b_in": b_in,
            "ssm_lambda_re": ssm_lambda_re, "ssm_lambda_im": ssm_lambda_im,
            "ssm_log_dt": ssm_log_dt, "ssm_b_re": ssm_b_re, "ssm_b_im": ssm_b_im,
            "ssm_c_re": ssm_c_re, "ssm_c_im": ssm_c_im, "ssm_d": ssm_d,
            "glu_w": glu_w, "glu_b": glu_b, "w_ssm_out": w_ssm_out,
            "conv_w": conv_w, "w_conv_out": w_conv_out, "w_o": w_o,
            "ln1_g": ln1_g, "ln1_b": ln1_b, "w_gate": w_gate, "w_up": w_up,
            "w_down": w_down, "ln2_g": ln2_g, "ln2_b": ln2_b}

def second_block(x, w_in, b_in, ssm_lambda_re, ssm_lambda_im, ssm_log_dt, ssm_b_re, ssm_b_im,
              ssm_c_re, ssm_c_im, ssm_d, glu_w, glu_b, w_ssm_out, conv_w, w_conv_out, w_o,
              ln1_g, ln1_b, w_gate, w_up, w_down, ln2_g, ln2_b):
    for l in range(DEPTH):
        x = hybrid_layer(x, w_in[l], b_in[l], ssm_lambda_re[l], ssm_lambda_im[l], ssm_log_dt[l],
                         ssm_b_re[l], ssm_b_im[l], ssm_c_re[l], ssm_c_im[l], ssm_d[l],
                         glu_w[l], glu_b[l], w_ssm_out[l], conv_w[l], w_conv_out[l], w_o[l],
                         ln1_g[l], ln1_b[l], w_gate[l], w_up[l], w_down[l], ln2_g[l], ln2_b[l])
    return x


_first_inputs_2 = second_inputs


def second_inputs(seed=0):
    import zlib

    import numpy as np

    out = dict(_first_inputs_2(seed))
    spreads = {}
    factors = {'b_in': 8.0,
     'ssm_lambda_re': 64.0,
     'ssm_lambda_im': 64.0,
     'ssm_log_dt': 64.0,
     'ssm_b_re': 64.0,
     'ssm_b_im': 64.0,
     'ssm_c_re': 64.0,
     'ssm_c_im': 64.0,
     'glu_w': 3.046,
     'glu_b': 200.0,
     'ln1_g': 95.381,
     'ln1_b': 95.05,
     'ln2_g': 179.777,
     'ln2_b': 185.188}
    for name, (base, spread) in spreads.items():
        noise = np.random.default_rng([zlib.crc32(name.encode()), seed]).standard_normal(out[name].shape)
        drawn = base * np.exp(spread * noise) if base else spread * noise
        out[name] = __import__('jax').numpy.asarray(drawn.astype(out[name].dtype))
    for name, factor in factors.items():
        out[name] = (out[name] * factor).astype(out[name].dtype)
    return out


_narrow_inputs_2 = second_inputs


def second_inputs(seed=0):
    out = dict(_narrow_inputs_2(seed))
    wider = {'ln1_g': 4.56, 'ln1_b': 4.56, 'ln2_g': 6.35, 'ln2_b': 6.35}
    for name, times in wider.items():
        mean = out[name].mean()
        out[name] = (mean + times * (out[name] - mean)).astype(out[name].dtype)
    return out


def setup_inputs(seed=0):
    out = dict(first_inputs(seed))
    for name, value in second_inputs(seed + 1).items():
        if name != "x":
            out[name + "_2"] = value
    return out


def reference(
    x, norm_mix, w_in, conv_w, a_log_fwd, dt_bias_fwd, a_log_bwd, dt_bias_bwd, gdn_norm,
    sgu_v_norm, sgu_w, sgu_b, sgu_out_norm, w_out, norm_ffn, w_ff1, w_ff2, norm_final, w_in_2,
    b_in_2, ssm_lambda_re_2, ssm_lambda_im_2, ssm_log_dt_2, ssm_b_re_2, ssm_b_im_2, ssm_c_re_2,
    ssm_c_im_2, ssm_d_2, glu_w_2, glu_b_2, w_ssm_out_2, conv_w_2, w_conv_out_2, w_o_2, ln1_g_2,
    ln1_b_2, w_gate_2, w_up_2, w_down_2, ln2_g_2, ln2_b_2,
):
    x = first_block(
        x, norm_mix, w_in, conv_w, a_log_fwd, dt_bias_fwd, a_log_bwd, dt_bias_bwd, gdn_norm,
        sgu_v_norm, sgu_w, sgu_b, sgu_out_norm, w_out, norm_ffn, w_ff1, w_ff2, norm_final,
    )
    return second_block(
        x, w_in_2, b_in_2, ssm_lambda_re_2, ssm_lambda_im_2, ssm_log_dt_2, ssm_b_re_2,
        ssm_b_im_2, ssm_c_re_2, ssm_c_im_2, ssm_d_2, glu_w_2, glu_b_2, w_ssm_out_2, conv_w_2,
        w_conv_out_2, w_o_2, ln1_g_2, ln1_b_2, w_gate_2, w_up_2, w_down_2, ln2_g_2, ln2_b_2,
    )


_drawn_inputs = setup_inputs


def setup_inputs(seed=0):
    import zlib

    import numpy as np

    out = dict(_drawn_inputs(seed))
    spreads = {}
    factors = {'glu_b_2': 2.921}
    for name, (base, spread) in spreads.items():
        noise = np.random.default_rng([zlib.crc32(name.encode()), seed]).standard_normal(out[name].shape)
        drawn = base * np.exp(spread * noise) if base else spread * noise
        out[name] = __import__('jax').numpy.asarray(drawn.astype(out[name].dtype))
    for name, factor in factors.items():
        out[name] = (out[name] * factor).astype(out[name].dtype)
    return out
```

```python
from contextlib import ExitStack

import numpy as np

import concourse.bass as bass
from concourse import mybir

F32 = mybir.dt.float32
F32R = mybir.dt.float32r
ALU = mybir.AluOpType
ACT = mybir.ActivationFunctionType
AX_X = mybir.AxisListType.X

P = 128
SEQ = 1024
D = 1024
NT = SEQ // P
KT = D // P
BANKS = 8
HEADS, HD = 8, 64
GW = HEADS * HD
CONV_K = 5
SG = 4
FF = 4096
EPS = 1e-6
LN_EPS = 1e-5
ALPHA = 2.0 ** 0.25
W2 = 512
WT = W2 // P
SSM_C = 16
SSM_G = W2 // SSM_C
SSM_P = 64
SUB = 8
GE = 4
SSM_ROUNDS = SSM_G // GE
F2 = 2816
F2_ROUNDS = F2 // 256
TWO_PI = 2.0 * np.pi
TWO_PI_HI = 6.28125
TWO_PI_LO = float(TWO_PI - 6.28125)
LN2_HI = 0.693359375
LN2_LO = float(np.log(2.0) - 0.693359375)
ROUNDER = 12582912.0
LEVELS = 7
MASKS = 2 * LEVELS + 4


def shape_constants():
    i = np.arange(P)[:, None]
    j = np.arange(P)[None, :]
    out = np.zeros((P, MASKS, P), np.float32)
    for lv in range(LEVELS):
        b = 1 << lv
        low = (i // (2 * b) == j // (2 * b)) & ((i // b) % 2 == 1) & ((j // b) % 2 == 0)
        out[:, lv] = low
        out[:, LEVELS + lv] = low.T
    out[:, 2 * LEVELS] = i <= j
    out[:, 2 * LEVELS + 1] = i >= j
    out[:, 2 * LEVELS + 2] = i == j
    out[:, 2 * LEVELS + 3] = 1.0
    return out


G_NORM1 = 0
G_QKV = G_NORM1 + 16
G_ROWS = G_QKV + 48
G_SGU = G_ROWS + 25
G_GDN = G_SGU + 16
GDN_STEP = 56
GDN_ROUND = 2 * GDN_STEP
G_MIXT = G_GDN + NT * GDN_ROUND
G_WOUT = G_MIXT + 8
G_NORM2 = G_WOUT + 16
G_FF = G_NORM2 + 16
FF_ROUND = 24
FF_ROUNDS = FF // 512
G_NORM3 = G_FF + FF_ROUNDS * FF_ROUND
G_U = G_NORM3 + 16
G_SSM = G_U + 8
SSM_ROUND = 8
G_HCB = G_SSM + SSM_ROUNDS * SSM_ROUND
G_YT = G_HCB + 24
G_GLU = G_YT + 8
G_MRG = G_GLU + 8
MRG_ROUND = 16
MRG_ROUNDS = 4
G_WO = G_MRG + MRG_ROUNDS * MRG_ROUND
G_LN1 = G_WO + 16
G_F2 = G_LN1 + 16
F2_ROUND = 24


def build(nc, A, out, consts):
    with ExitStack() as ctx:
        def sem(name):
            return ctx.enter_context(nc.semaphore(name))

        WORDS = 52736
        arena = (nc.sbuf_base + 31) // 32 * 32
        sb = ctx.enter_context(nc.sbuf_tensor("sb", [P, WORDS], F32))
        ps = ctx.enter_context(nc.psum_tensor("ps", [P, BANKS, 512], F32))

        def area(at, *shape, parts=P):
            size = int(np.prod(shape))
            assert at + size <= WORDS
            v = sb[0:parts, at:at + size]
            if len(shape) == 2:
                v = v.rearrange("p (a b) -> p a b", b=shape[1])
            elif len(shape) == 3:
                v = v.rearrange("p (a b c) -> p a b c", b=shape[1], c=shape[2])
            return v

        def split_area(name, at, *shape):
            assert at + int(np.prod(shape)) <= WORDS
            return nc.alloc_sbuf_tensor_at(name, [P, *shape], F32R, offset=arena + 4 * at)

        def plain_area(name, at, *shape):
            assert at + int(np.prod(shape)) <= WORDS
            return nc.alloc_sbuf_tensor_at(name, [P, *shape], F32, offset=arena + 4 * at).ap()

        AT_X, AT_H, AT_W, AT_WORK, AT_CONST = 0, 8192, 16384, 24576, 46336
        X = area(AT_X, NT, D)
        H = area(AT_H, KT, SEQ)
        ring = [area(AT_W, 8, 512), area(AT_W + 4096, 8, 512)]
        ring_wide = [area(AT_W, 4, 1024), area(AT_W + 4096, 4, 1024)]
        masks = area(AT_CONST, MASKS, P)
        ident, ones = masks[:, 2 * LEVELS + 2, :], masks[:, 2 * LEVELS + 3, :]
        at = AT_CONST + MASKS * P
        gain = area(at, D)
        shift = area(at + D, D)
        at += 2 * D
        ssum = area(at, NT)
        rstd = area(at + 8, NT)
        mean = area(at + 16, NT)
        at += 32
        sgu_vg = area(at, SG, P)
        sgu_og = area(at + 512, SG, P)
        at += 1024
        sgu_bt = area(at, SG)
        conv_taps = area(at + 4, 12, CONV_K)
        gdn_gain = area(at + 64, HD)
        dt_row = area(at + 128, 16)
        alog_row = area(at + 144, 16)
        rs_arg, rs_root, rs_y, rs_t = (area(at + 160 + 128 * n, 128) for n in range(4))
        assert at + 672 <= WORDS

        QKV = area(AT_WORK, NT, 3 * GW)
        Z = area(AT_X, NT, GW)
        SU = area(AT_X + 4096, NT, GW)
        SV = area(AT_WORK + 12288, NT, GW)
        O = SV
        TMP = AT_WORK + 16384
        raw = [area(TMP + 1028 * b, 1028) for b in range(2)]
        cv = [area(TMP + 2056 + 1024 * b, SEQ) for b in range(2)]
        GT = TMP + 4104
        wgate = area(GT, KT, 32)
        graw = area(GT + 256, NT, 32)
        gdec = area(GT + 512, NT, 16)
        gbeta = area(GT + 640, NT, 16)
        gt1 = area(GT + 768, NT, 16)
        gt2 = area(GT + 896, NT, 16)
        assert GT + 1024 <= AT_CONST
        sgu_w = area(TMP, SG, P)
        sq = area(TMP + 512, 1024)
        vst = area(TMP + 1536, 16)
        gd = AT_W
        Lm = area(gd, 8, P)
        Tm = area(gd + 1024, 8, P)
        Um = area(gd + 2048, 8, P)
        Qt = area(gd + 3072, 8, P)
        Cm = area(gd + 4096, 8, P)
        DTm = area(gd + 5120, 8, P)
        Rm = area(gd + 6144, 8, P)
        Ks = area(gd + 7168, HEADS, HD)
        Qs = area(gd + 7680, HEADS, HD)
        KQ = area(gd + 7168, 17, HD)
        gd = AT_X + 4096
        Vb = area(gd, HEADS, HD)
        Kbe = area(gd + 512, HEADS, HD)
        Kdec = area(gd + 1024, HEADS, HD)
        un = area(gd + 1536, HEADS, HD)
        vnew = area(gd + 2048, HEADS, HD)
        S = [area(gd + 2560 + 512 * d, HEADS, HD, parts=HD) for d in range(2)]
        exin = area(gd + 3584, 3, HEADS)
        ex = area(gd + 3616, 3, HEADS)
        bege = area(gd + 3648, HEADS)
        gd = AT_H
        KTr = area(gd, HEADS, P, parts=HD)
        QTr = area(gd + 1024, HEADS, P, parts=HD)
        QdT = area(gd + 2048, HEADS, P, parts=HD)
        wT = area(gd + 3072, HEADS, P, parts=HD)
        mixT = H
        xin = area(AT_WORK, NT, D)
        Hs = [split_area(f"H_{n}", AT_H + 8192 * q, KT, SEQ) for q, n in enumerate(("hi", "lo"))]
        ffs = [split_area(f"ff_{n}", AT_WORK + 4096 * q, 4, SEQ) for q, n in enumerate(("hi", "lo"))]
        ws = [[split_area(f"w{b}_{n}", AT_WORK + 8192 + 4096 * b + 2048 * q, 2048) for q, n in enumerate(("hi", "lo"))]
              for b in range(2)]
        wraw = [plain_area(f"wraw{b}", AT_WORK + 16384 + 2048 * b, 2048) for b in range(2)]
        fft = [plain_area(f"fft{b}", AT_WORK + 20480 + 512 * b, 512) for b in range(2)]
        xn = area(AT_WORK + 8192, NT, D)

        BZ = area(AT_WORK, WT, SEQ)
        U = area(AT_WORK + 4096, NT, W2)
        YA = area(AT_WORK + 4096, WT, SEQ)
        M = area(AT_WORK + 8192, KT, SEQ)
        gT = area(AT_WORK + 8192, WT, SEQ)
        T2 = AT_WORK + 16384
        zp = [area(T2 + 1280 * b, 10 * P) for b in range(2)]
        d_row = area(T2 + 2560, W2)
        u_row = area(T2 + 3072, W2)
        sig = [area(T2 + 512 * b, 512) for b in range(4)]
        hids = [split_area(f"hid_{n}", AT_WORK + 2048 * q, 2, SEQ) for q, n in enumerate(("hi", "lo"))]
        ws2 = [[split_area(f"v{b}_{n}", AT_WORK + 4096 + 4096 * b + 2048 * q, 2048) for q, n in enumerate(("hi", "lo"))]
               for b in range(3)]
        wraw2 = [plain_area(f"vraw{b}", AT_WORK + 16384 + 2048 * b, 2048) for b in range(3)]
        hg = [plain_area(f"hg{b}", AT_WORK + 16384 + 6144 + 512 * b, 512) for b in range(2)]
        assert AT_WORK + 16384 + 6144 + 1024 <= AT_CONST + 2 * LEVELS * P
        at2 = AT_CONST
        bias_col = area(at2, 28)
        glu_col = area(at2 + 28, WT)
        taps2 = area(at2 + 32, WT, 3)
        bias_now = area(at2 + 44, 2, 2)
        at2 += 64

        def small(n):
            return area(at2 + 32 * n, SSM_G, parts=SSM_P)
        (s_lr, s_li, s_dt, s_x, s_k, s_r, s_e, s_mag, s_th, s_sin, s_cos, s_half, s_den, s_nr, s_fr, s_fi,
         s_phi, s_r8, s_t1, s_t2) = (small(n) for n in range(20))
        at2 += 640
        pw_re = area(at2, 9, SSM_G, parts=SSM_P)
        pw_im = area(at2 + 288, 9, SSM_G, parts=SSM_P)
        assert at2 + 576 <= AT_CONST + 2 * LEVELS * P
        sm = AT_WORK
        b_re, b_im, c_re, c_im = (area(sm + 512 * n, SSM_G, SSM_C, parts=SSM_P) for n in range(4))
        bb_re, bb_im = (area(sm + 2048 + 512 * n, SSM_G, SSM_C, parts=SSM_P) for n in range(2))
        rv_re, rv_im = (area(sm + 3072 + 256 * n, SUB, SSM_G, parts=SSM_P) for n in range(2))
        bst = area(sm + 3584, 2, 192, parts=SSM_P)
        iota = area(sm + 3968, P, parts=SSM_P)
        sm = AT_WORK + 8192
        wt_re, wt_im = (area(sm + 512 * n, GE, SUB * SSM_C, parts=SSM_P) for n in range(2))
        v_re, v_im = (area(sm + 1024 + 576 * n, GE, 9 * SSM_C, parts=SSM_P) for n in range(2))
        kall = area(sm + 2176, GE, P, parts=SSM_C)
        toep = area(sm + 2688, GE, P)
        wl_re, wl_im = (area(sm + 3200 + 256 * n, GE, SSM_P) for n in range(2))
        e_re, e_im = (area(sm + 3712 + 512 * n, GE, P, parts=SSM_P) for n in range(2))
        r8 = area(sm + 4736, GE, P, parts=SSM_P)
        d_re, d_im = (area(sm + 5248 + 512 * n, GE, P, parts=SSM_P) for n in range(2))
        uT = area(sm + 6272, GE, P)
        Uq = area(sm + 6784, GE, P)
        not_first = area(sm + 7296, GE, P, parts=SSM_P)
        tt = [area(T2 + 576 * n, 576, parts=SSM_P) for n in range(2)]
        tt4 = [area(T2 + 576 * n, GE, P, parts=SSM_P) for n in range(2)]
        s_re, s_im = wt_re, wt_im
        yt = area(T2 + 1152, GE, P)

        b2_in = sem("b2_in")
        ssm_in = sem("ssm_in")
        ssm_sin = sem("ssm_sin")
        ssm_half = sem("ssm_half")
        ssm_own = sem("ssm_own")
        ssm_pre = sem("ssm_pre")
        ssm_w = sem("ssm_w")
        ssm_k = sem("ssm_k")
        ssm_u = sem("ssm_u")
        ssm_angle = sem("ssm_angle")
        ssm_trig = sem("ssm_trig")
        ssm_state = sem("ssm_state")
        toep_in = sem("toep_in")
        cgate = sem("cgate")
        z_own = sem("z_own")
        sig_done = sem("sig_done")
        mrg_own = sem("mrg_own")
        f2_gate = sem("f2_gate")
        ln_sum = sem("ln_sum")
        ln_mean = sem("ln_mean")
        ln_sq = sem("ln_sq")
        ln_scaled = sem("ln_scaled")
        ln_rows = sem("ln_rows")
        merged_rows = sem("merged_rows")
        alpha_done = sem("alpha_done")
        ln_mean2 = sem("ln_mean2")
        bias_set = sem("bias_set")

        full = [sem(f"full{b}") for b in range(BANKS)]
        drained = [sem(f"drained{b}") for b in range(BANKS)]
        consts_in = sem("consts_in")
        x_in = sem("x_in")
        slab_in = [sem(f"slab_in{b}") for b in range(2)]
        gain_in = sem("gain_in")
        wgate_in = sem("wgate_in")
        sguw_in = sem("sguw_in")
        dve_step = sem("dve_step")
        act_step = sem("act_step")
        norm_sums = sem("norm_sums")
        norm_rows = sem("norm_rows")
        root_ask = sem("root_ask")
        root_done = sem("root_done")
        conv_done = sem("conv_done")
        silu_done = sem("silu_done")
        pads_set = sem("pads_set")
        gate_in = sem("gate_in")
        gate_out = sem("gate_out")
        sgu_v = sem("sgu_v")
        sgu_o = sem("sgu_o")
        gdn_ready = sem("gdn_ready")
        gdn_rg = sem("gdn_rg")
        gdn_exin = sem("gdn_exin")
        gdn_ex = sem("gdn_ex")
        gdn_stage = sem("gdn_stage")
        gdn_go = sem("gdn_go")
        gdn_rexp = sem("gdn_rexp")
        gdn_din = sem("gdn_din")
        gdn_dexp = sem("gdn_dexp")
        gdn_vk = sem("gdn_vk")
        gdn_t0 = sem("gdn_t0")
        gdn_c = sem("gdn_c")
        gdn_qd = sem("gdn_qd")
        gdn_step = sem("gdn_step")
        gdn_over = sem("gdn_over")
        mix_rows = sem("mix_rows")
        xin_in = sem("xin_in")
        relu_done = sem("relu_done")
        square_done = sem("square_done")
        raw_in = [sem(f"raw_in{b}") for b in range(2)]
        raw2_in = [sem(f"raw2_in{b}") for b in range(3)]
        w_hi = sem("w_hi")
        w_lo = sem("w_lo")
        v_hi = sem("v_hi")
        v_lo = sem("v_lo")
        feat_hi = sem("feat_hi")
        ff_hi = sem("ff_hi")
        hid_f = sem("hid_f")
        hid_hi = sem("hid_hi")
        out_done = sem("out_done")

        block = ctx.enter_context(nc.Block())

        def where(start, k, i=None, per=0):
            g = start + k
            use = g // BANKS
            return g % BANKS, (use if i is None else i * (per // BANKS) + use)

        def wait_full(eng, start, k, i=None, per=0):
            b, use = where(start, k, i, per)
            eng.wait_ge(full[b], use + 1)
            return b

        def wait_drained(eng, start, k, i=None, per=0):
            b, use = where(start, k, i, per)
            eng.wait_ge(drained[b], use + 1)

        def wait_bank(eng, start, k, i=None, per=0):
            b, use = where(start, k, i, per)
            if i is not None or use > 0:
                eng.wait_ge(drained[b], use)
            return b

        HI_LO = ((0, 0), (0, 1), (1, 0))

        FF_SLAB_END = (3, 7, 15, 23)

        def ff_slab_done(eng, q, i):
            start = G_FF if q >= 0 else G_FF - FF_ROUND
            if isinstance(i, int):
                if q >= 0 or i > 0:
                    wait_full(eng, start + i * FF_ROUND, FF_SLAB_END[q])
            else:
                wait_full(eng, start, FF_SLAB_END[q], i, FF_ROUND)

        def at_round(start, i, per):
            return (start + i * per, {}) if isinstance(i, int) else (start, dict(i=i, per=per))

        def rounds(eng, count, body):
            with eng.Fori(0, count - 1) as i:
                body(i, False)
            body(count - 1, True)

        def strided_view(hview):
            return hview.rearrange("p k (c j) -> p k c j", j=8)

        last_mrg = G_MRG + (MRG_ROUNDS - 1) * MRG_ROUND
        last_f2 = G_F2 + (F2_ROUNDS - 1) * F2_ROUND
        w_in, w_out, w_ff1, w_ff2 = A["w_in"], A["w_out"], A["w_ff1"], A["w_ff2"]
        Z0 = 3 * GW
        SU0 = 4 * GW + 4 * HEADS
        slab_cols = [0, 512, 1024, Z0, SU0, SU0 + GW]
        slab_last = [(G_QKV, 13), (G_QKV, 29), (G_QKV, 45), (G_ROWS, 7), (G_ROWS, 15), (G_ROWS, 23),
                     (G_WOUT, 7), (G_WOUT, 15)]
        def dense_at(ct):
            return 2 * ct if ct == 0 else 4 * ct - 2
        def turn_at(ct):
            return 4 * ct + 4 if ct < 11 else 46

        @block.sync
        def _(sp):
            xv = A["x"].rearrange("(p j) d -> p j d", j=NT)
            for h in range(2):
                sp.dma_start(X[:, 4 * h:4 * h + 4, :], xv[:, 4 * h:4 * h + 4, :]).then_inc(x_in, 16)
            sp.dma_start(gain, A["norm_mix"].partition_broadcast(P)).then_inc(gain_in, 16)
            sp.dma_start(masks, consts).then_inc(consts_in, 16)
            sp.dma_start(conv_taps, A["conv_wT"].rearrange("(t p) k -> p t k", p=P)).then_inc(consts_in, 16)
            sp.dma_start(sgu_vg, A["sgu_v_norm"].partition_broadcast(P)).then_inc(consts_in, 16)
            sp.dma_start(sgu_og, A["sgu_out_norm"].partition_broadcast(P)).then_inc(consts_in, 16)
            sp.dma_start(sgu_bt, A["sgu_bT"]).then_inc(consts_in, 16)
            sp.dma_start(gdn_gain, A["gdn_norm"].partition_broadcast(P)).then_inc(consts_in, 16)
            sp.dma_start(dt_row[:, 0:8], A["dt_bias_fwd"].partition_broadcast(P)).then_inc(consts_in, 16)
            sp.dma_start(dt_row[:, 8:16], A["dt_bias_bwd"].partition_broadcast(P)).then_inc(consts_in, 16)
            sp.dma_start(alog_row[:, 0:8], A["a_log_fwd"].partition_broadcast(P)).then_inc(consts_in, 16)
            sp.dma_start(alog_row[:, 8:16], A["a_log_bwd"].partition_broadcast(P)).then_inc(consts_in, 16)
            sp.dma_start(wgate, w_in[:, 4 * GW:4 * GW + 32].rearrange("(k p) n -> p k n", p=P)).then_inc(wgate_in, 16)
            for n, c0 in enumerate(slab_cols):
                if n >= 2:
                    wait_full(sp, *slab_last[n - 2])
                sp.dma_start(ring[n % 2], w_in[:, c0:c0 + 512].rearrange("(k p) n -> p k n", p=P)
                             ).then_inc(slab_in[n % 2], 16)
                if n == 4:
                    wait_drained(sp, G_QKV, 47)
                    sp.dma_start(sgu_w, A["sgu_wT"].rearrange("g s t -> s g t")).then_inc(sguw_in, 16)
            sp.wait_ge(gdn_over, 1)
            for h in range(2):
                sp.dma_start(xin[:, 4 * h:4 * h + 4, :], xv[:, 4 * h:4 * h + 4, :]).then_inc(xin_in, 16)
            for h in range(2):
                sp.dma_start(ring[h], w_out[:, 512 * h:512 * h + 512].rearrange("(k p) n -> p k n", p=P)
                             ).then_inc(slab_in[h], 16)
            wait_full(sp, G_NORM1, 15)
            sp.dma_start(gain, A["norm_ffn"].partition_broadcast(P)).then_inc(gain_in, 16)
            w1v = w_ff1.rearrange("(k p) (r n) -> p k r n", p=P, n=256)
            w2v = w_ff2.rearrange("(r k p) n -> p r k n", k=4, p=P)

            def ff_load(q, i):
                row = bass.ds(i, 1)
                dst = wraw[q % 2]
                if q < 2:
                    src = w1v[:, :, bass.ds(i * 2 + q, 1), :]
                    dst = dst.rearrange("p (k n) -> p k n", n=256)
                else:
                    src = w2v[:, row, :, 512 * (q - 2):512 * (q - 2) + 512]
                    dst = dst.rearrange("p (k n) -> p k n", n=512)
                sp.dma_start(dst, src).then_inc(raw_in[q % 2], 16)

            def ff_loads(i, last):
                for q in range(4):
                    if isinstance(i, int) or q > -1:
                        sp.wait_ge(w_lo, i * 4 + q + 1)
                    if q < 2:
                        ff_load(q + 2, i)
                    elif not last:
                        ff_load(q - 2, i + 1)

            wait_full(sp, G_WOUT, 15)
            ff_load(0, 0)
            ff_load(1, 0)
            rounds(sp, FF_ROUNDS, ff_loads)
            wait_full(sp, G_NORM2, 15)
            sp.dma_start(gain, A["norm_final"].partition_broadcast(P)).then_inc(gain_in, 16)
            last_ff = G_FF + (FF_ROUNDS - 1) * FF_ROUND
            wi2 = A["w_in_2"].rearrange("(k p) n -> p k n", p=P)
            wait_full(sp, last_ff, 7)
            sp.dma_start(ring[0], wi2[:, :, 0:512]).then_inc(slab_in[0], 16)
            sp.dma_start(bias_col, A["bias_col"]).then_inc(b2_in, 16)
            sp.dma_start(glu_col, A["glu_col"]).then_inc(b2_in, 16)
            sp.dma_start(taps2, A["conv_taps_2"].rearrange("p (t k) -> p t k", k=3)).then_inc(b2_in, 16)
            sp.dma_start(ring[1], wi2[:, :, 512:1024]).then_inc(slab_in[1], 16)
            wait_full(sp, last_ff, 23)
            sp.dma_start(s_lr, A["lam_re"]).then_inc(ssm_in, 16)
            sp.dma_start(s_li, A["lam_im"]).then_inc(ssm_in, 16)
            sp.dma_start(s_x, A["log_dt"].partition_broadcast(SSM_P)).then_inc(ssm_in, 16)
            for dst, name in ((b_re, "b_re"), (b_im, "b_im"), (c_re, "c_re"), (c_im, "c_im")):
                sp.dma_start(dst, A[name]).then_inc(ssm_in, 16)
            sp.dma_start(iota, A["counts"].partition_broadcast(SSM_P)).then_inc(ssm_in, 16)
            sp.dma_start(d_row, A["ssm_d"].partition_broadcast(P)).then_inc(ssm_in, 16)
            sp.dma_start(u_row, A["b_in"].rearrange("(a n) -> a n", a=1)[0, 0:W2].partition_broadcast(P)).then_inc(ssm_in, 16)
            sp.wait_ge(norm_rows, 24)
            sp.dma_start(gain, A["ln1_g"].partition_broadcast(P)).then_inc(gain_in, 16)
            sp.dma_start(shift, A["ln1_b"].partition_broadcast(P)).then_inc(gain_in, 16)
            with sp.Fori(0, SSM_ROUNDS) as i:
                wait_drained(sp, G_SSM, 2, i, SSM_ROUND)
                for lag in range(SUB):
                    rows = slice(SSM_C * lag, SSM_C * (lag + 1))
                    sp.dma_start(toep[rows, :, SSM_C * lag:P], kall[:, :, 0:P - SSM_C * lag]).then_inc(toep_in, 16)
            wait_full(sp, G_U, 7)
            sp.dma_start(ring[0], wi2[:, :, 1024:1536]).then_inc(slab_in[0], 16)
            wait_full(sp, G_HCB, 7)
            sp.dma_start(ring[1], wi2[:, :, 1536:2048]).then_inc(slab_in[1], 16)
            wait_full(sp, G_HCB, 15)
            sp.dma_start(ring[0][:, 0:4, :], A["glu_w"].rearrange("(k p) n -> p k n", p=P)).then_inc(slab_in[0], 16)
            wsv = A["w_ssm_out"].rearrange("(k p) (n c) -> p k n c", p=P, c=4)
            wcv = A["w_conv_out"].rearrange("(k p) (n c) -> p k n c", p=P, c=4)
            with sp.Fori(0, MRG_ROUNDS) as i:
                wait_full(sp, G_MRG - MRG_ROUND, 13, i, MRG_ROUND)
                sp.dma_start(ring[1][:, :, 0:256], wi2[:, :, bass.ds(i * 256 + 2048, 256)]).then_inc(slab_in[1], 16)
                sp.dma_start(ring[1][:, :, 256:512], wi2[:, :, bass.ds(i * 256 + 3072, 256)]).then_inc(slab_in[1], 16)
                wait_full(sp, G_MRG - MRG_ROUND, 15, i, MRG_ROUND)
                sp.dma_start(ring[0][:, 0:4, 0:256].rearrange("p k (n c) -> p k n c", c=4), wsv[:, :, bass.ds(i * 64, 64), :]).then_inc(slab_in[0], 16)
                sp.dma_start(ring[0][:, 0:4, 256:512].rearrange("p k (n c) -> p k n c", c=4), wcv[:, :, bass.ds(i * 64, 64), :]).then_inc(slab_in[0], 16)
            wov = A["w_o"].rearrange("(k p) n -> p k n", p=P)
            last_mrg = G_MRG + (MRG_ROUNDS - 1) * MRG_ROUND
            wait_full(sp, last_mrg, 13)
            sp.dma_start(ring[1], wov[:, :, 0:512]).then_inc(slab_in[1], 16)
            wait_full(sp, last_mrg, 15)
            sp.dma_start(ring[0], wov[:, :, 512:1024]).then_inc(slab_in[0], 16)
            wgv = A["w_gate"].rearrange("(k p) n -> p k n", p=P)
            wuv = A["w_up"].rearrange("(k p) n -> p k n", p=P)
            wgv = A["w_gate"].rearrange("(k p) (r n) -> p k r n", p=P, n=P)
            wuv = A["w_up"].rearrange("(k p) (r n) -> p k r n", p=P, n=P)
            wdv = A["w_down"].rearrange("(r k p) n -> p r k n", k=2, p=P)

            def f2_load(q, i):
                if q < 2:
                    dst = wraw2[q].rearrange("p (k n) -> p k n", n=256)
                    for n, src in enumerate((wgv, wuv)):
                        sp.dma_start(dst[:, :, P * n:P * n + P], src[:, :, bass.ds(i * 2 + q, 1), :]
                                     ).then_inc(raw2_in[q], 16)
                else:
                    sp.dma_start(wraw2[2].rearrange("p (k n) -> p k n", n=D), wdv[:, bass.ds(i, 1), :, :]
                                 ).then_inc(raw2_in[2], 16)

            def f2_loads(i, last):
                for q in range(3):
                    sp.wait_ge(v_lo, i * 3 + q + 1)
                    if not last:
                        f2_load(q, i + 1)

            wait_drained(sp, G_LN1, 15)
            for q in range(3):
                f2_load(q, 0)
            rounds(sp, F2_ROUNDS, f2_loads)
            sp.wait_ge(ln_rows, 8)
            sp.dma_start(gain, A["ln2_g"].partition_broadcast(P)).then_inc(gain_in, 16)
            sp.dma_start(shift, A["ln2_b"].partition_broadcast(P)).then_inc(gain_in, 16)
            ov = out.rearrange("(p j) d -> p j d", j=NT)
            for j in range(NT):
                sp.wait_ge(ln_rows, 8 + j + 1)
                sp.dma_start(ov[:, j, :], X[:, j, :]).then_inc(out_done, 16)
            sp.wait_ge(out_done, 16 * NT)

        @block.tensor
        def _(pe):
            def turn(dst, src):
                return nc.tensor.transpose(dst, src, ident)

            def rows_to_features(start, src):
                for j in range(NT):
                    pe.wait_ge(norm_rows, norm_base[0] + j + 1)
                    for h in range(2):
                        b = wait_bank(pe, start, 2 * j + h)
                        for q in range(4):
                            k = 4 * h + q
                            mm = turn(ps[:, b, q * P:(q + 1) * P], src[:, j, k * P:(k + 1) * P])
                        mm.then_inc(full[b], 1)
                norm_base[0] += NT

            norm_base = [0]
            pe.wait_ge(consts_in, 16 * 10)
            rows_to_features(G_NORM1, xn)

            wait_drained(pe, G_NORM1, 14)
            wait_drained(pe, G_NORM1, 15)
            for b in range(6):
                wait_drained(pe, G_NORM1, 8 + b)

            def feature_tile(slot, ft, start, k0, kts=KT, src=H):
                for h in range(2):
                    b = wait_bank(pe, start, k0 + h)
                    for k in range(kts):
                        mm = nc.tensor.matmul(ps[:, b, :], ring[slot][:, k, ft * P:(ft + 1) * P],
                                              src[:, k, h * 512:h * 512 + 512], start=(k == 0), stop=(k == kts - 1))
                    mm.then_inc(full[b], 1)

            for ct in range(13):
                if ct < 12:
                    n = ct // 4
                    if ct % 4 == 0:
                        pe.wait_ge(slab_in[n % 2], 16 * (n // 2 + 1))
                    feature_tile(n % 2, ct % 4, G_QKV, dense_at(ct))
                if ct >= 1:
                    pe.wait_ge(silu_done, ct)
                    for h in range(2):
                        b = wait_bank(pe, G_QKV, turn_at(ct - 1) + h)
                        for q in range(4):
                            t = 4 * h + q
                            mm = turn(ps[:, b, q * P:(q + 1) * P], cv[(ct - 1) % 2][:, t * P:(t + 1) * P])
                        mm.then_inc(full[b], 1)

            def row_tiles(slot, start, k0, kts=KT, src=H):
                for t in range(NT):
                    b = wait_bank(pe, start, k0 + t)
                    for k in range(kts):
                        mm = nc.tensor.matmul(ps[:, b, :], src[:, k, t * P:(t + 1) * P], ring[slot][:, k, :],
                                              start=(k == 0), stop=(k == kts - 1))
                    mm.then_inc(full[b], 1)

            for n in range(3, 6):
                pe.wait_ge(slab_in[n % 2], 16 * (n // 2 + 1))
                row_tiles(n % 2, G_ROWS, 8 * (n - 3))
            pe.wait_ge(wgate_in, 16)
            b = wait_bank(pe, G_ROWS, 24)
            for t in range(NT):
                for k in range(KT):
                    mm = nc.tensor.matmul(ps[:, b, t * 32:(t + 1) * 32], H[:, k, t * P:(t + 1) * P], wgate[:, k, :],
                                          start=(k == 0), stop=(k == KT - 1))
            mm.then_inc(full[b], 1)

            pe.wait_ge(sguw_in, 16)
            for t in range(NT):
                pe.wait_ge(sgu_v, t + 1)
                b = wait_bank(pe, G_SGU, t)
                for g in range(SG):
                    mm = nc.tensor.matmul(ps[:, b, g * P:(g + 1) * P], sgu_w[:, g, :], SV[:, t, g * P:(g + 1) * P],
                                          start=True, stop=True)
                mm.then_inc(full[b], 1)
            for t in range(NT):
                pe.wait_ge(sgu_o, t + 1)
                b = wait_bank(pe, G_SGU, NT + t)
                for g in range(SG):
                    mm = turn(ps[:, b, g * P:(g + 1) * P], SU[:, t, g * P:(g + 1) * P])
                mm.then_inc(full[b], 1)

            pe.wait_ge(gdn_ready, 1)
            with pe.Fori(0, NT) as i:
                for d in range(2):
                    base = G_GDN + d * GDN_STEP
                    tile = i if d == 0 else i * -1 + 7
                    tri = masks[:, 2 * LEVELS + d, :]

                    def bank(k):
                        return wait_bank(pe, base, k, i, GDN_ROUND)

                    def ready(k):
                        wait_drained(pe, base, k, i, GDN_ROUND)

                    def done(mm, b):
                        mm.then_inc(full[b], 1)

                    b = bank(0)
                    gt = gdec[:, bass.ds(tile, 1), 8 * d:8 * d + 8]
                    nc.tensor.matmul(ps[:, b, 0:8], tri, gt, start=True, stop=True)
                    done(nc.tensor.matmul(ps[:, b, 8:16], ones, gt, start=True, stop=True), b)
                    pe.wait_ge(gdn_rg, i * 2 + d + 1)
                    for h in range(2):
                        b = bank(1 + h)
                        done(nc.tensor.matmul(ps[:, b, :], ones, Lm[:, 4 * h:4 * h + 4, :], start=True, stop=True), b)
                    pe.wait_ge(gdn_stage, i * 2 + d + 1)
                    for n in range(2):
                        for h in range(2):
                            b = bank(3 + 2 * n + h)
                            for q in range(4):
                                at = 8 * n + 4 * h + q
                                mm = turn(ps[:, b, q * P:(q + 1) * P], KQ[:, at:at + 2, :])
                            done(mm, b)
                    for n, rhs in enumerate((KTr, QTr)):
                        for h in range(2):
                            ready(3 + 2 * n + h)
                            b = bank(7 + 2 * n + h)
                            for q in range(4):
                                hh = 4 * h + q
                                mm = nc.tensor.matmul(ps[:, b, q * P:(q + 1) * P], KTr[:, hh, :], rhs[:, hh, :],
                                                      start=True, stop=True)
                            done(mm, b)
                    for h in range(2):
                        pe.wait_ge(gdn_t0, i * 4 + 2 * d + h + 1)
                        b = bank(11 + h)
                        for q in range(4):
                            mm = turn(ps[:, b, q * P:(q + 1) * P], Tm[:, 4 * h + q, :])
                        done(mm, b)
                    for lv in range(1, LEVELS):
                        k0 = 13 + 6 * (lv - 1)
                        for h in range(2):
                            pe.wait_ge(gdn_c, (i * 2 + d) * 12 + 2 * (lv - 1) + h + 1)
                            ready(11 + h if lv == 1 else k0 - 2 + h)
                            b = bank(k0 + h)
                            for q in range(4):
                                hh = 4 * h + q
                                mm = nc.tensor.matmul(ps[:, b, q * P:(q + 1) * P], Cm[:, hh, :], Um[:, hh, :],
                                                      start=True, stop=True)
                            done(mm, b)
                        for h in range(2):
                            ready(k0 + h)
                            b = bank(k0 + 2 + h)
                            for q in range(4):
                                hh = 4 * h + q
                                mm = nc.tensor.matmul(ps[:, b, q * P:(q + 1) * P], Qt[:, hh, :], Tm[:, hh, :],
                                                      start=True, stop=True)
                            done(mm, b)
                        for h in range(2):
                            ready(k0 + 2 + h)
                            b = bank(k0 + 4 + h)
                            for q in range(4):
                                mm = turn(ps[:, b, q * P:(q + 1) * P], Tm[:, 4 * h + q, :])
                            done(mm, b)
                    pe.wait_ge(gdn_vk, i * 2 + d + 1)
                    ready(47)
                    ready(48)
                    b = bank(49)
                    for hh in range(HEADS):
                        mm = nc.tensor.matmul(ps[:, b, hh * HD:(hh + 1) * HD], Um[:, hh, :], Vb[:, hh, :],
                                              start=True, stop=True)
                    done(mm, b)
                    for h in range(2):
                        b = bank(50 + h)
                        for q in range(4):
                            hh = 4 * h + q
                            mm = nc.tensor.matmul(ps[0:HD, b, q * P:(q + 1) * P], Kbe[:, hh, :], Um[:, hh, :],
                                                  start=True, stop=True)
                        done(mm, b)
                    ready(50)
                    ready(51)
                    b = bank(52)
                    for hh in range(HEADS):
                        mm = nc.tensor.matmul(ps[:, b, hh * HD:(hh + 1) * HD], wT[:, hh, :], S[d][:, hh, :],
                                              start=True, stop=True)
                    done(mm, b)
                    pe.wait_ge(gdn_qd, i * 2 + d + 1)
                    ready(52)
                    b = bank(53)
                    for hh in range(HEADS):
                        nc.tensor.matmul(ps[:, b, hh * HD:(hh + 1) * HD], QdT[:, hh, :], S[d][:, hh, :],
                                         start=True, stop=False)
                        mm = nc.tensor.matmul(ps[:, b, hh * HD:(hh + 1) * HD], DTm[:, hh, :], vnew[:, hh, :],
                                              start=False, stop=True)
                    done(mm, b)
                    b = bank(54)
                    for hh in range(HEADS):
                        mm = nc.tensor.matmul(ps[0:HD, b, hh * HD:(hh + 1) * HD], Kdec[:, hh, :], vnew[:, hh, :],
                                              start=True, stop=True)
                    done(mm, b)
                    b = bank(55)
                    done(turn(ps[:, b, 0:P], KQ[:, 0:2, :]), b)

            for t in range(NT):
                pe.wait_ge(mix_rows, t + 1)
                b = wait_bank(pe, G_MIXT, t)
                for q in range(4):
                    mm = turn(ps[:, b, q * P:(q + 1) * P], O[:, t, q * P:(q + 1) * P])
                mm.then_inc(full[b], 1)
            for t in range(NT):
                wait_drained(pe, G_MIXT, t)
            for n in range(2):
                pe.wait_ge(slab_in[n], 16 * 4)
                row_tiles(n, G_WOUT, 8 * n, src=mixT)

            rows_to_features(G_NORM2, xn)
            for k in range(8, 16):
                wait_drained(pe, G_NORM2, k)
            def split_product(out_ap, stationary, moving, kts):
                for k in range(kts):
                    for n, (a, c) in enumerate(HI_LO):
                        mm = nc.tensor.matmul(out_ap, stationary(a, k), moving(c, k), start=(k == 0 and n == 0),
                                              stop=(k == kts - 1 and n == 2))
                return mm

            def ff_round(i, last):
                start, at = at_round(G_FF, i, FF_ROUND)
                for ft in range(4):
                    if ft % 2 == 0:
                        pe.wait_ge(w_lo, i * 4 + ft // 2 + 1)
                    wv = [w.ap().rearrange("p (k n) -> p k n", n=256) for w in ws[ft // 2]]
                    for h in range(2):
                        b = wait_bank(pe, start, 2 * ft + h, **at)
                        cols = slice((ft % 2) * P, (ft % 2) * P + P)
                        split_product(ps[:, b, :], lambda a, k: wv[a][:, k, cols],
                                      lambda a, k: Hs[a][:, k, h * 512:h * 512 + 512], KT).then_inc(full[b], 1)
                for k in range(8):
                    wait_drained(pe, start, k, **at)
                for h in range(2):
                    pe.wait_ge(w_lo, i * 4 + 2 + h + 1)
                    wv = [w.ap().rearrange("p (k n) -> p k n", n=512) for w in ws[h]]
                    for t in range(NT):
                        b = wait_bank(pe, start, 8 + 8 * h + t, **at)
                        split_product(ps[:, b, :], lambda a, k: ffs[a][:, k, t * P:(t + 1) * P],
                                      lambda a, k: wv[a][:, k, :], 4).then_inc(full[b], 1)
            rounds(pe, FF_ROUNDS, ff_round)
            rows_to_features(G_NORM3, X)
            for k in range(8, 16):
                wait_drained(pe, G_NORM3, k)

            def product(start, k0, out_ap, terms, i=None, per=0):
                b = wait_bank(pe, start, k0, i, per)
                for n, (lhs, rhs) in enumerate(terms):
                    mm = nc.tensor.matmul(out_ap(b), lhs, rhs, start=(n == 0), stop=(n == len(terms) - 1))
                mm.then_inc(full[b], 1)

            pe.wait_ge(slab_in[0], 16 * 5)
            row_tiles(0, G_U, 0)
            pe.wait_ge(ssm_pre, 1)
            with pe.Fori(0, SSM_ROUNDS) as i:
                def bank(k):
                    return wait_bank(pe, G_SSM, k, i, SSM_ROUND)
                pe.wait_ge(ssm_w, i + 1)
                for n, src in enumerate((wt_re, wt_im)):
                    b = bank(n)
                    for g in range(GE):
                        mm = nc.tensor.matmul(ps[:, b, g * SSM_P:(g + 1) * SSM_P], src[:, g, :],
                                              ident[0:SSM_P, 0:SSM_P], start=True, stop=True)
                    mm.then_inc(full[b], 1)
                b = bank(2)
                for g in range(GE):
                    nc.tensor.matmul(ps[:, b, g * P:(g + 1) * P], bst[:, 0, SSM_C * g:SSM_C * g + P], v_re[:, g, 0:P],
                                     start=True, stop=False)
                    mm = nc.tensor.matmul(ps[:, b, g * P:(g + 1) * P], bst[:, 1, SSM_C * g:SSM_C * g + P], v_im[:, g, 0:P],
                                          start=False, stop=True)
                mm.then_inc(full[b], 1)
                pe.wait_ge(ssm_u, i + 1)
                b = bank(3)
                for g in range(GE):
                    mm = turn(ps[:, b, g * P:(g + 1) * P], Uq[:, g, :])
                mm.then_inc(full[b], 1)
                for n, wl in enumerate((wl_re, wl_im)):
                    wait_drained(pe, G_SSM, n, i, SSM_ROUND)
                    wait_drained(pe, G_SSM, 3, i, SSM_ROUND)
                    b = bank(4 + n)
                    for g in range(GE):
                        mm = nc.tensor.matmul(ps[0:SSM_P, b, g * P:(g + 1) * P], wl[:, g, :], uT[:, g, :],
                                              start=True, stop=True)
                    mm.then_inc(full[b], 1)
                pe.wait_ge(toep_in, i * 16 * SUB + 16 * SUB + 16)
                pe.wait_ge(ssm_state, i + 1)
                for n in range(2):
                    b = bank(6 + n)
                    for q in range(2):
                        g = 2 * n + q
                        o = ps[:, b, q * P:(q + 1) * P]
                        nc.tensor.matmul(o, uT[:, g, :], toep[:, g, :], start=True, stop=False)
                        nc.tensor.matmul(o, d_re[:, g, :], v_re[:, g, SSM_C:SSM_C + P], start=False, stop=False)
                        mm = nc.tensor.matmul(o, d_im[:, g, :], v_im[:, g, SSM_C:SSM_C + P], start=False, stop=True)
                    mm.then_inc(full[b], 1)
            for n, slot in enumerate((1, 0, 1)):
                pe.wait_ge(slab_in[slot], 16 * (5 + (n + 1) // 2))
                for ft in range(4):
                    feature_tile(slot, ft, G_HCB, 8 * n + 2 * ft)
            for j in range(NT):
                b = wait_bank(pe, G_YT, j)
                for q in range(4):
                    mm = turn(ps[:, b, q * P:(q + 1) * P], U[:, j, q * P:(q + 1) * P])
                mm.then_inc(full[b], 1)
            pe.wait_ge(slab_in[0], 16 * 7)
            for j in range(NT):
                wait_drained(pe, G_YT, j)
            for ft in range(4):
                feature_tile(0, ft, G_GLU, 2 * ft, kts=4, src=gT)
            for k in range(8):
                wait_drained(pe, G_GLU, k)
            with pe.Fori(0, MRG_ROUNDS) as i:
                pe.wait_ge(slab_in[1], i * 32 + 16 * 8)
                pe.wait_ge(slab_in[0], i * 32 + 16 * 9)
                for ft in range(2):
                    for h in range(2):
                        hc = slice(512 * h, 512 * h + 512)
                        k0 = 4 * (2 * ft + h)
                        ca = slice(ft * P, ft * P + P)
                        cb = slice(256 + ft * P, 256 + ft * P + P)
                        for n, (slot, cols, src, kts) in enumerate(((1, ca, H, 8), (1, cb, H, 8),
                                                                    (0, ca, YA, 4), (0, cb, BZ, 4))):
                            product(G_MRG, k0 + n, lambda b: ps[:, b, :],
                                    [(ring[slot][:, k, cols], src[:, k, hc]) for k in range(kts)], i, MRG_ROUND)
            for k in range(3, 16, 4):
                wait_drained(pe, last_mrg, k)
            pe.wait_ge(merged_rows, 8 + 4 * MRG_ROUNDS)
            for n, slot in enumerate((1, 0)):
                pe.wait_ge(slab_in[slot], 16 * (15 if slot == 1 else 16))
                row_tiles(slot, G_WO, 8 * n, src=M)

            def ln_rows_to_features(start):
                for j in range(NT):
                    pe.wait_ge(ln_rows, j + 1)
                    for h in range(2):
                        b = wait_bank(pe, start, 2 * j + h)
                        for q in range(4):
                            k = 4 * h + q
                            mm = turn(ps[:, b, q * P:(q + 1) * P], X[:, j, k * P:(k + 1) * P])
                        mm.then_inc(full[b], 1)
            ln_rows_to_features(G_LN1)
            for k in range(8, 16):
                wait_drained(pe, G_LN1, k)
            def f2_round(i, last):
                start, at = at_round(G_F2, i, F2_ROUND)
                for ft in range(2):
                    pe.wait_ge(v_lo, i * 3 + ft + 1)
                    wv = [w.ap().rearrange("p (k n) -> p k n", n=256) for w in ws2[ft]]
                    for h in range(2):
                        for n in range(2):
                            b = wait_bank(pe, start, 4 * ft + 2 * h + n, **at)
                            split_product(ps[:, b, :], lambda a, k: wv[a][:, k, P * n:P * n + P],
                                          lambda a, k: Hs[a][:, k, 512 * h:512 * h + 512], KT).then_inc(full[b], 1)
                pe.wait_ge(v_lo, i * 3 + 3)
                for k in range(1, 8, 2):
                    wait_drained(pe, start, k, **at)
                wv = [w.ap().rearrange("p (k n) -> p k n", n=D) for w in ws2[2]]
                for t in range(NT):
                    for h in range(2):
                        b = wait_bank(pe, start, 8 + 2 * t + h, **at)
                        split_product(ps[:, b, :], lambda a, k: hids[a][:, k, t * P:(t + 1) * P],
                                      lambda a, k: wv[a][:, k, 512 * h:512 * h + 512], 2).then_inc(full[b], 1)
            rounds(pe, F2_ROUNDS, f2_round)

        @block.scalar
        def _(act):
            steps = [0]

            def then(ins):
                ins.then_inc(act_step, 1)
                steps[0] += 1
                act.wait_ge(act_step, steps[0])

            def square_sums(src, waits, junk=None):
                junk = xn if junk is None else junk
                for j in range(NT):
                    waits(j)
                    nc.scalar.activation(junk[:, j, :], src[:, j, :], ACT.Square,
                                         accum_out=ssum[:, j:j + 1]).then_inc(norm_sums, 1)

            asked = [0]

            def root(n):
                asked[0] += 1
                act.wait_ge(root_ask, asked[0])
                nc.scalar.activation(rs_root[:, 0:n], rs_arg[:, 0:n], ACT.Sqrt).then_inc(root_done, 1)

            def copy_features(start, dst_of):
                for j in range(NT):
                    for h in range(2):
                        b = wait_full(act, start, 2 * j + h)
                        nc.scalar.copy(dst_of(j, h), ps[:, b, :].rearrange("p (k c) -> p k c", c=P)
                                       ).then_inc(drained[b], 1)

            def natural(j, h):
                return H[:, 4 * h:4 * h + 4, :].rearrange("p k (c j) -> p k c j", j=8)[:, :, :, j]

            def strided(j, h):
                return H[:, 4 * h:4 * h + 4, j * P:(j + 1) * P]

            square_sums(X, lambda j: act.wait_ge(x_in, 32))
            root(NT)
            copy_features(G_NORM1, natural)

            act.wait_ge(pads_set, 1)
            for ct in range(13):
                if ct < 12:
                    if ct >= 2:
                        act.wait_ge(conv_done, ct - 1)
                    for h in range(2):
                        b = wait_full(act, G_QKV, dense_at(ct) + h)
                        nc.scalar.copy(raw[ct % 2][:, 2 + 512 * h:514 + 512 * h], ps[:, b, :]).then_inc(drained[b], 1)
                if ct >= 1:
                    c = ct - 1
                    act.wait_ge(conv_done, c + 1)
                    nc.scalar.activation(cv[c % 2], cv[c % 2], ACT.Silu).then_inc(silu_done, 1)
                    for h in range(2):
                        b = wait_full(act, G_QKV, turn_at(c) + h)
                        nc.scalar.copy(QKV[:, 4 * h:4 * h + 4, c * P:(c + 1) * P],
                                       ps[:, b, :].rearrange("p (t c) -> p t c", c=P)).then_inc(drained[b], 1)
            root(128)
            for n, (dst, fn) in enumerate(((Z, ACT.Silu), (SU, ACT.Gelu), (SV, ACT.Gelu))):
                for t in range(NT):
                    b = wait_full(act, G_ROWS, 8 * n + t)
                    nc.scalar.activation(dst[:, t, :], ps[:, b, :], fn).then_inc(drained[b], 1)
            act.wait_ge(gate_in, 1)
            nc.scalar.activation(gbeta, graw[:, :, 0:16], ACT.Sigmoid).then_inc(gate_out, 1)
            nc.scalar.activation(alog_row, alog_row, ACT.Exp).then_inc(gate_out, 1)
            then(nc.scalar.activation(gt1, gt1, ACT.Exp))
            nc.scalar.activation(gt1, gt1, ACT.Ln, bias=1.0).then_inc(gate_out, 1)
            root(NT * SG)
            root(NT * SG)
            for t in range(NT):
                b = wait_full(act, G_SGU, NT + t)
                nc.scalar.copy(mixT[:, 4:8, :].rearrange("p k (j c) -> p k j c", j=8)[:, :, :, 16 * t:16 * t + 16],
                               ps[:, b, :].rearrange("p (k c j) -> p k j c", c=16, j=8)).then_inc(drained[b], 1)

            with act.Fori(0, NT) as i:
                for d in range(2):
                    base = G_GDN + d * GDN_STEP
                    tile = i if d == 0 else i * -1 + 7

                    def arrived(k):
                        return wait_full(act, base, k, i, GDN_ROUND)

                    act.wait_ge(gdn_go, i * 2 + d + 1)
                    nc.scalar.copy(Ks, QKV[:, bass.ds(tile, 1), GW:2 * GW].rearrange("p t (h e) -> p (t h) e", e=HD))
                    nc.scalar.copy(Qs, QKV[:, bass.ds(tile, 1), 0:GW].rearrange("p t (h e) -> p (t h) e", e=HD)
                                   ).then_inc(gdn_stage, 1)
                    act.wait_ge(gdn_exin, i * 2 + d + 1)
                    nc.scalar.activation(ex, exin, ACT.Exp).then_inc(gdn_ex, 1)
                    for h in range(2):
                        b = arrived(1 + h)
                        nc.scalar.activation(QdT[:, 4 * h:4 * h + 4, :],
                                             ps[0:HD, b, :].rearrange("p (k c) -> p k c", c=P), ACT.Exp
                                             ).then_inc(gdn_rexp, 1)
                    for n, dst in enumerate((KTr, QTr)):
                        for h in range(2):
                            b = arrived(3 + 2 * n + h)
                            nc.scalar.copy(dst[:, 4 * h:4 * h + 4, :],
                                           ps[0:HD, b, :].rearrange("p (k c) -> p k c", c=P)).then_inc(drained[b], 1)
                    for h in range(2):
                        act.wait_ge(gdn_din, (i * 2 + d) * 2 + h + 1)
                        hs = slice(4 * h, 4 * h + 4)
                        nc.scalar.activation(Cm[:, hs, :], Cm[:, hs, :], ACT.Exp)
                        nc.scalar.activation(DTm[:, hs, :], DTm[:, hs, :], ACT.Exp).then_inc(gdn_dexp, 1)

                    def drain(k, dst):
                        b = arrived(k)
                        nc.scalar.copy(dst, ps[0:dst.shape[0], b, :].rearrange("p (k c) -> p k c", c=dst.shape[2])
                                       ).then_inc(drained[b], 1)

                    for h in range(2):
                        drain(11 + h, Um[:, 4 * h:4 * h + 4, :])
                    for lv in range(1, LEVELS):
                        k0 = 13 + 6 * (lv - 1)
                        for h in range(2):
                            drain(k0 + h, Qt[:, 4 * h:4 * h + 4, :])
                        for h in range(2):
                            drain(k0 + 4 + h, Um[:, 4 * h:4 * h + 4, :])
                    drain(49, un)
                    for h in range(2):
                        drain(50 + h, wT[:, 4 * h:4 * h + 4, :])

            root(NT * HEADS)
            for t in range(NT):
                b = wait_full(act, G_MIXT, t)
                nc.scalar.copy(mixT[:, 0:4, :].rearrange("p k (j c) -> p k j c", j=8)[:, :, :, 16 * t:16 * t + 16],
                               ps[:, b, :].rearrange("p (k c j) -> p k j c", c=16, j=8)).then_inc(drained[b], 1)

            def after_wout(j):
                wait_drained(act, G_WOUT, 8 + j)
            square_sums(X, after_wout)
            root(NT)
            def round_features(start, count):
                for j in range(NT):
                    for h in range(2):
                        b = wait_full(act, start, 2 * j + h)
                        nc.scalar.copy(Hs[0][:, 4 * h:4 * h + 4, j * P:(j + 1) * P],
                                       ps[:, b, :].rearrange("p (k c) -> p k c", c=P)).then_inc(feat_hi, 1)
            def round_slab(q, i):
                act.wait_ge(raw_in[q % 2], i * 32 + 16 * (q // 2 + 1))
                ff_slab_done(act, q - 2, i)
                nc.scalar.copy(ws[q % 2][0].ap(), wraw[q % 2]).then_inc(w_hi, 1)
            round_features(G_NORM2, 0)
            round_slab(0, 0)
            def ff_round(i, last):
                start, at = at_round(G_FF, i, FF_ROUND)
                for k in range(8):
                    b = wait_full(act, start, k, **at)
                    if isinstance(i, int) or k >= 2:
                        wait_drained(act, start, k - 2, **at)
                    else:
                        wait_drained(act, start - FF_ROUND, 6 + k, **at)
                    nc.scalar.activation(fft[k % 2], ps[:, b, :], ACT.Relu).then_inc(relu_done, 1)
                    act.wait_ge(relu_done, i * 8 + k + 1)
                    nc.scalar.activation(fft[k % 2], fft[k % 2], ACT.Square).then_inc(square_done, 1)
                    if k in (0, 4):
                        round_slab(1 + k // 4, i)
                for h in range(2):
                    wait_full(act, start, 8 + 8 * h, **at)
                    if h == 0:
                        round_slab(3, i)
                    elif not last:
                        round_slab(0, i + 1)
            rounds(act, FF_ROUNDS, ff_round)
            last_ff = G_FF + (FF_ROUNDS - 1) * FF_ROUND

            def after_ff(j):
                for h in range(2):
                    wait_drained(act, last_ff, 8 + 8 * h + j)
            square_sums(X, after_ff, junk=area(AT_H, NT, D))
            root(NT)
            copy_features(G_NORM3, strided)

            act.wait_ge(ssm_angle, 1)
            nc.scalar.activation(s_sin, s_th, ACT.Sin)
            nc.scalar.activation(s_half, s_th, ACT.Sin, scale=0.5).then_inc(ssm_sin, 1)
            with act.Fori(0, SSM_ROUNDS) as i:
                def drain(k, dst, parts, width):
                    b = wait_full(act, G_SSM, k, i, SSM_ROUND)
                    nc.scalar.copy(dst, ps[0:parts, b, 0:GE * width].rearrange("p (k c) -> p k c", c=width)
                                   ).then_inc(drained[b], 1)
                act.wait_ge(ssm_angle, i + 2)
                nc.scalar.activation(e_im, tt4[0], ACT.Sin)
                nc.scalar.activation(e_re, tt4[0], ACT.Sin, scale=0.5).then_inc(ssm_trig, 1)
                drain(0, wl_re, P, SSM_P)
                drain(1, wl_im, P, SSM_P)
                act.wait_ge(toep_in, i * 16 * SUB + 16)
                drain(2, kall, SSM_C, P)
                drain(3, uT, P, P)
            act.wait_ge(b2_in, 48)
            for k in range(8):
                b = wait_full(act, G_HCB, k)
                nc.scalar.activation(BZ[:, k // 2, 512 * (k % 2):512 * (k % 2) + 512], ps[:, b, :], ACT.Identity,
                                     bias=bias_col[:, k // 2:k // 2 + 1]).then_inc(drained[b], 1)
            for j in range(NT):
                b = wait_full(act, G_YT, j)
                nc.scalar.activation(gT[:, :, j * P:(j + 1) * P], ps[:, b, :].rearrange("p (k c) -> p k c", c=P),
                                     ACT.Gelu_apprx_tanh).then_inc(drained[b], 1)
            for k in range(8):
                b = wait_full(act, G_GLU, k)
                if k >= 4:
                    wait_drained(act, G_GLU, k - 4)
                nc.scalar.activation(sig[k % 4], ps[:, b, :], ACT.Sigmoid, bias=glu_col[:, k // 2:k // 2 + 1]
                                     ).then_inc(sig_done, 1)
            with act.Fori(0, MRG_ROUNDS) as i:
                wait_drained(act, G_MRG - MRG_ROUND, 13, i, MRG_ROUND)
                nc.scalar.copy(bias_now[:, 0, :], bias_col[:, bass.ds(i * 2 + 12, 2)])
                nc.scalar.copy(bias_now[:, 1, :], bias_col[:, bass.ds(i * 2 + 20, 2)]).then_inc(bias_set, 1)
                act.wait_ge(bias_set, i + 1)
                for ft in range(2):
                    for h in range(2):
                        k0 = 4 * (2 * ft + h)
                        r = 2 * ft + h
                        act.wait_ge(merged_rows, i * 4 + r + 7)
                        for n in range(2):
                            b = wait_full(act, G_MRG, k0 + n, i, MRG_ROUND)
                            nc.scalar.activation(sig[2 * (r % 2) + n], ps[:, b, :], ACT.Sigmoid,
                                                 bias=bias_now[:, n, ft:ft + 1]
                                                 ).then_inc(drained[b], 1)

            def layer_sums(waits, count):
                junk = area(AT_H, NT, D)
                for j in range(NT):
                    waits(j)
                    nc.scalar.activation(junk[:, j, :], X[:, j, :], ACT.Copy, accum_out=ssum[:, j:j + 1]
                                         ).then_inc(ln_sum, 1)
                act.wait_ge(ln_mean, count)
                act.wait_ge(ln_sum, count * NT)
                for j in range(NT):
                    nc.scalar.activation(junk[:, j, :], X[:, j, :], ACT.Square, bias=mean[:, j:j + 1],
                                         accum_out=rstd[:, j:j + 1]).then_inc(ln_sq, 1)
                root(NT)
                act.wait_ge(ln_sq, count * NT)
                act.wait_ge(ln_mean2, count)
                for j in range(NT):
                    nc.scalar.activation(xn[:, j, :], X[:, j, :], ACT.Identity, bias=ssum[:, j:j + 1],
                                         scale=rs_y[:, j:j + 1]).then_inc(ln_scaled, 1)

            def after_wo(j):
                if j == 0:
                    for t in range(NT):
                        wait_drained(act, G_WO, 8 + t)
            layer_sums(after_wo, 1)
            round_features(G_LN1, 1)

            def round_slab2(q, i, waited=True):
                act.wait_ge(raw2_in[q], i * (32 if q < 2 else 16) + (32 if q < 2 else 16))
                nc.scalar.copy(ws2[q][0].ap(), wraw2[q]).then_inc(v_hi, 1)
            for q in range(3):
                round_slab2(q, 0)
            def f2_round(i, last):
                start, at = at_round(G_F2, i, F2_ROUND)
                for q in range(4):
                    b = wait_full(act, start, 2 * q, **at)
                    if q >= 2:
                        wait_drained(act, start, 2 * q - 3, **at)
                    else:
                        wait_drained(act, start - F2_ROUND, 5 + 2 * q, **at)
                    nc.scalar.activation(hg[q % 2], ps[:, b, :], ACT.Silu).then_inc(drained[b], 1)
                    act.wait_ge(hid_f, i * 4 + q + 1)
                    nc.scalar.copy(hids[0][:, q // 2, 512 * (q % 2):512 * (q % 2) + 512], hg[q % 2]).then_inc(hid_hi, 1)
                if not last:
                    for q in range(3):
                        wait_full(act, start, (3, 7, 23)[q], **at)
                        if q == 2:
                            pass
                        round_slab2(q, i + 1)
            rounds(act, F2_ROUNDS, f2_round)

            def after_f2(j):
                for h in range(2):
                    wait_drained(act, last_f2, 8 + 2 * j + h)
            layer_sums(after_f2, 2)

        @block.vector
        def _(dve):
            V = nc.vector
            steps = [0]

            def then(ins):
                ins.then_inc(dve_step, 1)
                steps[0] += 1
                dve.wait_ge(dve_step, steps[0])

            asked = [0]

            def inverse_root(n, factor=1.0):
                asked[0] += 1
                arg, y, t = rs_arg[:, 0:n], rs_y[:, 0:n], rs_t[:, 0:n]
                dve.wait_ge(root_ask, asked[0])
                dve.wait_ge(root_done, asked[0])
                then(V.reciprocal(y, rs_root[:, 0:n]))
                then(V.tensor_tensor(t, y, y, ALU.mult))
                then(V.tensor_tensor(t, t, arg, ALU.mult))
                then(V.tensor_scalar(t, t, -0.5, 1.5, ALU.mult, ALU.add))
                then(V.tensor_tensor(y, y, t, ALU.mult))

            def rms_rows(src, dst, count):
                dve.wait_ge(gain_in, 16 * count)
                dve.wait_ge(norm_sums, count * NT)
                V.tensor_scalar(rs_arg[:, 0:NT], ssum, 1.0 / D, EPS, ALU.mult, ALU.add).then_inc(root_ask, 1)
                inverse_root(NT)
                for j in range(NT):
                    V.scalar_tensor_tensor(dst[:, j, :], src[:, j, :], rs_y[:, j:j + 1], gain,
                                           ALU.mult, ALU.mult).then_inc(norm_rows, 1)

            rms_rows(X, xn, 1)

            for b in range(2):
                V.memset(raw[b][:, 0:2], 0.0)
                pad = V.memset(raw[b][:, 1026:1028], 0.0)
            pad.then_inc(pads_set, 1)
            dve.wait_ge(pads_set, 1)
            dve.wait_ge(consts_in, 16 * 10)
            for ct in range(12):
                for h in range(2):
                    wait_drained(dve, G_QKV, dense_at(ct) + h)
                if ct >= 2:
                    wait_full(dve, G_QKV, turn_at(ct - 2) + 1)
                r, c = raw[ct % 2], cv[ct % 2]
                then(V.tensor_scalar(c, r[:, 0:SEQ], conv_taps[:, ct, 0:1], None, ALU.mult))
                for k in range(1, CONV_K):
                    ins = V.scalar_tensor_tensor(c, r[:, k:k + SEQ], conv_taps[:, ct, k:k + 1], c, ALU.mult, ALU.add)
                    if k < CONV_K - 1:
                        then(ins)
                ins.then_inc(conv_done, 1)

            s3 = sq.rearrange("p (h e) -> p h e", e=HD)
            for ct in range(8):
                for h in range(2):
                    wait_drained(dve, G_QKV, turn_at(ct) + h)
            wait_full(dve, G_QKV, 47)
            for t in range(NT):
                qk = QKV[:, t, 0:2 * GW].rearrange("p (h e) -> p h e", e=HD)
                then(V.tensor_tensor(s3, qk, qk, ALU.mult))
                then(V.tensor_reduce(vst[:, 0:16], s3, AX_X, ALU.add))
                ins = V.tensor_scalar(rs_arg[:, 16 * t:16 * t + 16], vst[:, 0:16], EPS, None, ALU.add)
            ins.then_inc(root_ask, 1)
            inverse_root(128)
            y3 = rs_y.rearrange("p (t h) -> p t h", h=16)
            then(V.tensor_scalar(y3[:, :, 0:8], y3[:, :, 0:8], HD ** -0.5, None, ALU.mult))
            for t in range(NT):
                qk = QKV[:, t, 0:2 * GW].rearrange("p (h e) -> p h e", e=HD)
                V.tensor_tensor(qk, qk, y3[:, t, :].unsqueeze(2).broadcast_to([P, 16, HD]), ALU.mult)

            b = wait_full(dve, G_ROWS, 24)
            gv = ps[:, b, 0:256].rearrange("p (t n) -> p t n", n=32)
            then(V.tensor_copy(graw, gv))
            then(V.tensor_tensor(gt2, graw[:, :, 16:32], dt_row.unsqueeze(1).broadcast_to([P, NT, 16]), ALU.add))
            then(V.tensor_scalar(gt1, gt2, -1.0, None, ALU.mult))
            then(V.tensor_tensor(gt1, gt1, gt2, ALU.min))
            V.tensor_copy(graw[:, 0:1, 0:1], graw[:, 0:1, 0:1]).then_inc(gate_in, 1)
            dve.wait_ge(gate_out, 3)
            then(V.scalar_tensor_tensor(gt2, gt2, 0.0, gt1, ALU.max, ALU.add))
            then(V.tensor_tensor(gt2, gt2, alog_row.unsqueeze(1).broadcast_to([P, NT, 16]), ALU.mult))
            then(V.tensor_scalar(gdec, gt2, -1.0, None, ALU.mult))
            V.tensor_copy(graw[:, 0:1, 0:1], graw[:, 0:1, 0:1]).then_inc(drained[b], 1)

            def heads_of(rows, width):
                return rows.rearrange("p (g c) -> p g c", c=width)

            def group_sums(t, rows, width, count, scratch):
                r3 = heads_of(rows, width)
                then(V.tensor_tensor(scratch, r3, r3, ALU.mult))
                then(V.tensor_reduce(vst[:, 0:count], scratch, AX_X, ALU.add))
                return V.tensor_scalar(rs_arg[:, count * t:count * t + count], vst[:, 0:count], 1.0 / width, EPS,
                                       ALU.mult, ALU.add)

            def group_scale(t, rows, width, count):
                return V.tensor_tensor(heads_of(rows, width), heads_of(rows, width),
                                       rs_y[:, count * t:count * t + count].unsqueeze(2)
                                       .broadcast_to([P, count, width]), ALU.mult)

            sq4 = sq[:, 0:512].rearrange("p (g c) -> p g c", c=P)
            for t in range(NT):
                wait_drained(dve, G_ROWS, 16 + t)
                ins = group_sums(t, SV[:, t, :], P, SG, sq4)
            ins.then_inc(root_ask, 1)
            inverse_root(NT * SG)
            for t in range(NT):
                then(group_scale(t, SV[:, t, :], P, SG))
                V.tensor_tensor(heads_of(SV[:, t, :], P), heads_of(SV[:, t, :], P), sgu_vg, ALU.mult
                                ).then_inc(sgu_v, 1)
            for t in range(NT):
                b = wait_full(dve, G_SGU, t)
                wait_drained(dve, G_ROWS, 8 + t)
                V.tensor_tensor(sq4, heads_of(ps[:, b, :], P), sgu_bt.unsqueeze(2).broadcast_to([P, SG, P]), ALU.add
                                ).then_inc(drained[b], 1)
                wait_drained(dve, G_SGU, t)
                u4 = heads_of(SU[:, t, :], P)
                then(V.tensor_tensor(u4, sq4, u4, ALU.mult))
                ins = group_sums(t, SU[:, t, :], P, SG, sq4)
            ins.then_inc(root_ask, 1)
            inverse_root(NT * SG)
            for t in range(NT):
                then(group_scale(t, SU[:, t, :], P, SG))
                V.tensor_tensor(heads_of(SU[:, t, :], P), heads_of(SU[:, t, :], P), sgu_og, ALU.mult
                                ).then_inc(sgu_o, 1)

            V.memset(SV.rearrange("p t c -> p (t c)"), 0.0)
            wait_full(dve, G_SGU, NT + 7)
            V.memset(S[0], 0.0)
            ins = V.memset(S[1], 0.0)
            ins.then_inc(gdn_ready, 1)
            dve.wait_ge(gdn_ready, 1)

            with dve.Fori(0, NT) as i:
                own = [0]
                for d in range(2):
                    base = G_GDN + d * GDN_STEP
                    tile = i if d == 0 else i * -1 + 7
                    tri = masks[:, 2 * LEVELS + d, :]

                    def chain(ins):
                        ins.then_inc(gdn_step, 1)
                        own[0] += 1
                        dve.wait_ge(gdn_step, i * GDN_OWN + own[0])

                    def arrived(k):
                        return wait_full(dve, base, k, i, GDN_ROUND)

                    def view(b, c=P):
                        return ps[:, b, :].rearrange("p (k c) -> p k c", c=c)

                    def per_head(col, n=HEADS, width=HD, parts=P):
                        return col.unsqueeze(2).broadcast_to([parts, n, width])

                    gcol = gdec[:, bass.ds(tile, 1), 8 * d:8 * d + 8].rearrange("p t h -> p (t h)")
                    bcol = gbeta[:, bass.ds(tile, 1), 8 * d:8 * d + 8].rearrange("p t h -> p (t h)")
                    if d == 0:
                        wait_full(dve, G_GDN - GDN_ROUND, 2 * GDN_STEP - 1, i, GDN_ROUND)
                    V.tensor_tensor(Lm, per_head(gcol, width=P), tri.unsqueeze(1).broadcast_to([P, HEADS, P]),
                                    ALU.mult).then_inc(gdn_rg, 1)
                    V.tensor_copy(bege, bcol).then_inc(gdn_go, 1)
                    dve.wait_ge(gdn_go, i * 2 + d + 1)
                    b = arrived(0)
                    V.tensor_copy(exin[:, 0:2, :], ps[:, b, 0:16].rearrange("p (a h) -> p a h", h=8)
                                  ).then_inc(drained[b], 1)
                    wait_drained(dve, base, 0, i, GDN_ROUND)
                    V.tensor_tensor(exin[:, 2, :], exin[:, 1, :], exin[:, 0, :], ALU.subtract).then_inc(gdn_exin, 1)
                    vrow = QKV[:, bass.ds(tile, 1), 2 * GW:3 * GW].rearrange("p t (h e) -> p (t h) e", e=HD)
                    V.tensor_tensor(Vb, vrow, per_head(bege), ALU.mult)
                    for h in range(2):
                        dve.wait_ge(gdn_rexp, (i * 2 + d) * 2 + h + 1)
                        b = arrived(1 + h)
                        hs = slice(4 * h, 4 * h + 4)
                        V.tensor_tensor(Rm[:, hs, :], view(b), per_head(exin[:, 0, 4 * h:4 * h + 4], 4, P),
                                        ALU.subtract).then_inc(drained[b], 1)
                        wait_drained(dve, base, 1 + h, i, GDN_ROUND)
                        V.tensor_scalar(Cm[:, hs, :], Rm[:, hs, :], -1.0, 0.0, ALU.mult, ALU.min)
                        V.tensor_scalar(DTm[:, hs, :], Rm[:, hs, :], 0.0, None, ALU.min).then_inc(gdn_din, 1)
                    dve.wait_ge(gdn_ex, i * 2 + d + 1)
                    chain(V.tensor_tensor(exin[:, 0, :], ex[:, 0, :], bege, ALU.mult))
                    krow = QKV[:, bass.ds(tile, 1), GW:2 * GW].rearrange("p t (h e) -> p (t h) e", e=HD)
                    V.tensor_tensor(Kbe, krow, per_head(exin[:, 0, :]), ALU.mult)
                    V.tensor_tensor(Kdec, krow, per_head(ex[:, 2, :]), ALU.mult).then_inc(gdn_vk, 1)
                    for h in range(2):
                        hs = slice(4 * h, 4 * h + 4)
                        b = arrived(7 + h)
                        dve.wait_ge(gdn_dexp, (i * 2 + d) * 2 + h + 1)
                        V.tensor_tensor(Lm[:, hs, :], view(b), Cm[:, hs, :], ALU.mult).then_inc(drained[b], 1)
                        wait_drained(dve, base, 7 + h, i, GDN_ROUND)
                        chain(V.tensor_tensor(Lm[:, hs, :], Lm[:, hs, :], per_head(bege[:, 4 * h:4 * h + 4], 4, P),
                                              ALU.mult))
                        lvm = masks[:, LEVELS * d, :].unsqueeze(1).broadcast_to([P, 4, P])
                        chain(V.tensor_tensor(Tm[:, hs, :], Lm[:, hs, :], lvm, ALU.mult))
                        V.tensor_tensor(Tm[:, hs, :], ident.unsqueeze(1).broadcast_to([P, 4, P]), Tm[:, hs, :],
                                        ALU.subtract).then_inc(gdn_t0, 1)

                    def cut(lv, h):
                        hs = slice(4 * h, 4 * h + 4)
                        lvm = masks[:, LEVELS * d + lv, :].unsqueeze(1).broadcast_to([P, 4, P])
                        V.tensor_tensor(Cm[:, hs, :], Lm[:, hs, :], lvm, ALU.mult).then_inc(gdn_c, 1)

                    for h in range(2):
                        cut(1, h)
                    for h in range(2):
                        hs = slice(4 * h, 4 * h + 4)
                        wait_drained(dve, base, 5 + h, i, GDN_ROUND)
                        ins = V.tensor_tensor(QdT[:, hs, :], QdT[:, hs, :], QTr[:, hs, :], ALU.mult)
                        b = arrived(9 + h)
                        V.tensor_tensor(DTm[:, hs, :], view(b), DTm[:, hs, :], ALU.mult).then_inc(drained[b], 1)
                        wait_drained(dve, base, 9 + h, i, GDN_ROUND)
                    V.tensor_tensor(DTm, DTm, tri.unsqueeze(1).broadcast_to([P, HEADS, P]), ALU.mult
                                    ).then_inc(gdn_qd, 1)
                    for lv in range(1, LEVELS):
                        k0 = 13 + 6 * (lv - 1)
                        for h in range(2):
                            hs = slice(4 * h, 4 * h + 4)
                            b = arrived(k0 + 2 + h)
                            V.tensor_tensor(Tm[:, hs, :], Tm[:, hs, :], view(b), ALU.subtract
                                            ).then_inc(drained[b], 1)
                            if lv < LEVELS - 1:
                                cut(lv + 1, h)
                    wait_drained(dve, base, 49, i, GDN_ROUND)
                    b = arrived(52)
                    V.tensor_tensor(vnew, un, view(b, HD), ALU.subtract).then_inc(drained[b], 1)
                    b = arrived(53)
                    orow = O[:, bass.ds(tile, 1), :].rearrange("p t (h e) -> p (t h) e", e=HD)
                    V.tensor_tensor(orow, orow, view(b, HD), ALU.add).then_inc(drained[b], 1)
                    chain(V.tensor_tensor(S[d], S[d], per_head(ex[0:HD, 1, :], parts=HD), ALU.mult))
                    b = arrived(54)
                    V.tensor_tensor(S[d], S[d], ps[0:HD, b, :].rearrange("p (k c) -> p k c", c=HD), ALU.add
                                    ).then_inc(drained[b], 1)
                    b = arrived(55)
                    V.tensor_copy(exin[0:1, 0, 0:1], ps[0:1, b, 0:1]).then_inc(drained[b], 1)
                assert own[0] == GDN_OWN, own[0]

            for k in (53, 54, 55):
                wait_drained(dve, G_GDN + (NT - 1) * GDN_ROUND, GDN_STEP + k)
            V.tensor_copy(exin[0:1, 0, 0:1], exin[0:1, 1, 0:1]).then_inc(gdn_over, 1)
            sq8 = heads_of(sq[:, 0:512], HD)
            for t in range(NT):
                ins = group_sums(t, O[:, t, :], HD, HEADS, sq8)
            ins.then_inc(root_ask, 1)
            inverse_root(NT * HEADS)
            for t in range(NT):
                o3 = heads_of(O[:, t, :], HD)
                then(group_scale(t, O[:, t, :], HD, HEADS))
                then(V.tensor_tensor(o3, o3, gdn_gain.unsqueeze(1).broadcast_to([P, HEADS, HD]), ALU.mult))
                V.tensor_tensor(O[:, t, :], O[:, t, :], Z[:, t, :], ALU.mult).then_inc(mix_rows, 1)

            dve.wait_ge(xin_in, 32)
            for h in range(2):
                for t in range(NT):
                    b = wait_full(dve, G_WOUT, 8 * h + t)
                    V.tensor_tensor(X[:, t, 512 * h:512 * h + 512], xin[:, t, 512 * h:512 * h + 512], ps[:, b, :],
                                    ALU.add).then_inc(drained[b], 1)
            for t in range(NT):
                for h in range(2):
                    wait_drained(dve, G_WOUT, 8 * h + t)
            rms_rows(X, xn, 2)

            def rest_features(start, count):
                for j in range(NT):
                    for h in range(2):
                        dve.wait_ge(feat_hi, 16 * count + 2 * j + h + 1)
                        b = wait_full(dve, start, 2 * j + h)
                        part = (slice(None), slice(4 * h, 4 * h + 4), slice(j * P, (j + 1) * P))
                        V.tensor_tensor(Hs[1][part], ps[:, b, :].rearrange("p (k c) -> p k c", c=P),
                                        Hs[0][part].bitcast(F32), ALU.subtract).then_inc(drained[b], 1)

            def rest_slab(q, i):
                dve.wait_ge(w_hi, i * 4 + q + 1)
                V.tensor_tensor(ws[q % 2][1].ap(), wraw[q % 2], ws[q % 2][0].ap().bitcast(F32), ALU.subtract
                                ).then_inc(w_lo, 1)
            rest_features(G_NORM2, 0)
            rest_slab(0, 0)
            def ff_round(i, last):
                start, at = at_round(G_FF, i, FF_ROUND)
                for k in range(8):
                    dve.wait_ge(square_done, i * 8 + k + 1)
                    part = (slice(None), k // 2, slice((k % 2) * 512, (k % 2) * 512 + 512))
                    V.tensor_copy(ffs[0][part], fft[k % 2]).then_inc(ff_hi, 1)
                    dve.wait_ge(ff_hi, i * 8 + k + 1)
                    V.tensor_tensor(ffs[1][part], fft[k % 2], ffs[0][part].bitcast(F32), ALU.subtract
                                    ).then_inc(drained[where(start, k)[0]], 1)
                    if k in (0, 4):
                        rest_slab(1 + k // 4, i)
                for h in range(2):
                    for t in range(NT):
                        b = wait_full(dve, start, 8 + 8 * h + t, **at)
                        xs = X[:, t, 512 * h:512 * h + 512]
                        V.tensor_tensor(xs, xs, ps[:, b, :], ALU.add).then_inc(drained[b], 1)
                        if t == 0 and h == 0:
                            rest_slab(3, i)
                        elif t == 0 and not last:
                            rest_slab(0, i + 1)
            rounds(dve, FF_ROUNDS, ff_round)
            for k in range(8, 24):
                wait_drained(dve, G_FF + (FF_ROUNDS - 1) * FF_ROUND, k)
            rms_rows(X, X, 3)

            dve.wait_ge(ssm_in, 16 * 10)
            mul, add, sub = ALU.mult, ALU.add, ALU.subtract

            def tt2(out, a, b, op):
                then(V.tensor_tensor(out, a, b, op))

            def ts2(out, a, x, op0, y=None, op1=None):
                if op1 is None:
                    then(V.tensor_scalar(out, a, x, None, op0))
                else:
                    then(V.tensor_scalar(out, a, x, y, op0, op1))

            def exp_to(out, x):
                ts2(s_k, x, 1.0 / float(np.log(2.0)), mul, -1e6, ALU.max)
                ts2(s_k, s_k, ROUNDER, add)
                ts2(s_k, s_k, ROUNDER, sub)
                then(V.scalar_tensor_tensor(s_r, s_k, -LN2_HI, x, mul, add))
                then(V.scalar_tensor_tensor(s_r, s_k, -LN2_LO, s_r, mul, add))
                ts2(s_r, s_r, -1.0, ALU.max, 1.0, ALU.min)
                ts2(s_e, s_r, 1.0 / 5040, mul, 1.0 / 720, add)
                for c in (1.0 / 120, 1.0 / 24, 1.0 / 6, 0.5, 1.0, 1.0):
                    tt2(s_e, s_e, s_r, mul)
                    ts2(s_e, s_e, c, add)
                ts2(s_k, s_k, -127.0, ALU.max, 128.0, ALU.min)
                ts2(s_k, s_k, 127.0, add, 8388608.0, mul)
                then(V.tensor_copy(s_t1.bitcast(mybir.dt.int32), s_k))
                tt2(out, s_e, s_t1, mul)

            def reduce_angle(out, x, k, clamp_out=None):
                ts2(k, x, 1.0 / TWO_PI, mul, ROUNDER, add)
                ts2(k, k, ROUNDER, sub)
                then(V.scalar_tensor_tensor(out, k, -TWO_PI_HI, x, mul, add))
                then(V.scalar_tensor_tensor(out, k, -TWO_PI_LO, out, mul, add))
                return V.tensor_scalar(out, out, PI_IN, -PI_IN, ALU.min, ALU.max)

            exp_to(s_dt, s_x)
            tt2(s_x, s_lr, s_dt, mul)
            exp_to(s_mag, s_x)
            ts2(s_x, s_x, 8.0, mul)
            exp_to(s_r8, s_x)
            tt2(s_x, s_li, s_dt, mul)
            reduce_angle(s_th, s_x, s_k).then_inc(ssm_angle, 1)
            dve.wait_ge(ssm_sin, 1)
            tt2(s_cos, s_half, s_half, mul)
            ts2(s_cos, s_cos, -2.0, mul, 1.0, add)
            V.memset(pw_re[:, 0, :], 1.0)
            V.memset(pw_im[:, 0, :], 0.0)
            tt2(pw_re[:, 1, :], s_mag, s_cos, mul)
            tt2(pw_im[:, 1, :], s_mag, s_sin, mul)

            def power_rows(first, count, by):
                lo, hi = slice(1, 1 + count), slice(first, first + count)
                xr = pw_re[:, by, :].unsqueeze(1).broadcast_to([SSM_P, count, SSM_G])
                xi = pw_im[:, by, :].unsqueeze(1).broadcast_to([SSM_P, count, SSM_G])
                n = count * SSM_G
                t0, t1 = (tt[q][:, 0:n].rearrange("p (a b) -> p a b", b=SSM_G) for q in range(2))
                tt2(t0, pw_re[:, lo, :], xr, mul)
                tt2(t1, pw_im[:, lo, :], xi, mul)
                tt2(pw_re[:, hi, :], t0, t1, sub)
                tt2(t0, pw_re[:, lo, :], xi, mul)
                tt2(t1, pw_im[:, lo, :], xr, mul)
                tt2(pw_im[:, hi, :], t0, t1, add)

            power_rows(2, 1, 1)
            power_rows(3, 2, 2)
            power_rows(5, 4, 4)
            for j in range(SUB):
                then(V.tensor_copy(rv_re[:, j, :], pw_re[:, SUB - 1 - j, :]))
                then(V.tensor_copy(rv_im[:, j, :], pw_im[:, SUB - 1 - j, :]))
            ts2(s_x, s_th, 8.0, mul)
            then(reduce_angle(s_phi, s_x, s_k))
            tt2(s_den, s_lr, s_lr, mul)
            tt2(s_t1, s_li, s_li, mul)
            tt2(s_den, s_den, s_t1, add)
            then(V.reciprocal(s_den, s_den))
            ts2(s_nr, pw_re[:, 1, :], 1.0, sub)
            tt2(s_t1, s_nr, s_lr, mul)
            tt2(s_t2, pw_im[:, 1, :], s_li, mul)
            tt2(s_fr, s_t1, s_t2, add)
            tt2(s_fr, s_fr, s_den, mul)
            tt2(s_t1, pw_im[:, 1, :], s_lr, mul)
            tt2(s_t2, s_nr, s_li, mul)
            tt2(s_fi, s_t1, s_t2, sub)
            tt2(s_fi, s_fi, s_den, mul)
            t0, t1 = (tt[q][:, 0:512].rearrange("p (a b) -> p a b", b=SSM_C) for q in range(2))
            fr = s_fr.unsqueeze(2).broadcast_to([SSM_P, SSM_G, SSM_C])
            fi = s_fi.unsqueeze(2).broadcast_to([SSM_P, SSM_G, SSM_C])
            tt2(t0, b_re, fr, mul)
            tt2(t1, b_im, fi, mul)
            tt2(bb_re, t0, t1, sub)
            tt2(t0, b_im, fr, mul)
            tt2(t1, b_re, fi, mul)
            tt2(bb_im, t0, t1, add)
            V.memset(bst.rearrange("p a b -> p (a b)"), 0.0)
            V.memset(toep.rearrange("p a b -> p (a b)"), 0.0).then_inc(toep_in, 16)
            then(V.memset(not_first.rearrange("p a b -> p (a b)"), 1.0))
            then(V.memset(not_first[:, :, 0], 0.0))
            then(V.memset(d_re[:, :, 0], 0.0))
            then(V.memset(d_im[:, :, 0], 0.0))
            for j in range(NT):
                b = wait_full(dve, G_U, j)
                V.tensor_tensor(U[:, j, :], ps[:, b, :], u_row, add).then_inc(drained[b], 1)
            for j in range(NT):
                wait_drained(dve, G_U, j)
            V.memset(s_t1, 0.0).then_inc(ssm_pre, 1)
            dve.wait_ge(ssm_pre, 1)

            with dve.Fori(0, SSM_ROUNDS) as i:
                own = [0]

                def chain(ins):
                    ins.then_inc(ssm_own, 1)
                    own[0] += 1
                    dve.wait_ge(ssm_own, i * SSM_OWN + own[0])

                def complex_product(out_re, out_im, a, b, t, conj=False, last_im=None):
                    (ar, ai), (br, bi) = a, b
                    chain(V.tensor_tensor(t[0], ar, br, mul))
                    chain(V.tensor_tensor(t[1], ai, bi, mul))
                    chain(V.tensor_tensor(out_re, t[0], t[1], add if conj else sub))
                    chain(V.tensor_tensor(t[0], ar, bi, mul))
                    chain(V.tensor_tensor(t[1], ai, br, mul))
                    return V.tensor_tensor(out_im, t[0], t[1], sub if conj else add)

                gs = bass.ds(i * GE, GE)

                def groups(x):
                    return x[:, :, gs].rearrange("p j g -> p g j")

                def lags(x, n):
                    return groups(x).unsqueeze(3).broadcast_to([SSM_P, GE, n, SSM_C])

                def chans(x, n):
                    return x[:, gs, :].unsqueeze(2).broadcast_to([SSM_P, GE, n, SSM_C])

                def split(x):
                    return x.rearrange("p g (j c) -> p g j c", c=SSM_C)

                def scratch(n):
                    return [tt[q][:, 0:GE * n * SSM_C].rearrange("p (g j c) -> p g j c", j=n, c=SSM_C)
                            for q in range(2)]

                chain(V.tensor_tensor(tt4[0], s_phi[:, gs].unsqueeze(2).broadcast_to([SSM_P, GE, P]),
                                      iota.unsqueeze(1).broadcast_to([SSM_P, GE, P]), mul))
                x, k = tt[0][:, 0:512], tt[1][:, 0:512]
                chain(V.tensor_scalar(k, x, 1.0 / TWO_PI, ROUNDER, mul, add))
                chain(V.tensor_scalar(k, k, ROUNDER, None, sub))
                chain(V.scalar_tensor_tensor(x, k, -TWO_PI_HI, x, mul, add))
                chain(V.scalar_tensor_tensor(x, k, -TWO_PI_LO, x, mul, add))
                V.tensor_scalar(x, x, PI_IN, -PI_IN, ALU.min, ALU.max).then_inc(ssm_angle, 1)
                V.tensor_tensor(r8, s_r8[:, gs].unsqueeze(2).broadcast_to([SSM_P, GE, P]), not_first, mul)
                Uv = U[:, :, bass.ds(i * (GE * SSM_C), GE * SSM_C)].rearrange("p j (g c) -> p g j c", c=SSM_C)
                Uqv = Uq.rearrange("p g (j c) -> p g j c", c=SSM_C)
                for g in range(GE):
                    ins = V.tensor_scalar(Uqv[:, g, :, :], Uv[:, g, :, :], 1.0, None, mul)
                ins.then_inc(ssm_u, 1)
                dve.wait_ge(ssm_u, i + 1)
                dve.wait_ge(ssm_trig, i + 1)
                chain(V.tensor_tensor(e_re, e_re, e_re, mul))
                chain(V.tensor_scalar(e_re, e_re, -2.0, 1.0, mul, add))
                t = scratch(9)
                chain(complex_product(split(v_re), split(v_im), (chans(c_re, 9), chans(c_im, 9)),
                                      (lags(pw_re, 9), lags(pw_im, 9)), t))
                chain(V.tensor_scalar(v_im, v_im, -1.0, None, mul))
                for n, x in enumerate((bb_re, bb_im)):
                    chain(V.tensor_scalar(bst[:, n, 0:GE * SSM_C].rearrange("p (g c) -> p g c", c=SSM_C), x[:, gs, :],
                                          1.0, None, mul))
                t = scratch(8)
                complex_product(split(wt_re), split(wt_im), (chans(bb_re, 8), chans(bb_im, 8)),
                                (lags(rv_re, 8), lags(rv_im, 8)), t).then_inc(ssm_w, 1)
                dve.wait_ge(ssm_w, i + 1)
                w = []
                for n in range(2):
                    b = wait_full(dve, G_SSM, 4 + n, i, SSM_ROUND)
                    w.append(ps[0:SSM_P, b, :].rearrange("p (g c) -> p g c", c=P)[:, :, 0:P - 1])
                er, ei = e_re[:, :, 1:P], e_im[:, :, 1:P]
                t = [tt4[0][:, :, 1:P], tt4[1][:, :, 1:P]]
                dr, di = d_re[:, :, 1:P], d_im[:, :, 1:P]
                chain(V.tensor_tensor(t[0], er, w[0], mul))
                chain(V.tensor_tensor(t[1], ei, w[1], mul))
                chain(V.tensor_tensor(dr, t[0], t[1], add))
                b1 = where(G_SSM, 5)[0]
                b0 = where(G_SSM, 4)[0]
                V.tensor_tensor(t[0], er, w[1], mul).then_inc(drained[b1], 1)
                V.tensor_tensor(t[1], ei, w[0], mul).then_inc(drained[b0], 1)
                wait_drained(dve, G_SSM, 5, i, SSM_ROUND)
                wait_drained(dve, G_SSM, 4, i, SSM_ROUND)
                chain(V.tensor_tensor(di, t[0], t[1], sub))

                def flat(x):
                    return x.rearrange("p a b -> p (a b)")
                chain(V.tensor_tensor_scan(flat(s_re), flat(r8), flat(d_re), 0.0, mul, add))
                chain(V.tensor_tensor_scan(flat(s_im), flat(r8), flat(d_im), 0.0, mul, add))
                complex_product(d_re, d_im, (e_re, e_im), (s_re, s_im), tt4).then_inc(ssm_state, 1)
                dve.wait_ge(ssm_state, i + 1)
                dv = d_row[:, bass.ds(i * (GE * SSM_C), GE * SSM_C)].rearrange("p (g c) -> p g c", c=SSM_C)
                ytv = yt.rearrange("p g (j c) -> p g j c", c=SSM_C)
                chain(V.tensor_tensor(ytv, Uqv, dv.unsqueeze(2).broadcast_to([P, GE, SUB, SSM_C]), mul))
                for n in range(2):
                    b = wait_full(dve, G_SSM, 6 + n, i, SSM_ROUND)
                    chain(V.tensor_tensor(yt[:, 2 * n:2 * n + 2, :], yt[:, 2 * n:2 * n + 2, :],
                                          ps[:, b, 0:2 * P].rearrange("p (g c) -> p g c", c=P), add))
                    for g in range(2 * n, 2 * n + 2):
                        ins = V.tensor_scalar(Uv[:, g, :, :], ytv[:, g, :, :], 1.0, None, mul)
                    ins.then_inc(drained[b], 1)
                    wait_drained(dve, G_SSM, 6 + n, i, SSM_ROUND)
                assert own[0] == SSM_OWN, own[0]

            dve.wait_ge(b2_in, 48)
            for b in range(2):
                then(V.memset(zp[b], 0.0))
            for ft in range(WT):
                z = zp[ft % 2]
                for h in range(2):
                    k = 2 * ft + h
                    wait_drained(dve, G_HCB, k)
                    b = wait_full(dve, G_HCB, 8 + k)
                    V.scalar_tensor_tensor(z[:, 2 * P + 512 * h:2 * P + 512 * h + 512], ps[:, b, :],
                                           bias_col[:, 4 + ft:5 + ft], BZ[:, ft, 512 * h:512 * h + 512],
                                           add, mul).then_inc(drained[b], 1)
                    wait_drained(dve, G_HCB, 8 + k)
                then(V.tensor_copy(z[:, 1:P], z[:, 8 * P:9 * P - 1]))
                then(V.tensor_copy(z[:, P + 1:2 * P], z[:, 9 * P:10 * P - 1]))
                o = BZ[:, ft, :]
                then(V.tensor_scalar(o, z[:, 0:SEQ], taps2[:, ft, 0:1], None, mul))
                then(V.scalar_tensor_tensor(o, z[:, P:P + SEQ], taps2[:, ft, 1:2], o, mul, add))
                then(V.scalar_tensor_tensor(o, z[:, 2 * P:2 * P + SEQ], taps2[:, ft, 2:3], o, mul, add))
            for k in range(8):
                b = wait_full(dve, G_HCB, 16 + k)
                o = BZ[:, k // 2, 512 * (k % 2):512 * (k % 2) + 512]
                V.scalar_tensor_tensor(o, ps[:, b, :], bias_col[:, 8 + k // 2:9 + k // 2], o, add, mul
                                       ).then_inc(drained[b], 1)
            for k in range(8):
                dve.wait_ge(sig_done, k + 1)
                hs = slice(512 * (k % 2), 512 * (k % 2) + 512)
                if k == 0:
                    wait_full(dve, G_YT, 7)
                b = where(G_GLU, k)[0]
                V.tensor_tensor(YA[:, k // 2, hs], gT[:, k // 2, hs], sig[k % 4], mul).then_inc(drained[b], 1)
            then(V.memset(s_t1, 0.0))
            for k in range(8):
                wait_drained(dve, G_GLU, k)
            V.memset(s_t2, 0.0).then_inc(merged_rows, 8)
            with dve.Fori(0, MRG_ROUNDS) as i:
                for ft in range(2):
                    for h in range(2):
                        r = 2 * ft + h
                        k0 = 4 * r
                        s0, s1 = sig[2 * (r % 2)], sig[2 * (r % 2) + 1]
                        for n, x in enumerate((s0, s1)):
                            wait_drained(dve, G_MRG, k0 + n, i, MRG_ROUND)
                            b = wait_full(dve, G_MRG, k0 + 2 + n, i, MRG_ROUND)
                            V.tensor_tensor(x, x, ps[:, b, :], mul).then_inc(drained[b], 1)
                        for n in range(2):
                            wait_drained(dve, G_MRG, k0 + 2 + n, i, MRG_ROUND)
                        V.tensor_tensor(M[:, bass.ds(i * 2 + ft, 1), 512 * h:512 * h + 512].rearrange("p a b -> p (a b)"),
                                        s0, s1, add).then_inc(merged_rows, 1)
            for h in range(2):
                for t in range(NT):
                    b = wait_full(dve, G_WO, 8 * h + t)
                    xs = X[:, t, 512 * h:512 * h + 512]
                    V.scalar_tensor_tensor(xs, xs, ALPHA, ps[:, b, :], mul, add).then_inc(drained[b], 1)

            def layer_rows(count):
                dve.wait_ge(ln_sum, count * NT)
                V.tensor_scalar(mean, ssum, -1.0 / D, None, mul).then_inc(ln_mean, 1)
                dve.wait_ge(ln_sq, count * NT)
                V.tensor_scalar(rs_arg[:, 0:NT], rstd, 1.0 / D, LN_EPS, mul, add).then_inc(root_ask, 1)
                inverse_root(NT)
                V.tensor_tensor(ssum, mean, rs_y[:, 0:NT], mul).then_inc(ln_mean2, 1)
                dve.wait_ge(gain_in, 16 * (3 + 2 * count))
                for j in range(NT):
                    dve.wait_ge(ln_scaled, (count - 1) * NT + j + 1)
                    then(V.tensor_tensor(X[:, j, :], xn[:, j, :], gain, mul))
                    V.tensor_tensor(X[:, j, :], X[:, j, :], shift, add).then_inc(ln_rows, 1)

            layer_rows(1)
            rest_features(G_LN1, 1)
            dve.wait_ge(ln_rows, 8)
            for j in range(NT):
                wait_full(dve, G_LN1, 2 * j + 1)
                ins = V.tensor_scalar(X[:, j, :], X[:, j, :], ALPHA, None, mul)
            then(ins)
            def rest_slab2(q, i):
                dve.wait_ge(v_hi, i * 3 + q + 1)
                V.tensor_tensor(ws2[q][1].ap(), wraw2[q], ws2[q][0].ap().bitcast(F32), sub).then_inc(v_lo, 1)
            for q in range(3):
                rest_slab2(q, 0)

            def f2_round(i, last):
                start, at = at_round(G_F2, i, F2_ROUND)
                for q in range(4):
                    wait_drained(dve, start, 2 * q, **at)
                    b = wait_full(dve, start, 2 * q + 1, **at)
                    V.tensor_tensor(hg[q % 2], hg[q % 2], ps[:, b, :], mul).then_inc(hid_f, 1)
                    dve.wait_ge(hid_hi, i * 4 + q + 1)
                    part = (slice(None), q // 2, slice(512 * (q % 2), 512 * (q % 2) + 512))
                    V.tensor_tensor(hids[1][part], hg[q % 2], hids[0][part].bitcast(F32), sub).then_inc(drained[b], 1)
                for t in range(NT):
                    if not last and t == 1:
                        for q in range(2):
                            rest_slab2(q, i + 1)
                    for h in range(2):
                        b = wait_full(dve, start, 8 + 2 * t + h, **at)
                        xs = X[:, t, 512 * h:512 * h + 512]
                        V.tensor_tensor(xs, xs, ps[:, b, :], add).then_inc(drained[b], 1)
                if not last:
                    rest_slab2(2, i + 1)
            rounds(dve, F2_ROUNDS, f2_round)
            for k in range(8, 24):
                wait_drained(dve, last_f2, k)
            layer_rows(2)


GDN_OWN = 12
SSM_OWN = 35
PI_IN = 3.1415925


def kernel(**inputs):
    import numpy as _np
    import concourse.bacc as _bacc
    from concourse import mybir as _mybir
    from concourse.bass_utils import run_bass_kernel_spmd as _run

    def c(a):
        return _np.ascontiguousarray(a)

    arrays = {n: c(inputs[n][0]) for n in ("x", "norm_mix", "w_in", "a_log_fwd", "dt_bias_fwd", "a_log_bwd",
                                           "dt_bias_bwd", "gdn_norm", "sgu_v_norm", "sgu_out_norm", "w_out",
                                           "norm_ffn", "w_ff1", "w_ff2")}
    arrays["norm_final"] = c(inputs["norm_final"])
    arrays["conv_wT"] = c(inputs["conv_w"][0].T)
    arrays["sgu_bT"] = c(inputs["sgu_b"][0].T)
    arrays["sgu_wT"] = c(_np.swapaxes(inputs["sgu_w"][0], 1, 2))
    arrays["shape_constants"] = shape_constants()
    for n in ("w_in", "glu_w", "w_ssm_out", "w_conv_out", "w_o", "ln1_g", "ln1_b", "w_gate", "w_up", "w_down",
              "ln2_g", "ln2_b", "ssm_d"):
        arrays[n if n != "w_in" else "w_in_2"] = c(inputs[n + "_2"][0])
    b_in = inputs["b_in_2"][0]
    arrays["b_in"] = c(b_in)
    arrays["bias_col"] = c(b_in[W2:].reshape(-1, P).T)
    arrays["glu_col"] = c(inputs["glu_b_2"][0].reshape(-1, P).T)
    arrays["conv_taps_2"] = c(inputs["conv_w_2"][0].T.reshape(WT, P, 3).transpose(1, 0, 2).reshape(P, WT * 3))
    arrays["lam_re"] = c(inputs["ssm_lambda_re_2"][0].T)
    arrays["lam_im"] = c(inputs["ssm_lambda_im_2"][0].T)
    arrays["log_dt"] = c(inputs["ssm_log_dt_2"][0])
    arrays["b_re"] = c(inputs["ssm_b_re_2"][0].transpose(1, 0, 2))
    arrays["b_im"] = c(inputs["ssm_b_im_2"][0].transpose(1, 0, 2))
    arrays["c_re"] = c(inputs["ssm_c_re_2"][0].transpose(2, 0, 1))
    arrays["c_im"] = c(inputs["ssm_c_im_2"][0].transpose(2, 0, 1))
    arrays["counts"] = _np.arange(P, dtype=_np.float32)

    nc = _bacc.Bacc("TRN2", target_bir_lowering=False, num_devices=1)
    A = {n: nc.dram_tensor(f"in_{n}", a.shape, _mybir.dt.from_np(a.dtype), kind="ExternalInput").ap()
         for n, a in arrays.items()}
    out = nc.dram_tensor("out_x", (SEQ, D), F32, kind="ExternalOutput").ap()
    build(nc, A, out, A["shape_constants"])
    r = _run(nc, [{f"in_{n}": a for n, a in arrays.items()}], core_ids=[0])
    return r.results[0]["out_x"].reshape(1, SEQ, D)
```

```python
from contextlib import ExitStack

import numpy as np

import concourse.bass as bass
from concourse import mybir

F32 = mybir.dt.float32
F32R = mybir.dt.float32r
ALU = mybir.AluOpType
ACT = mybir.ActivationFunctionType
AX_X = mybir.AxisListType.X

P = 128
SEQ = 1024
D = 1024
NT = SEQ // P
KT = D // P
BANKS = 8
HEADS, HD = 8, 64
GW = HEADS * HD
CONV_K = 5
SG = 4
FF = 4096
EPS = 1e-6
LN_EPS = 1e-5
ALPHA = 2.0 ** 0.25
W2 = 512
WT = W2 // P
SSM_C = 16
SSM_G = W2 // SSM_C
SSM_P = 64
SUB = 8
GE = 4
SSM_ROUNDS = SSM_G // GE
F2 = 2816
F2_ROUNDS = F2 // 256
TWO_PI = 2.0 * np.pi
TWO_PI_HI = 6.28125
TWO_PI_LO = float(TWO_PI - 6.28125)
LN2_HI = 0.693359375
LN2_LO = float(np.log(2.0) - 0.693359375)
ROUNDER = 12582912.0
LEVELS = 7
MASKS = 2 * LEVELS + 4


def shape_constants():
    i = np.arange(P)[:, None]
    j = np.arange(P)[None, :]
    out = np.zeros((P, MASKS, P), np.float32)
    for lv in range(LEVELS):
        b = 1 << lv
        low = (i // (2 * b) == j // (2 * b)) & ((i // b) % 2 == 1) & ((j // b) % 2 == 0)
        out[:, lv] = low
        out[:, LEVELS + lv] = low.T
    out[:, 2 * LEVELS] = i <= j
    out[:, 2 * LEVELS + 1] = i >= j
    out[:, 2 * LEVELS + 2] = i == j
    out[:, 2 * LEVELS + 3] = 1.0
    return out


G_NORM1 = 0
G_QKV = G_NORM1 + 16
G_ROWS = G_QKV + 48
G_SGU = G_ROWS + 25
G_GDN = G_SGU + 16


def gdn_order():
    both, batches = (0, 1), [(d, h) for d in (0, 1) for h in (0, 1)]
    order = [("sums", d) for d in both] + [("rows", *x) for x in batches]
    order += [("keys", d) for d in both] + [("queries", d) for d in both]
    order += [("kk", *x) for x in batches] + [("kq", *x) for x in batches] + [("U", 0, *x) for x in batches]
    for lv in range(1, LEVELS):
        for name in ("Q", "T", "U"):
            order += [(name, lv, *x) for x in batches]
    for name in ("u", "w", "wS", "o"):
        order += [(name, *x) for x in batches]
    order += [("kv", d) for d in both]
    return {key: n for n, key in enumerate(order)}


GDN_AT = gdn_order()
GDN_ROUND = len(GDN_AT)
assert GDN_ROUND % BANKS == 0
G_MIXT = G_GDN + NT * GDN_ROUND
G_WOUT = G_MIXT + 8
G_NORM2 = G_WOUT + 16
G_FF = G_NORM2 + 16
FF_ROUND = 24
FF_ROUNDS = FF // 512
G_NORM3 = G_FF + FF_ROUNDS * FF_ROUND
G_U = G_NORM3 + 16
G_SSM = G_U + 8
SSM_ROUND = 8
G_HCB = G_SSM + SSM_ROUNDS * SSM_ROUND
G_YT = G_HCB + 24
G_GLU = G_YT + 8
G_MRG = G_GLU + 8
MRG_ROUND = 16
MRG_ROUNDS = 4
G_WO = G_MRG + MRG_ROUNDS * MRG_ROUND
G_LN1 = G_WO + 16
G_F2 = G_LN1 + 16
F2_ROUND = 24


def build(nc, A, out, consts):
    with ExitStack() as ctx:
        def sem(name):
            return ctx.enter_context(nc.semaphore(name))

        WORDS = 52736
        arena = (nc.sbuf_base + 31) // 32 * 32
        sb = ctx.enter_context(nc.sbuf_tensor("sb", [P, WORDS], F32))
        ps = ctx.enter_context(nc.psum_tensor("ps", [P, BANKS, 512], F32))

        def area(at, *shape, parts=P):
            size = int(np.prod(shape))
            assert at + size <= WORDS
            v = sb[0:parts, at:at + size]
            if len(shape) == 2:
                v = v.rearrange("p (a b) -> p a b", b=shape[1])
            elif len(shape) == 3:
                v = v.rearrange("p (a b c) -> p a b c", b=shape[1], c=shape[2])
            return v

        def split_area(name, at, *shape):
            assert at + int(np.prod(shape)) <= WORDS
            return nc.alloc_sbuf_tensor_at(name, [P, *shape], F32R, offset=arena + 4 * at)

        def plain_area(name, at, *shape):
            assert at + int(np.prod(shape)) <= WORDS
            return nc.alloc_sbuf_tensor_at(name, [P, *shape], F32, offset=arena + 4 * at).ap()

        AT_X, AT_H, AT_W, AT_WORK, AT_CONST = 0, 8192, 16384, 24576, 46336
        X = area(AT_X, NT, D)
        H = area(AT_H, KT, SEQ)
        ring = [area(AT_W, 8, 512), area(AT_W + 4096, 8, 512)]
        ring_wide = [area(AT_W, 4, 1024), area(AT_W + 4096, 4, 1024)]
        masks = area(AT_CONST, MASKS, P)
        ident, ones = masks[:, 2 * LEVELS + 2, :], masks[:, 2 * LEVELS + 3, :]
        at = AT_CONST + MASKS * P
        gain = area(at, D)
        shift = area(at + D, D)
        at += 2 * D
        ssum = area(at, NT)
        rstd = area(at + 8, NT)
        mean = area(at + 16, NT)
        at += 32
        sgu_vg = area(at, SG, P)
        sgu_og = area(at + 512, SG, P)
        at += 1024
        sgu_bt = area(at, SG)
        conv_taps = area(at + 4, 12, CONV_K)
        gdn_gain = area(at + 64, HD)
        dt_row = area(at + 128, 16)
        alog_row = area(at + 144, 16)
        rs_arg, rs_root, rs_y, rs_t = (area(at + 160 + 128 * n, 128) for n in range(4))
        assert at + 672 <= WORDS

        QKV = area(AT_WORK, NT, 3 * GW)
        Z = area(AT_X, NT, GW)
        SU = area(AT_X + 4096, NT, GW)
        SV = area(AT_WORK + 12288, NT, GW)
        O = SV
        TMP = AT_WORK + 16384
        raw = [area(TMP + 1028 * b, 1028) for b in range(2)]
        cv = [area(TMP + 2056 + 1024 * b, SEQ) for b in range(2)]
        GT = TMP + 4104
        wgate = area(GT, KT, 32)
        graw = area(GT + 256, NT, 32)
        gdec = area(GT + 512, NT, 16)
        gbeta = area(GT + 640, NT, 16)
        gt1 = area(GT + 768, NT, 16)
        gt2 = area(GT + 896, NT, 16)
        assert GT + 1024 <= AT_CONST
        sgu_w = area(TMP, SG, P)
        sq = area(TMP + 512, 1024)
        vst = area(TMP + 1536, 16)
        Lm, Tm, Um, Cm = ([area(AT_W + 1024 * (2 * n + d), HEADS, P) for d in range(2)] for n in range(4))
        gd = AT_X + 4096
        Qt, DTm = ([area(gd + 1024 * (2 * n + d), HEADS, P) for d in range(2)] for n in range(2))
        Rm = Qt
        KTr, QTr, QdT, wT = ([area(AT_H + 512 * (2 * n + d), 4, P) for d in range(2)] for n in range(4))
        KQ = [area(TMP + 1024 * d, 2 * HEADS, HD) for d in range(2)]
        un = [x[:, 0:HEADS, :] for x in KQ]
        vnew = [x[:, HEADS:, :] for x in KQ]
        Kbe, Kdec = ([area(TMP + 2048 + 512 * (2 * n + d), HEADS, HD) for d in range(2)] for n in range(2))
        S = [area(TMP + 4096 + 256 * d, 4, HD) for d in range(2)]
        gd = AT_CONST + MASKS * P
        Vb = [area(gd + 512 * d, HEADS, HD) for d in range(2)]
        exin = [area(gd + 1024 + 64 * d, 3, HEADS) for d in range(2)]
        ex = [area(gd + 1152 + 64 * d, 3, HEADS) for d in range(2)]
        bege = [area(gd + 1280 + 64 * d, HEADS) for d in range(2)]
        egl = [area(gd + 1408 + 64 * d, 4) for d in range(2)]

        def batch(x, h):
            return x[:, h:HEADS:2]

        def half(x, head):
            lo = HD * (head % 2)
            return x[lo:lo + HD, head // 2, :]

        def level_columns(x, lv, d):
            width = 1 << lv
            return x.rearrange("p k (n a b) -> p k n a b", a=2, b=width)[:, :, :, d, :]

        mixT = H
        xin = area(AT_WORK, NT, D)
        Hs = [split_area(f"H_{n}", AT_H + 8192 * q, KT, SEQ) for q, n in enumerate(("hi", "lo"))]
        ffs = [split_area(f"ff_{n}", AT_WORK + 4096 * q, 4, SEQ) for q, n in enumerate(("hi", "lo"))]
        ws = [[split_area(f"w{b}_{n}", AT_WORK + 8192 + 4096 * b + 2048 * q, 2048) for q, n in enumerate(("hi", "lo"))]
              for b in range(2)]
        wraw = [plain_area(f"wraw{b}", AT_WORK + 16384 + 2048 * b, 2048) for b in range(2)]
        fft = [plain_area(f"fft{b}", AT_WORK + 20480 + 512 * b, 512) for b in range(2)]
        xn = area(AT_WORK + 8192, NT, D)

        BZ = area(AT_WORK, WT, SEQ)
        U = area(AT_WORK + 4096, NT, W2)
        YA = area(AT_WORK + 4096, WT, SEQ)
        M = area(AT_WORK + 8192, KT, SEQ)
        gT = area(AT_WORK + 8192, WT, SEQ)
        T2 = AT_WORK + 16384
        zp = [area(T2 + 1280 * b, 10 * P) for b in range(2)]
        d_row = area(T2 + 2560, W2)
        u_row = area(T2 + 3072, W2)
        sig = [area(T2 + 512 * b, 512) for b in range(4)]
        hids = [split_area(f"hid_{n}", AT_WORK + 2048 * q, 2, SEQ) for q, n in enumerate(("hi", "lo"))]
        ws2 = [[split_area(f"v{b}_{n}", AT_WORK + 4096 + 4096 * b + 2048 * q, 2048) for q, n in enumerate(("hi", "lo"))]
               for b in range(3)]
        wraw2 = [plain_area(f"vraw{b}", AT_WORK + 16384 + 2048 * b, 2048) for b in range(3)]
        hg = [plain_area(f"hg{b}", AT_WORK + 16384 + 6144 + 512 * b, 512) for b in range(2)]
        assert AT_WORK + 16384 + 6144 + 1024 <= AT_CONST + 2 * LEVELS * P
        at2 = AT_CONST
        bias_col = area(at2, 28)
        glu_col = area(at2 + 28, WT)
        taps2 = area(at2 + 32, WT, 3)
        bias_now = area(at2 + 44, 2, 2)
        at2 += 64

        def small(n):
            return area(at2 + 32 * n, SSM_G, parts=SSM_P)
        (s_lr, s_li, s_dt, s_x, s_k, s_r, s_e, s_mag, s_th, s_sin, s_cos, s_half, s_den, s_nr, s_fr, s_fi,
         s_phi, s_r8, s_t1, s_t2) = (small(n) for n in range(20))
        at2 += 640
        pw_re = area(at2, 9, SSM_G, parts=SSM_P)
        pw_im = area(at2 + 288, 9, SSM_G, parts=SSM_P)
        assert at2 + 576 <= AT_CONST + 2 * LEVELS * P
        sm = AT_WORK
        b_re, b_im, c_re, c_im = (area(sm + 512 * n, SSM_G, SSM_C, parts=SSM_P) for n in range(4))
        bb_re, bb_im = (area(sm + 2048 + 512 * n, SSM_G, SSM_C, parts=SSM_P) for n in range(2))
        rv_re, rv_im = (area(sm + 3072 + 256 * n, SUB, SSM_G, parts=SSM_P) for n in range(2))
        bst = area(sm + 3584, 2, 192, parts=SSM_P)
        iota = area(sm + 3968, P, parts=SSM_P)
        sm = AT_WORK + 8192
        wt_re, wt_im = (area(sm + 512 * n, GE, SUB * SSM_C, parts=SSM_P) for n in range(2))
        v_re, v_im = (area(sm + 1024 + 576 * n, GE, 9 * SSM_C, parts=SSM_P) for n in range(2))
        kall = area(sm + 2176, GE, P, parts=SSM_C)
        toep = area(sm + 2688, GE, P)
        wl_re, wl_im = (area(sm + 3200 + 256 * n, GE, SSM_P) for n in range(2))
        e_re, e_im = (area(sm + 3712 + 512 * n, GE, P, parts=SSM_P) for n in range(2))
        r8 = area(sm + 4736, GE, P, parts=SSM_P)
        d_re, d_im = (area(sm + 5248 + 512 * n, GE, P, parts=SSM_P) for n in range(2))
        uT = area(sm + 6272, GE, P)
        Uq = area(sm + 6784, GE, P)
        not_first = area(sm + 7296, GE, P, parts=SSM_P)
        tt = [area(T2 + 576 * n, 576, parts=SSM_P) for n in range(2)]
        tt4 = [area(T2 + 576 * n, GE, P, parts=SSM_P) for n in range(2)]
        s_re, s_im = wt_re, wt_im
        yt = area(T2 + 1152, GE, P)

        b2_in = sem("b2_in")
        ssm_in = sem("ssm_in")
        ssm_sin = sem("ssm_sin")
        ssm_half = sem("ssm_half")
        ssm_own = sem("ssm_own")
        ssm_pre = sem("ssm_pre")
        ssm_w = sem("ssm_w")
        ssm_k = sem("ssm_k")
        ssm_u = sem("ssm_u")
        ssm_angle = sem("ssm_angle")
        ssm_trig = sem("ssm_trig")
        ssm_state = sem("ssm_state")
        toep_in = sem("toep_in")
        cgate = sem("cgate")
        z_own = sem("z_own")
        sig_done = sem("sig_done")
        mrg_own = sem("mrg_own")
        f2_gate = sem("f2_gate")
        ln_sum = sem("ln_sum")
        ln_mean = sem("ln_mean")
        ln_sq = sem("ln_sq")
        ln_scaled = sem("ln_scaled")
        ln_rows = sem("ln_rows")
        merged_rows = sem("merged_rows")
        alpha_done = sem("alpha_done")
        ln_mean2 = sem("ln_mean2")
        bias_set = sem("bias_set")

        full = [sem(f"full{b}") for b in range(BANKS)]
        drained = [sem(f"drained{b}") for b in range(BANKS)]
        consts_in = sem("consts_in")
        x_in = sem("x_in")
        slab_in = [sem(f"slab_in{b}") for b in range(2)]
        gain_in = sem("gain_in")
        wgate_in = sem("wgate_in")
        sguw_in = sem("sguw_in")
        dve_step = sem("dve_step")
        act_step = sem("act_step")
        norm_sums = sem("norm_sums")
        norm_rows = sem("norm_rows")
        root_ask = sem("root_ask")
        root_done = sem("root_done")
        conv_done = sem("conv_done")
        silu_done = sem("silu_done")
        pads_set = sem("pads_set")
        gate_in = sem("gate_in")
        gate_out = sem("gate_out")
        sgu_v = sem("sgu_v")
        sgu_o = sem("sgu_o")
        gdn_ready = sem("gdn_ready")
        gdn_rg = sem("gdn_rg")
        gdn_exin = sem("gdn_exin")
        gdn_ex = sem("gdn_ex")
        gdn_stage = sem("gdn_stage")
        gdn_go = sem("gdn_go")
        gdn_rexp = sem("gdn_rexp")
        gdn_din = sem("gdn_din")
        gdn_dexp = sem("gdn_dexp")
        gdn_vk = sem("gdn_vk")
        gdn_t0 = sem("gdn_t0")
        gdn_c = sem("gdn_c")
        gdn_qd = sem("gdn_qd")
        gdn_step = sem("gdn_step")
        gdn_over = sem("gdn_over")
        mix_rows = sem("mix_rows")
        xin_in = sem("xin_in")
        relu_done = sem("relu_done")
        square_done = sem("square_done")
        raw_in = [sem(f"raw_in{b}") for b in range(2)]
        raw2_in = [sem(f"raw2_in{b}") for b in range(3)]
        w_hi = sem("w_hi")
        w_lo = sem("w_lo")
        v_hi = sem("v_hi")
        v_lo = sem("v_lo")
        feat_hi = sem("feat_hi")
        ff_hi = sem("ff_hi")
        hid_f = sem("hid_f")
        hid_hi = sem("hid_hi")
        out_done = sem("out_done")

        block = ctx.enter_context(nc.Block())

        def where(start, k, i=None, per=0):
            g = start + k
            use = g // BANKS
            return g % BANKS, (use if i is None else i * (per // BANKS) + use)

        def wait_full(eng, start, k, i=None, per=0):
            b, use = where(start, k, i, per)
            eng.wait_ge(full[b], use + 1)
            return b

        def wait_drained(eng, start, k, i=None, per=0):
            b, use = where(start, k, i, per)
            eng.wait_ge(drained[b], use + 1)

        def wait_bank(eng, start, k, i=None, per=0):
            b, use = where(start, k, i, per)
            if i is not None or use > 0:
                eng.wait_ge(drained[b], use)
            return b

        HI_LO = ((0, 0), (0, 1), (1, 0))

        FF_SLAB_END = (3, 7, 15, 23)

        def ff_slab_done(eng, q, i):
            start = G_FF if q >= 0 else G_FF - FF_ROUND
            if isinstance(i, int):
                if q >= 0 or i > 0:
                    wait_full(eng, start + i * FF_ROUND, FF_SLAB_END[q])
            else:
                wait_full(eng, start, FF_SLAB_END[q], i, FF_ROUND)

        def at_round(start, i, per):
            return (start + i * per, {}) if isinstance(i, int) else (start, dict(i=i, per=per))

        def rounds(eng, count, body):
            with eng.Fori(0, count - 1) as i:
                body(i, False)
            body(count - 1, True)

        def strided_view(hview):
            return hview.rearrange("p k (c j) -> p k c j", j=8)

        last_mrg = G_MRG + (MRG_ROUNDS - 1) * MRG_ROUND
        last_f2 = G_F2 + (F2_ROUNDS - 1) * F2_ROUND
        w_in, w_out, w_ff1, w_ff2 = A["w_in"], A["w_out"], A["w_ff1"], A["w_ff2"]
        Z0 = 3 * GW
        SU0 = 4 * GW + 4 * HEADS
        slab_cols = [0, 512, 1024, Z0, SU0, SU0 + GW]
        slab_last = [(G_QKV, 13), (G_QKV, 29), (G_QKV, 45), (G_ROWS, 7), (G_ROWS, 15), (G_ROWS, 23),
                     (G_WOUT, 7), (G_WOUT, 15)]
        def dense_at(ct):
            return 2 * ct if ct == 0 else 4 * ct - 2
        def turn_at(ct):
            return 4 * ct + 4 if ct < 11 else 46

        @block.sync
        def _(sp):
            xv = A["x"].rearrange("(p j) d -> p j d", j=NT)
            for h in range(2):
                sp.dma_start(X[:, 4 * h:4 * h + 4, :], xv[:, 4 * h:4 * h + 4, :]).then_inc(x_in, 16)
            sp.dma_start(gain, A["norm_mix"].partition_broadcast(P)).then_inc(gain_in, 16)
            sp.dma_start(masks, consts).then_inc(consts_in, 16)
            sp.dma_start(conv_taps, A["conv_wT"].rearrange("(t p) k -> p t k", p=P)).then_inc(consts_in, 16)
            sp.dma_start(sgu_vg, A["sgu_v_norm"].partition_broadcast(P)).then_inc(consts_in, 16)
            sp.dma_start(sgu_og, A["sgu_out_norm"].partition_broadcast(P)).then_inc(consts_in, 16)
            sp.dma_start(sgu_bt, A["sgu_bT"]).then_inc(consts_in, 16)
            sp.dma_start(gdn_gain, A["gdn_norm"].partition_broadcast(P)).then_inc(consts_in, 16)
            sp.dma_start(dt_row[:, 0:8], A["dt_bias_fwd"].partition_broadcast(P)).then_inc(consts_in, 16)
            sp.dma_start(dt_row[:, 8:16], A["dt_bias_bwd"].partition_broadcast(P)).then_inc(consts_in, 16)
            sp.dma_start(alog_row[:, 0:8], A["a_log_fwd"].partition_broadcast(P)).then_inc(consts_in, 16)
            sp.dma_start(alog_row[:, 8:16], A["a_log_bwd"].partition_broadcast(P)).then_inc(consts_in, 16)
            sp.dma_start(wgate, w_in[:, 4 * GW:4 * GW + 32].rearrange("(k p) n -> p k n", p=P)).then_inc(wgate_in, 16)
            for n, c0 in enumerate(slab_cols):
                if n >= 2:
                    wait_full(sp, *slab_last[n - 2])
                sp.dma_start(ring[n % 2], w_in[:, c0:c0 + 512].rearrange("(k p) n -> p k n", p=P)
                             ).then_inc(slab_in[n % 2], 16)
                if n == 4:
                    wait_drained(sp, G_QKV, 47)
                    sp.dma_start(sgu_w, A["sgu_wT"].rearrange("g s t -> s g t")).then_inc(sguw_in, 16)
            sp.wait_ge(gdn_over, 1)
            for h in range(2):
                sp.dma_start(xin[:, 4 * h:4 * h + 4, :], xv[:, 4 * h:4 * h + 4, :]).then_inc(xin_in, 16)
            for h in range(2):
                sp.dma_start(ring[h], w_out[:, 512 * h:512 * h + 512].rearrange("(k p) n -> p k n", p=P)
                             ).then_inc(slab_in[h], 16)
            wait_full(sp, G_NORM1, 15)
            sp.dma_start(gain, A["norm_ffn"].partition_broadcast(P)).then_inc(gain_in, 16)
            w1v = w_ff1.rearrange("(k p) (r n) -> p k r n", p=P, n=256)
            w2v = w_ff2.rearrange("(r k p) n -> p r k n", k=4, p=P)

            def ff_load(q, i):
                row = bass.ds(i, 1)
                dst = wraw[q % 2]
                if q < 2:
                    src = w1v[:, :, bass.ds(i * 2 + q, 1), :]
                    dst = dst.rearrange("p (k n) -> p k n", n=256)
                else:
                    src = w2v[:, row, :, 512 * (q - 2):512 * (q - 2) + 512]
                    dst = dst.rearrange("p (k n) -> p k n", n=512)
                sp.dma_start(dst, src).then_inc(raw_in[q % 2], 16)

            def ff_loads(i, last):
                for q in range(4):
                    if isinstance(i, int) or q > -1:
                        sp.wait_ge(w_lo, i * 4 + q + 1)
                    if q < 2:
                        ff_load(q + 2, i)
                    elif not last:
                        ff_load(q - 2, i + 1)

            wait_full(sp, G_WOUT, 15)
            ff_load(0, 0)
            ff_load(1, 0)
            rounds(sp, FF_ROUNDS, ff_loads)
            wait_full(sp, G_NORM2, 15)
            sp.dma_start(gain, A["norm_final"].partition_broadcast(P)).then_inc(gain_in, 16)
            last_ff = G_FF + (FF_ROUNDS - 1) * FF_ROUND
            wi2 = A["w_in_2"].rearrange("(k p) n -> p k n", p=P)
            wait_full(sp, last_ff, 7)
            sp.dma_start(ring[0], wi2[:, :, 0:512]).then_inc(slab_in[0], 16)
            sp.dma_start(bias_col, A["bias_col"]).then_inc(b2_in, 16)
            sp.dma_start(glu_col, A["glu_col"]).then_inc(b2_in, 16)
            sp.dma_start(taps2, A["conv_taps_2"].rearrange("p (t k) -> p t k", k=3)).then_inc(b2_in, 16)
            sp.dma_start(ring[1], wi2[:, :, 512:1024]).then_inc(slab_in[1], 16)
            wait_full(sp, last_ff, 23)
            sp.dma_start(s_lr, A["lam_re"]).then_inc(ssm_in, 16)
            sp.dma_start(s_li, A["lam_im"]).then_inc(ssm_in, 16)
            sp.dma_start(s_x, A["log_dt"].partition_broadcast(SSM_P)).then_inc(ssm_in, 16)
            for dst, name in ((b_re, "b_re"), (b_im, "b_im"), (c_re, "c_re"), (c_im, "c_im")):
                sp.dma_start(dst, A[name]).then_inc(ssm_in, 16)
            sp.dma_start(iota, A["counts"].partition_broadcast(SSM_P)).then_inc(ssm_in, 16)
            sp.dma_start(d_row, A["ssm_d"].partition_broadcast(P)).then_inc(ssm_in, 16)
            sp.dma_start(u_row, A["b_in"].rearrange("(a n) -> a n", a=1)[0, 0:W2].partition_broadcast(P)).then_inc(ssm_in, 16)
            sp.wait_ge(norm_rows, 24)
            sp.dma_start(gain, A["ln1_g"].partition_broadcast(P)).then_inc(gain_in, 16)
            sp.dma_start(shift, A["ln1_b"].partition_broadcast(P)).then_inc(gain_in, 16)
            with sp.Fori(0, SSM_ROUNDS) as i:
                wait_drained(sp, G_SSM, 2, i, SSM_ROUND)
                for lag in range(SUB):
                    rows = slice(SSM_C * lag, SSM_C * (lag + 1))
                    sp.dma_start(toep[rows, :, SSM_C * lag:P], kall[:, :, 0:P - SSM_C * lag]).then_inc(toep_in, 16)
            wait_full(sp, G_U, 7)
            sp.dma_start(ring[0], wi2[:, :, 1024:1536]).then_inc(slab_in[0], 16)
            wait_full(sp, G_HCB, 7)
            sp.dma_start(ring[1], wi2[:, :, 1536:2048]).then_inc(slab_in[1], 16)
            wait_full(sp, G_HCB, 15)
            sp.dma_start(ring[0][:, 0:4, :], A["glu_w"].rearrange("(k p) n -> p k n", p=P)).then_inc(slab_in[0], 16)
            wsv = A["w_ssm_out"].rearrange("(k p) (n c) -> p k n c", p=P, c=4)
            wcv = A["w_conv_out"].rearrange("(k p) (n c) -> p k n c", p=P, c=4)
            with sp.Fori(0, MRG_ROUNDS) as i:
                wait_full(sp, G_MRG - MRG_ROUND, 13, i, MRG_ROUND)
                sp.dma_start(ring[1][:, :, 0:256], wi2[:, :, bass.ds(i * 256 + 2048, 256)]).then_inc(slab_in[1], 16)
                sp.dma_start(ring[1][:, :, 256:512], wi2[:, :, bass.ds(i * 256 + 3072, 256)]).then_inc(slab_in[1], 16)
                wait_full(sp, G_MRG - MRG_ROUND, 15, i, MRG_ROUND)
                sp.dma_start(ring[0][:, 0:4, 0:256].rearrange("p k (n c) -> p k n c", c=4), wsv[:, :, bass.ds(i * 64, 64), :]).then_inc(slab_in[0], 16)
                sp.dma_start(ring[0][:, 0:4, 256:512].rearrange("p k (n c) -> p k n c", c=4), wcv[:, :, bass.ds(i * 64, 64), :]).then_inc(slab_in[0], 16)
            wov = A["w_o"].rearrange("(k p) n -> p k n", p=P)
            last_mrg = G_MRG + (MRG_ROUNDS - 1) * MRG_ROUND
            wait_full(sp, last_mrg, 13)
            sp.dma_start(ring[1], wov[:, :, 0:512]).then_inc(slab_in[1], 16)
            wait_full(sp, last_mrg, 15)
            sp.dma_start(ring[0], wov[:, :, 512:1024]).then_inc(slab_in[0], 16)
            wgv = A["w_gate"].rearrange("(k p) n -> p k n", p=P)
            wuv = A["w_up"].rearrange("(k p) n -> p k n", p=P)
            wgv = A["w_gate"].rearrange("(k p) (r n) -> p k r n", p=P, n=P)
            wuv = A["w_up"].rearrange("(k p) (r n) -> p k r n", p=P, n=P)
            wdv = A["w_down"].rearrange("(r k p) n -> p r k n", k=2, p=P)

            def f2_load(q, i):
                if q < 2:
                    dst = wraw2[q].rearrange("p (k n) -> p k n", n=256)
                    for n, src in enumerate((wgv, wuv)):
                        sp.dma_start(dst[:, :, P * n:P * n + P], src[:, :, bass.ds(i * 2 + q, 1), :]
                                     ).then_inc(raw2_in[q], 16)
                else:
                    sp.dma_start(wraw2[2].rearrange("p (k n) -> p k n", n=D), wdv[:, bass.ds(i, 1), :, :]
                                 ).then_inc(raw2_in[2], 16)

            def f2_loads(i, last):
                for q in range(3):
                    sp.wait_ge(v_lo, i * 3 + q + 1)
                    if not last:
                        f2_load(q, i + 1)

            wait_drained(sp, G_LN1, 15)
            for q in range(3):
                f2_load(q, 0)
            rounds(sp, F2_ROUNDS, f2_loads)
            sp.wait_ge(ln_rows, 8)
            sp.dma_start(gain, A["ln2_g"].partition_broadcast(P)).then_inc(gain_in, 16)
            sp.dma_start(shift, A["ln2_b"].partition_broadcast(P)).then_inc(gain_in, 16)
            ov = out.rearrange("(p j) d -> p j d", j=NT)
            for j in range(NT):
                sp.wait_ge(ln_rows, 8 + j + 1)
                sp.dma_start(ov[:, j, :], X[:, j, :]).then_inc(out_done, 16)
            sp.wait_ge(out_done, 16 * NT)

        @block.tensor
        def _(pe):
            def turn(dst, src):
                return nc.tensor.transpose(dst, src, ident)

            def rows_to_features(start, src):
                for j in range(NT):
                    pe.wait_ge(norm_rows, norm_base[0] + j + 1)
                    for h in range(2):
                        b = wait_bank(pe, start, 2 * j + h)
                        for q in range(4):
                            k = 4 * h + q
                            mm = turn(ps[:, b, q * P:(q + 1) * P], src[:, j, k * P:(k + 1) * P])
                        mm.then_inc(full[b], 1)
                norm_base[0] += NT

            norm_base = [0]
            pe.wait_ge(consts_in, 16 * 10)
            rows_to_features(G_NORM1, xn)

            wait_drained(pe, G_NORM1, 14)
            wait_drained(pe, G_NORM1, 15)
            for b in range(6):
                wait_drained(pe, G_NORM1, 8 + b)

            def feature_tile(slot, ft, start, k0, kts=KT, src=H):
                for h in range(2):
                    b = wait_bank(pe, start, k0 + h)
                    for k in range(kts):
                        mm = nc.tensor.matmul(ps[:, b, :], ring[slot][:, k, ft * P:(ft + 1) * P],
                                              src[:, k, h * 512:h * 512 + 512], start=(k == 0), stop=(k == kts - 1))
                    mm.then_inc(full[b], 1)

            for ct in range(13):
                if ct < 12:
                    n = ct // 4
                    if ct % 4 == 0:
                        pe.wait_ge(slab_in[n % 2], 16 * (n // 2 + 1))
                    feature_tile(n % 2, ct % 4, G_QKV, dense_at(ct))
                if ct >= 1:
                    pe.wait_ge(silu_done, ct)
                    for h in range(2):
                        b = wait_bank(pe, G_QKV, turn_at(ct - 1) + h)
                        for q in range(4):
                            t = 4 * h + q
                            mm = turn(ps[:, b, q * P:(q + 1) * P], cv[(ct - 1) % 2][:, t * P:(t + 1) * P])
                        mm.then_inc(full[b], 1)

            def row_tiles(slot, start, k0, kts=KT, src=H):
                for t in range(NT):
                    b = wait_bank(pe, start, k0 + t)
                    for k in range(kts):
                        mm = nc.tensor.matmul(ps[:, b, :], src[:, k, t * P:(t + 1) * P], ring[slot][:, k, :],
                                              start=(k == 0), stop=(k == kts - 1))
                    mm.then_inc(full[b], 1)

            for n in range(3, 6):
                pe.wait_ge(slab_in[n % 2], 16 * (n // 2 + 1))
                row_tiles(n % 2, G_ROWS, 8 * (n - 3))
            pe.wait_ge(wgate_in, 16)
            b = wait_bank(pe, G_ROWS, 24)
            for t in range(NT):
                for k in range(KT):
                    mm = nc.tensor.matmul(ps[:, b, t * 32:(t + 1) * 32], H[:, k, t * P:(t + 1) * P], wgate[:, k, :],
                                          start=(k == 0), stop=(k == KT - 1))
            mm.then_inc(full[b], 1)

            pe.wait_ge(sguw_in, 16)
            for t in range(NT):
                pe.wait_ge(sgu_v, t + 1)
                b = wait_bank(pe, G_SGU, t)
                for g in range(SG):
                    mm = nc.tensor.matmul(ps[:, b, g * P:(g + 1) * P], sgu_w[:, g, :], SV[:, t, g * P:(g + 1) * P],
                                          start=True, stop=True)
                mm.then_inc(full[b], 1)
            for t in range(NT):
                pe.wait_ge(sgu_o, t + 1)
                b = wait_bank(pe, G_SGU, NT + t)
                for g in range(SG):
                    mm = turn(ps[:, b, g * P:(g + 1) * P], SU[:, t, g * P:(g + 1) * P])
                mm.then_inc(full[b], 1)

            pe.wait_ge(gdn_ready, 1)
            with pe.Fori(0, NT) as i:
                both, batches = range(2), [(d, h) for d in range(2) for h in range(2)]

                def bank(*key):
                    return wait_bank(pe, G_GDN, GDN_AT[key], i, GDN_ROUND)

                def ready(*key):
                    wait_drained(pe, G_GDN, GDN_AT[key], i, GDN_ROUND)

                def four(key, h, lhs, rhs, width=P):
                    b = bank(*key)
                    for q in range(4):
                        mm = nc.tensor.matmul(ps[:, b, q * width:(q + 1) * width], lhs(2 * q + h), rhs(2 * q + h),
                                              start=True, stop=True)
                    mm.then_inc(full[b], 1)

                for d in both:
                    tile = i if d == 0 else i * -1 + 7
                    b = bank("sums", d)
                    gt = gdec[:, bass.ds(tile, 1), 8 * d:8 * d + 8]
                    nc.tensor.matmul(ps[:, b, 0:8], masks[:, 2 * LEVELS + d, :], gt, start=True, stop=True)
                    nc.tensor.matmul(ps[:, b, 8:16], ones, gt, start=True, stop=True).then_inc(full[b], 1)
                for d, h in batches:
                    pe.wait_ge(gdn_rg, i * 2 + d + 1)
                    b = bank("rows", d, h)
                    nc.tensor.matmul(ps[:, b, :], ones, batch(Lm[d], h), start=True, stop=True
                                     ).then_inc(full[b], 1)
                for n, name in enumerate(("keys", "queries")):
                    for d in both:
                        pe.wait_ge(gdn_stage, i * 2 + d + 1)
                        b = bank(name, d)
                        for q in range(4):
                            at = 8 * n + 2 * q
                            mm = turn(ps[:, b, q * P:(q + 1) * P], KQ[d][:, at:at + 2, :])
                        mm.then_inc(full[b], 1)
                for name, source, rhs in (("kk", "keys", KTr), ("kq", "queries", QTr)):
                    for d, h in batches:
                        ready(source, d)
                        four((name, d, h), h, lambda x: half(KTr[d], x), lambda x: half(rhs[d], x))
                for d, h in batches:
                    pe.wait_ge(gdn_t0, i * 4 + 2 * d + h + 1)
                    b = bank("U", 0, d, h)
                    for q in range(4):
                        mm = turn(ps[:, b, q * P:(q + 1) * P], Tm[d][:, 2 * q + h, :])
                    mm.then_inc(full[b], 1)
                for lv in range(1, LEVELS):
                    for d, h in batches:
                        pe.wait_ge(gdn_c, i * 24 + 4 * (lv - 1) + 2 * d + h + 1)
                        ready("U", lv - 1, d, h)
                        four(("Q", lv, d, h), h, lambda x: Cm[d][:, x, :], lambda x: Um[d][:, x, :])
                    for d, h in batches:
                        ready("Q", lv, d, h)
                        cols = level_columns(Tm[d], lv, d)
                        four(("T", lv, d, h), h, lambda x: Qt[d][:, x, :], lambda x: cols[:, x, :, :], HD)
                    for d, h in batches:
                        ready("T", lv, d, h)
                        b = bank("U", lv, d, h)
                        for q in range(4):
                            mm = turn(ps[:, b, q * P:(q + 1) * P], Tm[d][:, 2 * q + h, :])
                        mm.then_inc(full[b], 1)
                for d in both:
                    pe.wait_ge(gdn_vk, i * 2 + d + 1)
                for d, h in batches:
                    ready("U", LEVELS - 1, d, h)
                    four(("u", d, h), h, lambda x: Um[d][:, x, :], lambda x: Vb[d][:, x, :], HD)
                for d, h in batches:
                    b = bank("w", d, h)
                    for q in range(4):
                        mm = nc.tensor.matmul(ps[HD * h:HD * h + HD, b, q * P:(q + 1) * P], Kbe[d][:, 2 * q + h, :],
                                              Um[d][:, 2 * q + h, :], start=True, stop=True)
                    mm.then_inc(full[b], 1)
                for d, h in batches:
                    ready("w", d, h)
                    four(("wS", d, h), h, lambda x: half(wT[d], x), lambda x: half(S[d], x), HD)
                for d, h in batches:
                    pe.wait_ge(gdn_qd, i * 2 + d + 1)
                    ready("wS", d, h)
                    b = bank("o", d, h)
                    for q in range(4):
                        x = 2 * q + h
                        nc.tensor.matmul(ps[:, b, q * HD:(q + 1) * HD], half(QdT[d], x), half(S[d], x),
                                         start=True, stop=False)
                        mm = nc.tensor.matmul(ps[:, b, q * HD:(q + 1) * HD], DTm[d][:, x, :], vnew[d][:, x, :],
                                              start=False, stop=True)
                    mm.then_inc(full[b], 1)
                for d in both:
                    b = bank("kv", d)
                    for x in range(HEADS):
                        lo = HD * (x % 2)
                        mm = nc.tensor.matmul(ps[lo:lo + HD, b, (x // 2) * HD:(x // 2 + 1) * HD], Kdec[d][:, x, :],
                                              vnew[d][:, x, :], start=True, stop=True)
                    mm.then_inc(full[b], 1)

            for t in range(NT):
                pe.wait_ge(mix_rows, t + 1)
                b = wait_bank(pe, G_MIXT, t)
                for q in range(4):
                    mm = turn(ps[:, b, q * P:(q + 1) * P], O[:, t, q * P:(q + 1) * P])
                mm.then_inc(full[b], 1)
            for t in range(NT):
                wait_drained(pe, G_MIXT, t)
            for n in range(2):
                pe.wait_ge(slab_in[n], 16 * 4)
                row_tiles(n, G_WOUT, 8 * n, src=mixT)

            rows_to_features(G_NORM2, xn)
            for k in range(8, 16):
                wait_drained(pe, G_NORM2, k)
            def split_product(out_ap, stationary, moving, kts):
                for k in range(kts):
                    for n, (a, c) in enumerate(HI_LO):
                        mm = nc.tensor.matmul(out_ap, stationary(a, k), moving(c, k), start=(k == 0 and n == 0),
                                              stop=(k == kts - 1 and n == 2))
                return mm

            def ff_round(i, last):
                start, at = at_round(G_FF, i, FF_ROUND)
                for ft in range(4):
                    if ft % 2 == 0:
                        pe.wait_ge(w_lo, i * 4 + ft // 2 + 1)
                    wv = [w.ap().rearrange("p (k n) -> p k n", n=256) for w in ws[ft // 2]]
                    for h in range(2):
                        b = wait_bank(pe, start, 2 * ft + h, **at)
                        cols = slice((ft % 2) * P, (ft % 2) * P + P)
                        split_product(ps[:, b, :], lambda a, k: wv[a][:, k, cols],
                                      lambda a, k: Hs[a][:, k, h * 512:h * 512 + 512], KT).then_inc(full[b], 1)
                for k in range(8):
                    wait_drained(pe, start, k, **at)
                for h in range(2):
                    pe.wait_ge(w_lo, i * 4 + 2 + h + 1)
                    wv = [w.ap().rearrange("p (k n) -> p k n", n=512) for w in ws[h]]
                    for t in range(NT):
                        b = wait_bank(pe, start, 8 + 8 * h + t, **at)
                        split_product(ps[:, b, :], lambda a, k: ffs[a][:, k, t * P:(t + 1) * P],
                                      lambda a, k: wv[a][:, k, :], 4).then_inc(full[b], 1)
            rounds(pe, FF_ROUNDS, ff_round)
            rows_to_features(G_NORM3, X)
            for k in range(8, 16):
                wait_drained(pe, G_NORM3, k)

            def product(start, k0, out_ap, terms, i=None, per=0):
                b = wait_bank(pe, start, k0, i, per)
                for n, (lhs, rhs) in enumerate(terms):
                    mm = nc.tensor.matmul(out_ap(b), lhs, rhs, start=(n == 0), stop=(n == len(terms) - 1))
                mm.then_inc(full[b], 1)

            pe.wait_ge(slab_in[0], 16 * 5)
            row_tiles(0, G_U, 0)
            pe.wait_ge(ssm_pre, 1)
            with pe.Fori(0, SSM_ROUNDS) as i:
                def bank(k):
                    return wait_bank(pe, G_SSM, k, i, SSM_ROUND)
                pe.wait_ge(ssm_w, i + 1)
                for n, src in enumerate((wt_re, wt_im)):
                    b = bank(n)
                    for g in range(GE):
                        mm = nc.tensor.matmul(ps[:, b, g * SSM_P:(g + 1) * SSM_P], src[:, g, :],
                                              ident[0:SSM_P, 0:SSM_P], start=True, stop=True)
                    mm.then_inc(full[b], 1)
                b = bank(2)
                for g in range(GE):
                    nc.tensor.matmul(ps[:, b, g * P:(g + 1) * P], bst[:, 0, SSM_C * g:SSM_C * g + P], v_re[:, g, 0:P],
                                     start=True, stop=False)
                    mm = nc.tensor.matmul(ps[:, b, g * P:(g + 1) * P], bst[:, 1, SSM_C * g:SSM_C * g + P], v_im[:, g, 0:P],
                                          start=False, stop=True)
                mm.then_inc(full[b], 1)
                pe.wait_ge(ssm_u, i + 1)
                b = bank(3)
                for g in range(GE):
                    mm = turn(ps[:, b, g * P:(g + 1) * P], Uq[:, g, :])
                mm.then_inc(full[b], 1)
                for n, wl in enumerate((wl_re, wl_im)):
                    wait_drained(pe, G_SSM, n, i, SSM_ROUND)
                    wait_drained(pe, G_SSM, 3, i, SSM_ROUND)
                    b = bank(4 + n)
                    for g in range(GE):
                        mm = nc.tensor.matmul(ps[0:SSM_P, b, g * P:(g + 1) * P], wl[:, g, :], uT[:, g, :],
                                              start=True, stop=True)
                    mm.then_inc(full[b], 1)
                pe.wait_ge(toep_in, i * 16 * SUB + 16 * SUB + 16)
                pe.wait_ge(ssm_state, i + 1)
                for n in range(2):
                    b = bank(6 + n)
                    for q in range(2):
                        g = 2 * n + q
                        o = ps[:, b, q * P:(q + 1) * P]
                        nc.tensor.matmul(o, uT[:, g, :], toep[:, g, :], start=True, stop=False)
                        nc.tensor.matmul(o, d_re[:, g, :], v_re[:, g, SSM_C:SSM_C + P], start=False, stop=False)
                        mm = nc.tensor.matmul(o, d_im[:, g, :], v_im[:, g, SSM_C:SSM_C + P], start=False, stop=True)
                    mm.then_inc(full[b], 1)
            for n, slot in enumerate((1, 0, 1)):
                pe.wait_ge(slab_in[slot], 16 * (5 + (n + 1) // 2))
                for ft in range(4):
                    feature_tile(slot, ft, G_HCB, 8 * n + 2 * ft)
            for j in range(NT):
                b = wait_bank(pe, G_YT, j)
                for q in range(4):
                    mm = turn(ps[:, b, q * P:(q + 1) * P], U[:, j, q * P:(q + 1) * P])
                mm.then_inc(full[b], 1)
            pe.wait_ge(slab_in[0], 16 * 7)
            for j in range(NT):
                wait_drained(pe, G_YT, j)
            for ft in range(4):
                feature_tile(0, ft, G_GLU, 2 * ft, kts=4, src=gT)
            for k in range(8):
                wait_drained(pe, G_GLU, k)
            with pe.Fori(0, MRG_ROUNDS) as i:
                pe.wait_ge(slab_in[1], i * 32 + 16 * 8)
                pe.wait_ge(slab_in[0], i * 32 + 16 * 9)
                for ft in range(2):
                    for h in range(2):
                        hc = slice(512 * h, 512 * h + 512)
                        k0 = 4 * (2 * ft + h)
                        ca = slice(ft * P, ft * P + P)
                        cb = slice(256 + ft * P, 256 + ft * P + P)
                        for n, (slot, cols, src, kts) in enumerate(((1, ca, H, 8), (1, cb, H, 8),
                                                                    (0, ca, YA, 4), (0, cb, BZ, 4))):
                            product(G_MRG, k0 + n, lambda b: ps[:, b, :],
                                    [(ring[slot][:, k, cols], src[:, k, hc]) for k in range(kts)], i, MRG_ROUND)
            for k in range(3, 16, 4):
                wait_drained(pe, last_mrg, k)
            pe.wait_ge(merged_rows, 8 + 4 * MRG_ROUNDS)
            for n, slot in enumerate((1, 0)):
                pe.wait_ge(slab_in[slot], 16 * (15 if slot == 1 else 16))
                row_tiles(slot, G_WO, 8 * n, src=M)

            def ln_rows_to_features(start):
                for j in range(NT):
                    pe.wait_ge(ln_rows, j + 1)
                    for h in range(2):
                        b = wait_bank(pe, start, 2 * j + h)
                        for q in range(4):
                            k = 4 * h + q
                            mm = turn(ps[:, b, q * P:(q + 1) * P], X[:, j, k * P:(k + 1) * P])
                        mm.then_inc(full[b], 1)
            ln_rows_to_features(G_LN1)
            for k in range(8, 16):
                wait_drained(pe, G_LN1, k)
            def f2_round(i, last):
                start, at = at_round(G_F2, i, F2_ROUND)
                for ft in range(2):
                    pe.wait_ge(v_lo, i * 3 + ft + 1)
                    wv = [w.ap().rearrange("p (k n) -> p k n", n=256) for w in ws2[ft]]
                    for h in range(2):
                        for n in range(2):
                            b = wait_bank(pe, start, 4 * ft + 2 * h + n, **at)
                            split_product(ps[:, b, :], lambda a, k: wv[a][:, k, P * n:P * n + P],
                                          lambda a, k: Hs[a][:, k, 512 * h:512 * h + 512], KT).then_inc(full[b], 1)
                pe.wait_ge(v_lo, i * 3 + 3)
                for k in range(1, 8, 2):
                    wait_drained(pe, start, k, **at)
                wv = [w.ap().rearrange("p (k n) -> p k n", n=D) for w in ws2[2]]
                for t in range(NT):
                    for h in range(2):
                        b = wait_bank(pe, start, 8 + 2 * t + h, **at)
                        split_product(ps[:, b, :], lambda a, k: hids[a][:, k, t * P:(t + 1) * P],
                                      lambda a, k: wv[a][:, k, 512 * h:512 * h + 512], 2).then_inc(full[b], 1)
            rounds(pe, F2_ROUNDS, f2_round)

        @block.scalar
        def _(act):
            steps = [0]

            def then(ins):
                ins.then_inc(act_step, 1)
                steps[0] += 1
                act.wait_ge(act_step, steps[0])

            def square_sums(src, waits, junk=None):
                junk = xn if junk is None else junk
                for j in range(NT):
                    waits(j)
                    nc.scalar.activation(junk[:, j, :], src[:, j, :], ACT.Square,
                                         accum_out=ssum[:, j:j + 1]).then_inc(norm_sums, 1)

            asked = [0]

            def root(n):
                asked[0] += 1
                act.wait_ge(root_ask, asked[0])
                nc.scalar.activation(rs_root[:, 0:n], rs_arg[:, 0:n], ACT.Sqrt).then_inc(root_done, 1)

            def copy_features(start, dst_of):
                for j in range(NT):
                    for h in range(2):
                        b = wait_full(act, start, 2 * j + h)
                        nc.scalar.copy(dst_of(j, h), ps[:, b, :].rearrange("p (k c) -> p k c", c=P)
                                       ).then_inc(drained[b], 1)

            def natural(j, h):
                return H[:, 4 * h:4 * h + 4, :].rearrange("p k (c j) -> p k c j", j=8)[:, :, :, j]

            def strided(j, h):
                return H[:, 4 * h:4 * h + 4, j * P:(j + 1) * P]

            square_sums(X, lambda j: act.wait_ge(x_in, 32))
            root(NT)
            copy_features(G_NORM1, natural)

            act.wait_ge(pads_set, 1)
            for ct in range(13):
                if ct < 12:
                    if ct >= 2:
                        act.wait_ge(conv_done, ct - 1)
                    for h in range(2):
                        b = wait_full(act, G_QKV, dense_at(ct) + h)
                        nc.scalar.copy(raw[ct % 2][:, 2 + 512 * h:514 + 512 * h], ps[:, b, :]).then_inc(drained[b], 1)
                if ct >= 1:
                    c = ct - 1
                    act.wait_ge(conv_done, c + 1)
                    nc.scalar.activation(cv[c % 2], cv[c % 2], ACT.Silu).then_inc(silu_done, 1)
                    for h in range(2):
                        b = wait_full(act, G_QKV, turn_at(c) + h)
                        nc.scalar.copy(QKV[:, 4 * h:4 * h + 4, c * P:(c + 1) * P],
                                       ps[:, b, :].rearrange("p (t c) -> p t c", c=P)).then_inc(drained[b], 1)
            root(128)
            for n, (dst, fn) in enumerate(((Z, ACT.Silu), (SU, ACT.Gelu), (SV, ACT.Gelu))):
                for t in range(NT):
                    b = wait_full(act, G_ROWS, 8 * n + t)
                    nc.scalar.activation(dst[:, t, :], ps[:, b, :], fn).then_inc(drained[b], 1)
            act.wait_ge(gate_in, 1)
            nc.scalar.activation(gbeta, graw[:, :, 0:16], ACT.Sigmoid).then_inc(gate_out, 1)
            nc.scalar.activation(alog_row, alog_row, ACT.Exp).then_inc(gate_out, 1)
            then(nc.scalar.activation(gt1, gt1, ACT.Exp))
            nc.scalar.activation(gt1, gt1, ACT.Ln, bias=1.0).then_inc(gate_out, 1)
            root(NT * SG)
            root(NT * SG)
            for t in range(NT):
                b = wait_full(act, G_SGU, NT + t)
                nc.scalar.copy(mixT[:, 4:8, :].rearrange("p k (j c) -> p k j c", j=8)[:, :, :, 16 * t:16 * t + 16],
                               ps[:, b, :].rearrange("p (k c j) -> p k j c", c=16, j=8)).then_inc(drained[b], 1)

            with act.Fori(0, NT) as i:
                both, batches = range(2), [(d, h) for d in range(2) for h in range(2)]

                def arrived(*key):
                    return wait_full(act, G_GDN, GDN_AT[key], i, GDN_ROUND)

                def drain(key, dst):
                    b = arrived(*key)
                    nc.scalar.copy(dst, ps[:, b, 0:dst.shape[1] * dst.shape[2]]
                                   .rearrange("p (k c) -> p k c", c=dst.shape[2])).then_inc(drained[b], 1)

                for d in both:
                    tile = i if d == 0 else i * -1 + 7
                    act.wait_ge(gdn_go, i * 2 + d + 1)
                    row = QKV[:, bass.ds(tile, 1), :]
                    nc.scalar.copy(KQ[d][:, 0:HEADS, :], row[:, :, GW:2 * GW].rearrange("p t (h e) -> p (t h) e", e=HD))
                    nc.scalar.copy(KQ[d][:, HEADS:, :], row[:, :, 0:GW].rearrange("p t (h e) -> p (t h) e", e=HD)
                                   ).then_inc(gdn_stage, 1)
                for d in both:
                    act.wait_ge(gdn_exin, i * 2 + d + 1)
                    nc.scalar.activation(ex[d], exin[d], ACT.Exp).then_inc(gdn_ex, 1)
                for d, h in batches:
                    b = arrived("rows", d, h)
                    lo = HD * h
                    nc.scalar.activation(QdT[d][lo:lo + HD], ps[lo:lo + HD, b, :].rearrange("p (k c) -> p k c", c=P),
                                         ACT.Exp).then_inc(gdn_rexp, 1)
                for name, dst in (("keys", KTr), ("queries", QTr)):
                    for d in both:
                        drain((name, d), dst[d])
                for d, h in batches:
                    act.wait_ge(gdn_din, i * 4 + 2 * d + h + 1)
                    nc.scalar.activation(batch(Cm[d], h), batch(Cm[d], h), ACT.Exp)
                    nc.scalar.activation(batch(DTm[d], h), batch(DTm[d], h), ACT.Exp).then_inc(gdn_dexp, 1)
                for d, h in batches:
                    drain(("U", 0, d, h), batch(Um[d], h))
                for lv in range(1, LEVELS):
                    for name, dst in (("Q", Qt), ("U", Um)):
                        for d, h in batches:
                            drain((name, lv, d, h), batch(dst[d], h))
                for d, h in batches:
                    drain(("u", d, h), batch(un[d], h))
                for d, h in batches:
                    b = arrived("w", d, h)
                    lo = HD * h
                    nc.scalar.copy(wT[d][lo:lo + HD], ps[lo:lo + HD, b, :].rearrange("p (k c) -> p k c", c=P)
                                   ).then_inc(drained[b], 1)

            root(NT * HEADS)
            for t in range(NT):
                b = wait_full(act, G_MIXT, t)
                nc.scalar.copy(mixT[:, 0:4, :].rearrange("p k (j c) -> p k j c", j=8)[:, :, :, 16 * t:16 * t + 16],
                               ps[:, b, :].rearrange("p (k c j) -> p k j c", c=16, j=8)).then_inc(drained[b], 1)

            def after_wout(j):
                wait_drained(act, G_WOUT, 8 + j)
            square_sums(X, after_wout)
            root(NT)
            def round_features(start, count):
                for j in range(NT):
                    for h in range(2):
                        b = wait_full(act, start, 2 * j + h)
                        nc.scalar.copy(Hs[0][:, 4 * h:4 * h + 4, j * P:(j + 1) * P],
                                       ps[:, b, :].rearrange("p (k c) -> p k c", c=P)).then_inc(feat_hi, 1)
            def round_slab(q, i):
                act.wait_ge(raw_in[q % 2], i * 32 + 16 * (q // 2 + 1))
                ff_slab_done(act, q - 2, i)
                nc.scalar.copy(ws[q % 2][0].ap(), wraw[q % 2]).then_inc(w_hi, 1)
            round_features(G_NORM2, 0)
            round_slab(0, 0)
            def ff_round(i, last):
                start, at = at_round(G_FF, i, FF_ROUND)
                for k in range(8):
                    b = wait_full(act, start, k, **at)
                    if isinstance(i, int) or k >= 2:
                        wait_drained(act, start, k - 2, **at)
                    else:
                        wait_drained(act, start - FF_ROUND, 6 + k, **at)
                    nc.scalar.activation(fft[k % 2], ps[:, b, :], ACT.Relu).then_inc(relu_done, 1)
                    act.wait_ge(relu_done, i * 8 + k + 1)
                    nc.scalar.activation(fft[k % 2], fft[k % 2], ACT.Square).then_inc(square_done, 1)
                    if k in (0, 4):
                        round_slab(1 + k // 4, i)
                for h in range(2):
                    wait_full(act, start, 8 + 8 * h, **at)
                    if h == 0:
                        round_slab(3, i)
                    elif not last:
                        round_slab(0, i + 1)
            rounds(act, FF_ROUNDS, ff_round)
            last_ff = G_FF + (FF_ROUNDS - 1) * FF_ROUND

            def after_ff(j):
                for h in range(2):
                    wait_drained(act, last_ff, 8 + 8 * h + j)
            square_sums(X, after_ff, junk=area(AT_H, NT, D))
            root(NT)
            copy_features(G_NORM3, strided)

            act.wait_ge(ssm_angle, 1)
            nc.scalar.activation(s_sin, s_th, ACT.Sin)
            nc.scalar.activation(s_half, s_th, ACT.Sin, scale=0.5).then_inc(ssm_sin, 1)
            with act.Fori(0, SSM_ROUNDS) as i:
                def drain(k, dst, parts, width):
                    b = wait_full(act, G_SSM, k, i, SSM_ROUND)
                    nc.scalar.copy(dst, ps[0:parts, b, 0:GE * width].rearrange("p (k c) -> p k c", c=width)
                                   ).then_inc(drained[b], 1)
                act.wait_ge(ssm_angle, i + 2)
                nc.scalar.activation(e_im, tt4[0], ACT.Sin)
                nc.scalar.activation(e_re, tt4[0], ACT.Sin, scale=0.5).then_inc(ssm_trig, 1)
                drain(0, wl_re, P, SSM_P)
                drain(1, wl_im, P, SSM_P)
                act.wait_ge(toep_in, i * 16 * SUB + 16)
                drain(2, kall, SSM_C, P)
                drain(3, uT, P, P)
            act.wait_ge(b2_in, 48)
            for k in range(8):
                b = wait_full(act, G_HCB, k)
                nc.scalar.activation(BZ[:, k // 2, 512 * (k % 2):512 * (k % 2) + 512], ps[:, b, :], ACT.Identity,
                                     bias=bias_col[:, k // 2:k // 2 + 1]).then_inc(drained[b], 1)
            for j in range(NT):
                b = wait_full(act, G_YT, j)
                nc.scalar.activation(gT[:, :, j * P:(j + 1) * P], ps[:, b, :].rearrange("p (k c) -> p k c", c=P),
                                     ACT.Gelu_apprx_tanh).then_inc(drained[b], 1)
            for k in range(8):
                b = wait_full(act, G_GLU, k)
                if k >= 4:
                    wait_drained(act, G_GLU, k - 4)
                nc.scalar.activation(sig[k % 4], ps[:, b, :], ACT.Sigmoid, bias=glu_col[:, k // 2:k // 2 + 1]
                                     ).then_inc(sig_done, 1)
            with act.Fori(0, MRG_ROUNDS) as i:
                wait_drained(act, G_MRG - MRG_ROUND, 13, i, MRG_ROUND)
                nc.scalar.copy(bias_now[:, 0, :], bias_col[:, bass.ds(i * 2 + 12, 2)])
                nc.scalar.copy(bias_now[:, 1, :], bias_col[:, bass.ds(i * 2 + 20, 2)]).then_inc(bias_set, 1)
                act.wait_ge(bias_set, i + 1)
                for ft in range(2):
                    for h in range(2):
                        k0 = 4 * (2 * ft + h)
                        r = 2 * ft + h
                        act.wait_ge(merged_rows, i * 4 + r + 7)
                        for n in range(2):
                            b = wait_full(act, G_MRG, k0 + n, i, MRG_ROUND)
                            nc.scalar.activation(sig[2 * (r % 2) + n], ps[:, b, :], ACT.Sigmoid,
                                                 bias=bias_now[:, n, ft:ft + 1]
                                                 ).then_inc(drained[b], 1)

            def layer_sums(waits, count):
                junk = area(AT_H, NT, D)
                for j in range(NT):
                    waits(j)
                    nc.scalar.activation(junk[:, j, :], X[:, j, :], ACT.Copy, accum_out=ssum[:, j:j + 1]
                                         ).then_inc(ln_sum, 1)
                act.wait_ge(ln_mean, count)
                act.wait_ge(ln_sum, count * NT)
                for j in range(NT):
                    nc.scalar.activation(junk[:, j, :], X[:, j, :], ACT.Square, bias=mean[:, j:j + 1],
                                         accum_out=rstd[:, j:j + 1]).then_inc(ln_sq, 1)
                root(NT)
                act.wait_ge(ln_sq, count * NT)
                act.wait_ge(ln_mean2, count)
                for j in range(NT):
                    nc.scalar.activation(xn[:, j, :], X[:, j, :], ACT.Identity, bias=ssum[:, j:j + 1],
                                         scale=rs_y[:, j:j + 1]).then_inc(ln_scaled, 1)

            def after_wo(j):
                if j == 0:
                    for t in range(NT):
                        wait_drained(act, G_WO, 8 + t)
            layer_sums(after_wo, 1)
            round_features(G_LN1, 1)

            def round_slab2(q, i, waited=True):
                act.wait_ge(raw2_in[q], i * (32 if q < 2 else 16) + (32 if q < 2 else 16))
                nc.scalar.copy(ws2[q][0].ap(), wraw2[q]).then_inc(v_hi, 1)
            for q in range(3):
                round_slab2(q, 0)
            def f2_round(i, last):
                start, at = at_round(G_F2, i, F2_ROUND)
                for q in range(4):
                    b = wait_full(act, start, 2 * q, **at)
                    if q >= 2:
                        wait_drained(act, start, 2 * q - 3, **at)
                    else:
                        wait_drained(act, start - F2_ROUND, 5 + 2 * q, **at)
                    nc.scalar.activation(hg[q % 2], ps[:, b, :], ACT.Silu).then_inc(drained[b], 1)
                    act.wait_ge(hid_f, i * 4 + q + 1)
                    nc.scalar.copy(hids[0][:, q // 2, 512 * (q % 2):512 * (q % 2) + 512], hg[q % 2]).then_inc(hid_hi, 1)
                if not last:
                    for q in range(3):
                        wait_full(act, start, (3, 7, 23)[q], **at)
                        if q == 2:
                            pass
                        round_slab2(q, i + 1)
            rounds(act, F2_ROUNDS, f2_round)

            def after_f2(j):
                for h in range(2):
                    wait_drained(act, last_f2, 8 + 2 * j + h)
            layer_sums(after_f2, 2)

        @block.vector
        def _(dve):
            V = nc.vector
            steps = [0]

            def then(ins):
                ins.then_inc(dve_step, 1)
                steps[0] += 1
                dve.wait_ge(dve_step, steps[0])

            asked = [0]

            def inverse_root(n, factor=1.0):
                asked[0] += 1
                arg, y, t = rs_arg[:, 0:n], rs_y[:, 0:n], rs_t[:, 0:n]
                dve.wait_ge(root_ask, asked[0])
                dve.wait_ge(root_done, asked[0])
                then(V.reciprocal(y, rs_root[:, 0:n]))
                then(V.tensor_tensor(t, y, y, ALU.mult))
                then(V.tensor_tensor(t, t, arg, ALU.mult))
                then(V.tensor_scalar(t, t, -0.5, 1.5, ALU.mult, ALU.add))
                then(V.tensor_tensor(y, y, t, ALU.mult))

            def rms_rows(src, dst, count):
                dve.wait_ge(gain_in, 16 * count)
                dve.wait_ge(norm_sums, count * NT)
                V.tensor_scalar(rs_arg[:, 0:NT], ssum, 1.0 / D, EPS, ALU.mult, ALU.add).then_inc(root_ask, 1)
                inverse_root(NT)
                for j in range(NT):
                    V.scalar_tensor_tensor(dst[:, j, :], src[:, j, :], rs_y[:, j:j + 1], gain,
                                           ALU.mult, ALU.mult).then_inc(norm_rows, 1)

            rms_rows(X, xn, 1)

            for b in range(2):
                V.memset(raw[b][:, 0:2], 0.0)
                pad = V.memset(raw[b][:, 1026:1028], 0.0)
            pad.then_inc(pads_set, 1)
            dve.wait_ge(pads_set, 1)
            dve.wait_ge(consts_in, 16 * 10)
            for ct in range(12):
                for h in range(2):
                    wait_drained(dve, G_QKV, dense_at(ct) + h)
                if ct >= 2:
                    wait_full(dve, G_QKV, turn_at(ct - 2) + 1)
                r, c = raw[ct % 2], cv[ct % 2]
                then(V.tensor_scalar(c, r[:, 0:SEQ], conv_taps[:, ct, 0:1], None, ALU.mult))
                for k in range(1, CONV_K):
                    ins = V.scalar_tensor_tensor(c, r[:, k:k + SEQ], conv_taps[:, ct, k:k + 1], c, ALU.mult, ALU.add)
                    if k < CONV_K - 1:
                        then(ins)
                ins.then_inc(conv_done, 1)

            s3 = sq.rearrange("p (h e) -> p h e", e=HD)
            for ct in range(8):
                for h in range(2):
                    wait_drained(dve, G_QKV, turn_at(ct) + h)
            wait_full(dve, G_QKV, 47)
            for t in range(NT):
                qk = QKV[:, t, 0:2 * GW].rearrange("p (h e) -> p h e", e=HD)
                then(V.tensor_tensor(s3, qk, qk, ALU.mult))
                then(V.tensor_reduce(vst[:, 0:16], s3, AX_X, ALU.add))
                ins = V.tensor_scalar(rs_arg[:, 16 * t:16 * t + 16], vst[:, 0:16], EPS, None, ALU.add)
            ins.then_inc(root_ask, 1)
            inverse_root(128)
            y3 = rs_y.rearrange("p (t h) -> p t h", h=16)
            then(V.tensor_scalar(y3[:, :, 0:8], y3[:, :, 0:8], HD ** -0.5, None, ALU.mult))
            for t in range(NT):
                qk = QKV[:, t, 0:2 * GW].rearrange("p (h e) -> p h e", e=HD)
                V.tensor_tensor(qk, qk, y3[:, t, :].unsqueeze(2).broadcast_to([P, 16, HD]), ALU.mult)

            b = wait_full(dve, G_ROWS, 24)
            gv = ps[:, b, 0:256].rearrange("p (t n) -> p t n", n=32)
            then(V.tensor_copy(graw, gv))
            then(V.tensor_tensor(gt2, graw[:, :, 16:32], dt_row.unsqueeze(1).broadcast_to([P, NT, 16]), ALU.add))
            then(V.tensor_scalar(gt1, gt2, -1.0, None, ALU.mult))
            then(V.tensor_tensor(gt1, gt1, gt2, ALU.min))
            V.tensor_copy(graw[:, 0:1, 0:1], graw[:, 0:1, 0:1]).then_inc(gate_in, 1)
            dve.wait_ge(gate_out, 3)
            then(V.scalar_tensor_tensor(gt2, gt2, 0.0, gt1, ALU.max, ALU.add))
            then(V.tensor_tensor(gt2, gt2, alog_row.unsqueeze(1).broadcast_to([P, NT, 16]), ALU.mult))
            then(V.tensor_scalar(gdec, gt2, -1.0, None, ALU.mult))
            V.tensor_copy(graw[:, 0:1, 0:1], graw[:, 0:1, 0:1]).then_inc(drained[b], 1)

            def heads_of(rows, width):
                return rows.rearrange("p (g c) -> p g c", c=width)

            def group_sums(t, rows, width, count, scratch):
                r3 = heads_of(rows, width)
                then(V.tensor_tensor(scratch, r3, r3, ALU.mult))
                then(V.tensor_reduce(vst[:, 0:count], scratch, AX_X, ALU.add))
                return V.tensor_scalar(rs_arg[:, count * t:count * t + count], vst[:, 0:count], 1.0 / width, EPS,
                                       ALU.mult, ALU.add)

            def group_scale(t, rows, width, count):
                return V.tensor_tensor(heads_of(rows, width), heads_of(rows, width),
                                       rs_y[:, count * t:count * t + count].unsqueeze(2)
                                       .broadcast_to([P, count, width]), ALU.mult)

            sq4 = sq[:, 0:512].rearrange("p (g c) -> p g c", c=P)
            for t in range(NT):
                wait_drained(dve, G_ROWS, 16 + t)
                ins = group_sums(t, SV[:, t, :], P, SG, sq4)
            ins.then_inc(root_ask, 1)
            inverse_root(NT * SG)
            for t in range(NT):
                then(group_scale(t, SV[:, t, :], P, SG))
                V.tensor_tensor(heads_of(SV[:, t, :], P), heads_of(SV[:, t, :], P), sgu_vg, ALU.mult
                                ).then_inc(sgu_v, 1)
            for t in range(NT):
                b = wait_full(dve, G_SGU, t)
                wait_drained(dve, G_ROWS, 8 + t)
                V.tensor_tensor(sq4, heads_of(ps[:, b, :], P), sgu_bt.unsqueeze(2).broadcast_to([P, SG, P]), ALU.add
                                ).then_inc(drained[b], 1)
                wait_drained(dve, G_SGU, t)
                u4 = heads_of(SU[:, t, :], P)
                then(V.tensor_tensor(u4, sq4, u4, ALU.mult))
                ins = group_sums(t, SU[:, t, :], P, SG, sq4)
            ins.then_inc(root_ask, 1)
            inverse_root(NT * SG)
            for t in range(NT):
                then(group_scale(t, SU[:, t, :], P, SG))
                V.tensor_tensor(heads_of(SU[:, t, :], P), heads_of(SU[:, t, :], P), sgu_og, ALU.mult
                                ).then_inc(sgu_o, 1)

            V.memset(SV.rearrange("p t c -> p (t c)"), 0.0)
            wait_full(dve, G_SGU, NT + 7)
            V.memset(S[0].rearrange("p a b -> p (a b)"), 0.0)
            ins = V.memset(S[1].rearrange("p a b -> p (a b)"), 0.0)
            ins.then_inc(gdn_ready, 1)
            dve.wait_ge(gdn_ready, 1)

            with dve.Fori(0, NT) as i:
                own = [0]
                both, batches = range(2), [(d, h) for d in range(2) for h in range(2)]
                tris = [masks[:, 2 * LEVELS + d, :] for d in both]
                tiles = [i, i * -1 + 7]

                def chain(ins):
                    ins.then_inc(gdn_step, 1)
                    own[0] += 1
                    dve.wait_ge(gdn_step, i * GDN_OWN + own[0])

                def arrived(*key):
                    return wait_full(dve, G_GDN, GDN_AT[key], i, GDN_ROUND)

                def ready(*key):
                    wait_drained(dve, G_GDN, GDN_AT[key], i, GDN_ROUND)

                def view(b, c=P, n=4):
                    return ps[:, b, 0:n * c].rearrange("p (k c) -> p k c", c=c)

                def per_head(col, n=HEADS, width=HD):
                    return col.unsqueeze(2).broadcast_to([P, n, width])

                def level_mask(d, lv):
                    return masks[:, LEVELS * d + lv, :].unsqueeze(1).broadcast_to([P, 4, P])

                def rows_of(d, c0):
                    return QKV[:, bass.ds(tiles[d], 1), c0:c0 + GW].rearrange("p t (h e) -> p (t h) e", e=HD)

                def gates_of(x, d):
                    return x[:, bass.ds(tiles[d], 1), 8 * d:8 * d + 8].rearrange("p t h -> p (t h)")

                for d in both:
                    V.tensor_tensor(Lm[d], per_head(gates_of(gdec, d), width=P),
                                    tris[d].unsqueeze(1).broadcast_to([P, HEADS, P]), ALU.mult).then_inc(gdn_rg, 1)
                    V.tensor_scalar(bege[d], gates_of(gbeta, d), 1.0, None, ALU.mult).then_inc(gdn_go, 1)
                for d in both:
                    b = arrived("sums", d)
                    V.tensor_copy(exin[d][:, 0:2, :], ps[:, b, 0:16].rearrange("p (a h) -> p a h", h=8)
                                  ).then_inc(drained[b], 1)
                    ready("sums", d)
                    V.tensor_tensor(exin[d][:, 2, :], exin[d][:, 1, :], exin[d][:, 0, :], ALU.subtract
                                    ).then_inc(gdn_exin, 1)
                dve.wait_ge(gdn_go, i * 2 + 2)
                for d, h in batches:
                    dve.wait_ge(gdn_rexp, i * 4 + 2 * d + h + 1)
                    b = arrived("rows", d, h)
                    hs = slice(h, HEADS, 2)
                    V.tensor_tensor(Rm[d][:, hs, :], view(b), per_head(exin[d][:, 0, hs], 4, P), ALU.subtract
                                    ).then_inc(drained[b], 1)
                    ready("rows", d, h)
                    V.tensor_scalar(Cm[d][:, hs, :], Rm[d][:, hs, :], -1.0, 0.0, ALU.mult, ALU.min)
                    V.tensor_scalar(DTm[d][:, hs, :], Rm[d][:, hs, :], 0.0, None, ALU.min).then_inc(gdn_din, 1)
                for d, h in batches:
                    hs = slice(h, HEADS, 2)
                    b = arrived("kk", d, h)
                    dve.wait_ge(gdn_dexp, i * 4 + 2 * d + h + 1)
                    V.tensor_tensor(Lm[d][:, hs, :], view(b), Cm[d][:, hs, :], ALU.mult).then_inc(drained[b], 1)
                    ready("kk", d, h)
                    chain(V.tensor_tensor(Lm[d][:, hs, :], Lm[d][:, hs, :], per_head(bege[d][:, hs], 4, P), ALU.mult))
                    chain(V.tensor_tensor(Tm[d][:, hs, :], Lm[d][:, hs, :], level_mask(d, 0), ALU.mult))
                    V.tensor_tensor(Tm[d][:, hs, :], ident.unsqueeze(1).broadcast_to([P, 4, P]), Tm[d][:, hs, :],
                                    ALU.subtract).then_inc(gdn_t0, 1)

                def cut(lv, d, h):
                    hs = slice(h, HEADS, 2)
                    V.tensor_tensor(Cm[d][:, hs, :], Lm[d][:, hs, :], level_mask(d, lv), ALU.mult).then_inc(gdn_c, 1)

                for d, h in batches:
                    cut(1, d, h)
                for d, h in batches:
                    hs = slice(h, HEADS, 2)
                    b = arrived("kq", d, h)
                    V.tensor_tensor(DTm[d][:, hs, :], view(b), DTm[d][:, hs, :], ALU.mult).then_inc(drained[b], 1)

                def between(lv):
                    if lv == 1:
                        for d in both:
                            V.tensor_tensor(Vb[d], rows_of(d, 2 * GW), per_head(bege[d]), ALU.mult)
                            dve.wait_ge(gdn_ex, i * 2 + d + 1)
                            chain(V.tensor_tensor(exin[d][:, 0, :], ex[d][:, 0, :], bege[d], ALU.mult))
                    if lv == 2:
                        for d in both:
                            V.tensor_tensor(Kbe[d], rows_of(d, GW), per_head(exin[d][:, 0, :]), ALU.mult)
                            V.tensor_tensor(Kdec[d], rows_of(d, GW), per_head(ex[d][:, 2, :]), ALU.mult
                                            ).then_inc(gdn_vk, 1)
                    if lv == 3:
                        for d in both:
                            ready("kq", d, 1)
                            ready("kq", d, 0)
                            V.tensor_tensor(QdT[d], QdT[d], QTr[d], ALU.mult)
                            V.tensor_tensor(DTm[d], DTm[d], tris[d].unsqueeze(1).broadcast_to([P, HEADS, P]),
                                            ALU.mult).then_inc(gdn_qd, 1)
                    if lv == 4:
                        for d in both:
                            for x in range(2):
                                lo = HD * x
                                ins = V.tensor_copy(egl[d][lo:lo + HD, :], ex[d][lo:lo + HD, 1, :]
                                                    .rearrange("p (m a) -> p m a", a=2)[:, :, x])
                            chain(ins)

                for d in both:
                    ready("queries", d)
                for lv in range(1, LEVELS):
                    for d, h in batches:
                        hs = slice(h, HEADS, 2)
                        b = arrived("T", lv, d, h)
                        cols = level_columns(Tm[d], lv, d)[:, hs, :, :]
                        V.tensor_tensor(cols, cols, ps[:, b, 0:4 * HD].rearrange("p (k n b) -> p k n b", k=4, b=1 << lv),
                                        ALU.subtract).then_inc(drained[b], 1)
                        if lv < LEVELS - 1:
                            cut(lv + 1, d, h)
                    between(lv)
                for d, h in batches:
                    ready("u", d, h)
                    b = arrived("wS", d, h)
                    V.tensor_tensor(batch(vnew[d], h), batch(un[d], h), view(b, HD), ALU.subtract
                                    ).then_inc(drained[b], 1)
                for d in both:
                    for h in range(2):
                        b = arrived("o", d, h)
                        orow = batch(O[:, bass.ds(tiles[d], 1), :].rearrange("p t (h e) -> p (t h) e", e=HD), h)
                        V.tensor_tensor(orow, orow, view(b, HD), ALU.add).then_inc(drained[b], 1)
                    chain(V.tensor_tensor(S[d], S[d], per_head(egl[d], 4), ALU.mult))
                for d in both:
                    b = arrived("kv", d)
                    V.tensor_tensor(S[d], S[d], view(b, HD), ALU.add).then_inc(drained[b], 1)
                assert own[0] == GDN_OWN, own[0]

            for d in range(2):
                for key in (("o", d, 0), ("o", d, 1), ("kv", d)):
                    wait_drained(dve, G_GDN + (NT - 1) * GDN_ROUND, GDN_AT[key])
            V.memset(vst, 0.0).then_inc(gdn_over, 1)
            dve.wait_ge(gdn_over, 1)
            sq8 = heads_of(sq[:, 0:512], HD)
            for t in range(NT):
                ins = group_sums(t, O[:, t, :], HD, HEADS, sq8)
            ins.then_inc(root_ask, 1)
            inverse_root(NT * HEADS)
            for t in range(NT):
                o3 = heads_of(O[:, t, :], HD)
                then(group_scale(t, O[:, t, :], HD, HEADS))
                then(V.tensor_tensor(o3, o3, gdn_gain.unsqueeze(1).broadcast_to([P, HEADS, HD]), ALU.mult))
                V.tensor_tensor(O[:, t, :], O[:, t, :], Z[:, t, :], ALU.mult).then_inc(mix_rows, 1)

            dve.wait_ge(xin_in, 32)
            for h in range(2):
                for t in range(NT):
                    b = wait_full(dve, G_WOUT, 8 * h + t)
                    V.tensor_tensor(X[:, t, 512 * h:512 * h + 512], xin[:, t, 512 * h:512 * h + 512], ps[:, b, :],
                                    ALU.add).then_inc(drained[b], 1)
            for t in range(NT):
                for h in range(2):
                    wait_drained(dve, G_WOUT, 8 * h + t)
            rms_rows(X, xn, 2)

            def rest_features(start, count):
                for j in range(NT):
                    for h in range(2):
                        dve.wait_ge(feat_hi, 16 * count + 2 * j + h + 1)
                        b = wait_full(dve, start, 2 * j + h)
                        part = (slice(None), slice(4 * h, 4 * h + 4), slice(j * P, (j + 1) * P))
                        V.tensor_tensor(Hs[1][part], ps[:, b, :].rearrange("p (k c) -> p k c", c=P),
                                        Hs[0][part].bitcast(F32), ALU.subtract).then_inc(drained[b], 1)

            def rest_slab(q, i):
                dve.wait_ge(w_hi, i * 4 + q + 1)
                V.tensor_tensor(ws[q % 2][1].ap(), wraw[q % 2], ws[q % 2][0].ap().bitcast(F32), ALU.subtract
                                ).then_inc(w_lo, 1)
            rest_features(G_NORM2, 0)
            rest_slab(0, 0)
            def ff_round(i, last):
                start, at = at_round(G_FF, i, FF_ROUND)
                for k in range(8):
                    dve.wait_ge(square_done, i * 8 + k + 1)
                    part = (slice(None), k // 2, slice((k % 2) * 512, (k % 2) * 512 + 512))
                    V.tensor_copy(ffs[0][part], fft[k % 2]).then_inc(ff_hi, 1)
                    dve.wait_ge(ff_hi, i * 8 + k + 1)
                    V.tensor_tensor(ffs[1][part], fft[k % 2], ffs[0][part].bitcast(F32), ALU.subtract
                                    ).then_inc(drained[where(start, k)[0]], 1)
                    if k in (0, 4):
                        rest_slab(1 + k // 4, i)
                for h in range(2):
                    for t in range(NT):
                        b = wait_full(dve, start, 8 + 8 * h + t, **at)
                        xs = X[:, t, 512 * h:512 * h + 512]
                        V.tensor_tensor(xs, xs, ps[:, b, :], ALU.add).then_inc(drained[b], 1)
                        if t == 0 and h == 0:
                            rest_slab(3, i)
                        elif t == 0 and not last:
                            rest_slab(0, i + 1)
            rounds(dve, FF_ROUNDS, ff_round)
            for k in range(8, 24):
                wait_drained(dve, G_FF + (FF_ROUNDS - 1) * FF_ROUND, k)
            rms_rows(X, X, 3)

            dve.wait_ge(ssm_in, 16 * 10)
            mul, add, sub = ALU.mult, ALU.add, ALU.subtract

            def tt2(out, a, b, op):
                then(V.tensor_tensor(out, a, b, op))

            def ts2(out, a, x, op0, y=None, op1=None):
                if op1 is None:
                    then(V.tensor_scalar(out, a, x, None, op0))
                else:
                    then(V.tensor_scalar(out, a, x, y, op0, op1))

            def exp_to(out, x):
                ts2(s_k, x, 1.0 / float(np.log(2.0)), mul, -1e6, ALU.max)
                ts2(s_k, s_k, ROUNDER, add)
                ts2(s_k, s_k, ROUNDER, sub)
                then(V.scalar_tensor_tensor(s_r, s_k, -LN2_HI, x, mul, add))
                then(V.scalar_tensor_tensor(s_r, s_k, -LN2_LO, s_r, mul, add))
                ts2(s_r, s_r, -1.0, ALU.max, 1.0, ALU.min)
                ts2(s_e, s_r, 1.0 / 5040, mul, 1.0 / 720, add)
                for c in (1.0 / 120, 1.0 / 24, 1.0 / 6, 0.5, 1.0, 1.0):
                    tt2(s_e, s_e, s_r, mul)
                    ts2(s_e, s_e, c, add)
                ts2(s_k, s_k, -127.0, ALU.max, 128.0, ALU.min)
                ts2(s_k, s_k, 127.0, add, 8388608.0, mul)
                then(V.tensor_copy(s_t1.bitcast(mybir.dt.int32), s_k))
                tt2(out, s_e, s_t1, mul)

            def reduce_angle(out, x, k, clamp_out=None):
                ts2(k, x, 1.0 / TWO_PI, mul, ROUNDER, add)
                ts2(k, k, ROUNDER, sub)
                then(V.scalar_tensor_tensor(out, k, -TWO_PI_HI, x, mul, add))
                then(V.scalar_tensor_tensor(out, k, -TWO_PI_LO, out, mul, add))
                return V.tensor_scalar(out, out, PI_IN, -PI_IN, ALU.min, ALU.max)

            exp_to(s_dt, s_x)
            tt2(s_x, s_lr, s_dt, mul)
            exp_to(s_mag, s_x)
            ts2(s_x, s_x, 8.0, mul)
            exp_to(s_r8, s_x)
            tt2(s_x, s_li, s_dt, mul)
            reduce_angle(s_th, s_x, s_k).then_inc(ssm_angle, 1)
            dve.wait_ge(ssm_sin, 1)
            tt2(s_cos, s_half, s_half, mul)
            ts2(s_cos, s_cos, -2.0, mul, 1.0, add)
            V.memset(pw_re[:, 0, :], 1.0)
            V.memset(pw_im[:, 0, :], 0.0)
            tt2(pw_re[:, 1, :], s_mag, s_cos, mul)
            tt2(pw_im[:, 1, :], s_mag, s_sin, mul)

            def power_rows(first, count, by):
                lo, hi = slice(1, 1 + count), slice(first, first + count)
                xr = pw_re[:, by, :].unsqueeze(1).broadcast_to([SSM_P, count, SSM_G])
                xi = pw_im[:, by, :].unsqueeze(1).broadcast_to([SSM_P, count, SSM_G])
                n = count * SSM_G
                t0, t1 = (tt[q][:, 0:n].rearrange("p (a b) -> p a b", b=SSM_G) for q in range(2))
                tt2(t0, pw_re[:, lo, :], xr, mul)
                tt2(t1, pw_im[:, lo, :], xi, mul)
                tt2(pw_re[:, hi, :], t0, t1, sub)
                tt2(t0, pw_re[:, lo, :], xi, mul)
                tt2(t1, pw_im[:, lo, :], xr, mul)
                tt2(pw_im[:, hi, :], t0, t1, add)

            power_rows(2, 1, 1)
            power_rows(3, 2, 2)
            power_rows(5, 4, 4)
            for j in range(SUB):
                then(V.tensor_copy(rv_re[:, j, :], pw_re[:, SUB - 1 - j, :]))
                then(V.tensor_copy(rv_im[:, j, :], pw_im[:, SUB - 1 - j, :]))
            ts2(s_x, s_th, 8.0, mul)
            then(reduce_angle(s_phi, s_x, s_k))
            tt2(s_den, s_lr, s_lr, mul)
            tt2(s_t1, s_li, s_li, mul)
            tt2(s_den, s_den, s_t1, add)
            then(V.reciprocal(s_den, s_den))
            ts2(s_nr, pw_re[:, 1, :], 1.0, sub)
            tt2(s_t1, s_nr, s_lr, mul)
            tt2(s_t2, pw_im[:, 1, :], s_li, mul)
            tt2(s_fr, s_t1, s_t2, add)
            tt2(s_fr, s_fr, s_den, mul)
            tt2(s_t1, pw_im[:, 1, :], s_lr, mul)
            tt2(s_t2, s_nr, s_li, mul)
            tt2(s_fi, s_t1, s_t2, sub)
            tt2(s_fi, s_fi, s_den, mul)
            t0, t1 = (tt[q][:, 0:512].rearrange("p (a b) -> p a b", b=SSM_C) for q in range(2))
            fr = s_fr.unsqueeze(2).broadcast_to([SSM_P, SSM_G, SSM_C])
            fi = s_fi.unsqueeze(2).broadcast_to([SSM_P, SSM_G, SSM_C])
            tt2(t0, b_re, fr, mul)
            tt2(t1, b_im, fi, mul)
            tt2(bb_re, t0, t1, sub)
            tt2(t0, b_im, fr, mul)
            tt2(t1, b_re, fi, mul)
            tt2(bb_im, t0, t1, add)
            V.memset(bst.rearrange("p a b -> p (a b)"), 0.0)
            V.memset(toep.rearrange("p a b -> p (a b)"), 0.0).then_inc(toep_in, 16)
            then(V.memset(not_first.rearrange("p a b -> p (a b)"), 1.0))
            then(V.memset(not_first[:, :, 0], 0.0))
            then(V.memset(d_re[:, :, 0], 0.0))
            then(V.memset(d_im[:, :, 0], 0.0))
            for j in range(NT):
                b = wait_full(dve, G_U, j)
                V.tensor_tensor(U[:, j, :], ps[:, b, :], u_row, add).then_inc(drained[b], 1)
            for j in range(NT):
                wait_drained(dve, G_U, j)
            V.memset(s_t1, 0.0).then_inc(ssm_pre, 1)
            dve.wait_ge(ssm_pre, 1)

            with dve.Fori(0, SSM_ROUNDS) as i:
                own = [0]

                def chain(ins):
                    ins.then_inc(ssm_own, 1)
                    own[0] += 1
                    dve.wait_ge(ssm_own, i * SSM_OWN + own[0])

                def complex_product(out_re, out_im, a, b, t, conj=False, last_im=None):
                    (ar, ai), (br, bi) = a, b
                    chain(V.tensor_tensor(t[0], ar, br, mul))
                    chain(V.tensor_tensor(t[1], ai, bi, mul))
                    chain(V.tensor_tensor(out_re, t[0], t[1], add if conj else sub))
                    chain(V.tensor_tensor(t[0], ar, bi, mul))
                    chain(V.tensor_tensor(t[1], ai, br, mul))
                    return V.tensor_tensor(out_im, t[0], t[1], sub if conj else add)

                gs = bass.ds(i * GE, GE)

                def groups(x):
                    return x[:, :, gs].rearrange("p j g -> p g j")

                def lags(x, n):
                    return groups(x).unsqueeze(3).broadcast_to([SSM_P, GE, n, SSM_C])

                def chans(x, n):
                    return x[:, gs, :].unsqueeze(2).broadcast_to([SSM_P, GE, n, SSM_C])

                def split(x):
                    return x.rearrange("p g (j c) -> p g j c", c=SSM_C)

                def scratch(n):
                    return [tt[q][:, 0:GE * n * SSM_C].rearrange("p (g j c) -> p g j c", j=n, c=SSM_C)
                            for q in range(2)]

                chain(V.tensor_tensor(tt4[0], s_phi[:, gs].unsqueeze(2).broadcast_to([SSM_P, GE, P]),
                                      iota.unsqueeze(1).broadcast_to([SSM_P, GE, P]), mul))
                x, k = tt[0][:, 0:512], tt[1][:, 0:512]
                chain(V.tensor_scalar(k, x, 1.0 / TWO_PI, ROUNDER, mul, add))
                chain(V.tensor_scalar(k, k, ROUNDER, None, sub))
                chain(V.scalar_tensor_tensor(x, k, -TWO_PI_HI, x, mul, add))
                chain(V.scalar_tensor_tensor(x, k, -TWO_PI_LO, x, mul, add))
                V.tensor_scalar(x, x, PI_IN, -PI_IN, ALU.min, ALU.max).then_inc(ssm_angle, 1)
                V.tensor_tensor(r8, s_r8[:, gs].unsqueeze(2).broadcast_to([SSM_P, GE, P]), not_first, mul)
                Uv = U[:, :, bass.ds(i * (GE * SSM_C), GE * SSM_C)].rearrange("p j (g c) -> p g j c", c=SSM_C)
                Uqv = Uq.rearrange("p g (j c) -> p g j c", c=SSM_C)
                for g in range(GE):
                    ins = V.tensor_scalar(Uqv[:, g, :, :], Uv[:, g, :, :], 1.0, None, mul)
                ins.then_inc(ssm_u, 1)
                dve.wait_ge(ssm_u, i + 1)
                dve.wait_ge(ssm_trig, i + 1)
                chain(V.tensor_tensor(e_re, e_re, e_re, mul))
                chain(V.tensor_scalar(e_re, e_re, -2.0, 1.0, mul, add))
                t = scratch(9)
                chain(complex_product(split(v_re), split(v_im), (chans(c_re, 9), chans(c_im, 9)),
                                      (lags(pw_re, 9), lags(pw_im, 9)), t))
                chain(V.tensor_scalar(v_im, v_im, -1.0, None, mul))
                for n, x in enumerate((bb_re, bb_im)):
                    chain(V.tensor_scalar(bst[:, n, 0:GE * SSM_C].rearrange("p (g c) -> p g c", c=SSM_C), x[:, gs, :],
                                          1.0, None, mul))
                t = scratch(8)
                complex_product(split(wt_re), split(wt_im), (chans(bb_re, 8), chans(bb_im, 8)),
                                (lags(rv_re, 8), lags(rv_im, 8)), t).then_inc(ssm_w, 1)
                dve.wait_ge(ssm_w, i + 1)
                w = []
                for n in range(2):
                    b = wait_full(dve, G_SSM, 4 + n, i, SSM_ROUND)
                    w.append(ps[0:SSM_P, b, :].rearrange("p (g c) -> p g c", c=P)[:, :, 0:P - 1])
                er, ei = e_re[:, :, 1:P], e_im[:, :, 1:P]
                t = [tt4[0][:, :, 1:P], tt4[1][:, :, 1:P]]
                dr, di = d_re[:, :, 1:P], d_im[:, :, 1:P]
                chain(V.tensor_tensor(t[0], er, w[0], mul))
                chain(V.tensor_tensor(t[1], ei, w[1], mul))
                chain(V.tensor_tensor(dr, t[0], t[1], add))
                b1 = where(G_SSM, 5)[0]
                b0 = where(G_SSM, 4)[0]
                V.tensor_tensor(t[0], er, w[1], mul).then_inc(drained[b1], 1)
                V.tensor_tensor(t[1], ei, w[0], mul).then_inc(drained[b0], 1)
                wait_drained(dve, G_SSM, 5, i, SSM_ROUND)
                wait_drained(dve, G_SSM, 4, i, SSM_ROUND)
                chain(V.tensor_tensor(di, t[0], t[1], sub))

                def flat(x):
                    return x.rearrange("p a b -> p (a b)")
                chain(V.tensor_tensor_scan(flat(s_re), flat(r8), flat(d_re), 0.0, mul, add))
                chain(V.tensor_tensor_scan(flat(s_im), flat(r8), flat(d_im), 0.0, mul, add))
                complex_product(d_re, d_im, (e_re, e_im), (s_re, s_im), tt4).then_inc(ssm_state, 1)
                dve.wait_ge(ssm_state, i + 1)
                dv = d_row[:, bass.ds(i * (GE * SSM_C), GE * SSM_C)].rearrange("p (g c) -> p g c", c=SSM_C)
                ytv = yt.rearrange("p g (j c) -> p g j c", c=SSM_C)
                chain(V.tensor_tensor(ytv, Uqv, dv.unsqueeze(2).broadcast_to([P, GE, SUB, SSM_C]), mul))
                for n in range(2):
                    b = wait_full(dve, G_SSM, 6 + n, i, SSM_ROUND)
                    chain(V.tensor_tensor(yt[:, 2 * n:2 * n + 2, :], yt[:, 2 * n:2 * n + 2, :],
                                          ps[:, b, 0:2 * P].rearrange("p (g c) -> p g c", c=P), add))
                    for g in range(2 * n, 2 * n + 2):
                        ins = V.tensor_scalar(Uv[:, g, :, :], ytv[:, g, :, :], 1.0, None, mul)
                    ins.then_inc(drained[b], 1)
                    wait_drained(dve, G_SSM, 6 + n, i, SSM_ROUND)
                assert own[0] == SSM_OWN, own[0]

            dve.wait_ge(b2_in, 48)
            for b in range(2):
                then(V.memset(zp[b], 0.0))
            for ft in range(WT):
                z = zp[ft % 2]
                for h in range(2):
                    k = 2 * ft + h
                    wait_drained(dve, G_HCB, k)
                    b = wait_full(dve, G_HCB, 8 + k)
                    V.scalar_tensor_tensor(z[:, 2 * P + 512 * h:2 * P + 512 * h + 512], ps[:, b, :],
                                           bias_col[:, 4 + ft:5 + ft], BZ[:, ft, 512 * h:512 * h + 512],
                                           add, mul).then_inc(drained[b], 1)
                    wait_drained(dve, G_HCB, 8 + k)
                then(V.tensor_copy(z[:, 1:P], z[:, 8 * P:9 * P - 1]))
                then(V.tensor_copy(z[:, P + 1:2 * P], z[:, 9 * P:10 * P - 1]))
                o = BZ[:, ft, :]
                then(V.tensor_scalar(o, z[:, 0:SEQ], taps2[:, ft, 0:1], None, mul))
                then(V.scalar_tensor_tensor(o, z[:, P:P + SEQ], taps2[:, ft, 1:2], o, mul, add))
                then(V.scalar_tensor_tensor(o, z[:, 2 * P:2 * P + SEQ], taps2[:, ft, 2:3], o, mul, add))
            for k in range(8):
                b = wait_full(dve, G_HCB, 16 + k)
                o = BZ[:, k // 2, 512 * (k % 2):512 * (k % 2) + 512]
                V.scalar_tensor_tensor(o, ps[:, b, :], bias_col[:, 8 + k // 2:9 + k // 2], o, add, mul
                                       ).then_inc(drained[b], 1)
            for k in range(8):
                dve.wait_ge(sig_done, k + 1)
                hs = slice(512 * (k % 2), 512 * (k % 2) + 512)
                if k == 0:
                    wait_full(dve, G_YT, 7)
                b = where(G_GLU, k)[0]
                V.tensor_tensor(YA[:, k // 2, hs], gT[:, k // 2, hs], sig[k % 4], mul).then_inc(drained[b], 1)
            then(V.memset(s_t1, 0.0))
            for k in range(8):
                wait_drained(dve, G_GLU, k)
            V.memset(s_t2, 0.0).then_inc(merged_rows, 8)
            with dve.Fori(0, MRG_ROUNDS) as i:
                for ft in range(2):
                    for h in range(2):
                        r = 2 * ft + h
                        k0 = 4 * r
                        s0, s1 = sig[2 * (r % 2)], sig[2 * (r % 2) + 1]
                        for n, x in enumerate((s0, s1)):
                            wait_drained(dve, G_MRG, k0 + n, i, MRG_ROUND)
                            b = wait_full(dve, G_MRG, k0 + 2 + n, i, MRG_ROUND)
                            V.tensor_tensor(x, x, ps[:, b, :], mul).then_inc(drained[b], 1)
                        for n in range(2):
                            wait_drained(dve, G_MRG, k0 + 2 + n, i, MRG_ROUND)
                        V.tensor_tensor(M[:, bass.ds(i * 2 + ft, 1), 512 * h:512 * h + 512].rearrange("p a b -> p (a b)"),
                                        s0, s1, add).then_inc(merged_rows, 1)
            for h in range(2):
                for t in range(NT):
                    b = wait_full(dve, G_WO, 8 * h + t)
                    xs = X[:, t, 512 * h:512 * h + 512]
                    V.scalar_tensor_tensor(xs, xs, ALPHA, ps[:, b, :], mul, add).then_inc(drained[b], 1)

            def layer_rows(count):
                dve.wait_ge(ln_sum, count * NT)
                V.tensor_scalar(mean, ssum, -1.0 / D, None, mul).then_inc(ln_mean, 1)
                dve.wait_ge(ln_sq, count * NT)
                V.tensor_scalar(rs_arg[:, 0:NT], rstd, 1.0 / D, LN_EPS, mul, add).then_inc(root_ask, 1)
                inverse_root(NT)
                V.tensor_tensor(ssum, mean, rs_y[:, 0:NT], mul).then_inc(ln_mean2, 1)
                dve.wait_ge(gain_in, 16 * (3 + 2 * count))
                for j in range(NT):
                    dve.wait_ge(ln_scaled, (count - 1) * NT + j + 1)
                    then(V.tensor_tensor(X[:, j, :], xn[:, j, :], gain, mul))
                    V.tensor_tensor(X[:, j, :], X[:, j, :], shift, add).then_inc(ln_rows, 1)

            layer_rows(1)
            rest_features(G_LN1, 1)
            dve.wait_ge(ln_rows, 8)
            for j in range(NT):
                wait_full(dve, G_LN1, 2 * j + 1)
                ins = V.tensor_scalar(X[:, j, :], X[:, j, :], ALPHA, None, mul)
            then(ins)
            def rest_slab2(q, i):
                dve.wait_ge(v_hi, i * 3 + q + 1)
                V.tensor_tensor(ws2[q][1].ap(), wraw2[q], ws2[q][0].ap().bitcast(F32), sub).then_inc(v_lo, 1)
            for q in range(3):
                rest_slab2(q, 0)

            def f2_round(i, last):
                start, at = at_round(G_F2, i, F2_ROUND)
                for q in range(4):
                    wait_drained(dve, start, 2 * q, **at)
                    b = wait_full(dve, start, 2 * q + 1, **at)
                    V.tensor_tensor(hg[q % 2], hg[q % 2], ps[:, b, :], mul).then_inc(hid_f, 1)
                    dve.wait_ge(hid_hi, i * 4 + q + 1)
                    part = (slice(None), q // 2, slice(512 * (q % 2), 512 * (q % 2) + 512))
                    V.tensor_tensor(hids[1][part], hg[q % 2], hids[0][part].bitcast(F32), sub).then_inc(drained[b], 1)
                for t in range(NT):
                    if not last and t == 1:
                        for q in range(2):
                            rest_slab2(q, i + 1)
                    for h in range(2):
                        b = wait_full(dve, start, 8 + 2 * t + h, **at)
                        xs = X[:, t, 512 * h:512 * h + 512]
                        V.tensor_tensor(xs, xs, ps[:, b, :], add).then_inc(drained[b], 1)
                if not last:
                    rest_slab2(2, i + 1)
            rounds(dve, F2_ROUNDS, f2_round)
            for k in range(8, 24):
                wait_drained(dve, last_f2, k)
            layer_rows(2)


GDN_OWN = 14
SSM_OWN = 35
PI_IN = 3.1415925


def kernel(**inputs):
    import numpy as _np
    import concourse.bacc as _bacc
    from concourse import mybir as _mybir
    from concourse.bass_utils import run_bass_kernel_spmd as _run

    def c(a):
        return _np.ascontiguousarray(a)

    arrays = {n: c(inputs[n][0]) for n in ("x", "norm_mix", "w_in", "a_log_fwd", "dt_bias_fwd", "a_log_bwd",
                                           "dt_bias_bwd", "gdn_norm", "sgu_v_norm", "sgu_out_norm", "w_out",
                                           "norm_ffn", "w_ff1", "w_ff2")}
    arrays["norm_final"] = c(inputs["norm_final"])
    arrays["conv_wT"] = c(inputs["conv_w"][0].T)
    arrays["sgu_bT"] = c(inputs["sgu_b"][0].T)
    arrays["sgu_wT"] = c(_np.swapaxes(inputs["sgu_w"][0], 1, 2))
    arrays["shape_constants"] = shape_constants()
    for n in ("w_in", "glu_w", "w_ssm_out", "w_conv_out", "w_o", "ln1_g", "ln1_b", "w_gate", "w_up", "w_down",
              "ln2_g", "ln2_b", "ssm_d"):
        arrays[n if n != "w_in" else "w_in_2"] = c(inputs[n + "_2"][0])
    b_in = inputs["b_in_2"][0]
    arrays["b_in"] = c(b_in)
    arrays["bias_col"] = c(b_in[W2:].reshape(-1, P).T)
    arrays["glu_col"] = c(inputs["glu_b_2"][0].reshape(-1, P).T)
    arrays["conv_taps_2"] = c(inputs["conv_w_2"][0].T.reshape(WT, P, 3).transpose(1, 0, 2).reshape(P, WT * 3))
    arrays["lam_re"] = c(inputs["ssm_lambda_re_2"][0].T)
    arrays["lam_im"] = c(inputs["ssm_lambda_im_2"][0].T)
    arrays["log_dt"] = c(inputs["ssm_log_dt_2"][0])
    arrays["b_re"] = c(inputs["ssm_b_re_2"][0].transpose(1, 0, 2))
    arrays["b_im"] = c(inputs["ssm_b_im_2"][0].transpose(1, 0, 2))
    arrays["c_re"] = c(inputs["ssm_c_re_2"][0].transpose(2, 0, 1))
    arrays["c_im"] = c(inputs["ssm_c_im_2"][0].transpose(2, 0, 1))
    arrays["counts"] = _np.arange(P, dtype=_np.float32)

    nc = _bacc.Bacc("TRN2", target_bir_lowering=False, num_devices=1)
    A = {n: nc.dram_tensor(f"in_{n}", a.shape, _mybir.dt.from_np(a.dtype), kind="ExternalInput").ap()
         for n, a in arrays.items()}
    out = nc.dram_tensor("out_x", (SEQ, D), F32, kind="ExternalOutput").ap()
    build(nc, A, out, A["shape_constants"])
    r = _run(nc, [{f"in_{n}": a for n, a in arrays.items()}], core_ids=[0])
    return r.results[0]["out_x"].reshape(1, SEQ, D)
```

```python
from contextlib import ExitStack

import numpy as np

import concourse.bass as bass
from concourse import mybir

F32 = mybir.dt.float32
F32R = mybir.dt.float32r
ALU = mybir.AluOpType
ACT = mybir.ActivationFunctionType
AX_X = mybir.AxisListType.X

P = 128
SEQ = 1024
D = 1024
NT = SEQ // P
KT = D // P
BANKS = 8
HEADS, HD = 8, 64
GW = HEADS * HD
CONV_K = 5
SG = 4
FF = 4096
EPS = 1e-6
LN_EPS = 1e-5
ALPHA = 2.0 ** 0.25
W2 = 512
WT = W2 // P
SSM_C = 16
SSM_G = W2 // SSM_C
SSM_P = 64
SUB = 8
GE = 4
SSM_ROUNDS = SSM_G // GE
F2 = 2816
F2_ROUNDS = F2 // 256
TWO_PI = 2.0 * np.pi
TWO_PI_HI = 6.28125
TWO_PI_LO = float(TWO_PI - 6.28125)
LN2_HI = 0.693359375
LN2_LO = float(np.log(2.0) - 0.693359375)
ROUNDER = 12582912.0
LEVELS = 7
MASKS = 2 * LEVELS + 4


def shape_constants():
    i = np.arange(P)[:, None]
    j = np.arange(P)[None, :]
    out = np.zeros((P, MASKS, P), np.float32)
    for lv in range(LEVELS):
        b = 1 << lv
        low = (i // (2 * b) == j // (2 * b)) & ((i // b) % 2 == 1) & ((j // b) % 2 == 0)
        out[:, lv] = low
        out[:, LEVELS + lv] = low.T
    out[:, 2 * LEVELS] = i <= j
    out[:, 2 * LEVELS + 1] = i >= j
    out[:, 2 * LEVELS + 2] = i == j
    out[:, 2 * LEVELS + 3] = 1.0
    return out


G_NORM1 = 0
G_QKV = G_NORM1 + 16
G_ROWS = G_QKV + 48
G_SGU = G_ROWS + 17
G_Z = G_SGU + 8
G_SGT = G_Z + 8
G_GDN = G_SGT + 8


def gdn_order():
    both, batches = (0, 1), [(d, h) for d in (0, 1) for h in (0, 1)]
    order = [("sums", d) for d in both] + [("rows", *x) for x in batches]
    order += [("keys", d) for d in both] + [("queries", d) for d in both]
    order += [("kk", *x) for x in batches] + [("kq", *x) for x in batches] + [("U", 0, *x) for x in batches]
    for lv in range(1, LEVELS):
        for name in ("Q", "T", "U") if lv < LEVELS - 1 else ("Q", "U"):
            order += [(name, lv, *x) for x in batches]
        if lv == 1:
            order += [("kS", *x) for x in batches]
    for name in ("v", "o"):
        order += [(name, *x) for x in batches]
    order += [("kv", d) for d in both]
    return {key: n for n, key in enumerate(order)}


GDN_AT = gdn_order()
GDN_ROUND = len(GDN_AT)
assert GDN_ROUND % BANKS == 0
G_MIXT = G_GDN + NT * GDN_ROUND
G_WOUT = G_MIXT + 8
G_NORM2 = G_WOUT + 16
G_FF = G_NORM2 + 16
FF_ROUND = 24
FF_ROUNDS = FF // 512
G_NORM3 = G_FF + FF_ROUNDS * FF_ROUND
G_U = G_NORM3 + 16
G_SSM = G_U + 8
SSM_STEP = 12
SSM_ROUND = 2 * SSM_STEP
S_HC, S_WT, S_KALL, S_UT, S_W, S_Y = 0, 2, 4, 5, 6, 8
G_YT = G_SSM + SSM_ROUNDS * SSM_STEP
G_GLU = G_YT + 8
G_B = G_GLU + 8
G_MRG = G_B + 8
MRG_ROUND = 16
MRG_ROUNDS = 4
G_WO = G_MRG + MRG_ROUNDS * MRG_ROUND
G_LN1 = G_WO + 16
G_F2 = G_LN1 + 16
F2_ROUND = 24


def build(nc, A, out, consts):
    with ExitStack() as ctx:
        def sem(name):
            return ctx.enter_context(nc.semaphore(name))

        WORDS = 52736
        arena = (nc.sbuf_base + 31) // 32 * 32
        sb = ctx.enter_context(nc.sbuf_tensor("sb", [P, WORDS], F32))
        ps = ctx.enter_context(nc.psum_tensor("ps", [P, BANKS, 512], F32))

        def area(at, *shape, parts=P):
            size = int(np.prod(shape))
            assert at + size <= WORDS
            v = sb[0:parts, at:at + size]
            if len(shape) == 2:
                v = v.rearrange("p (a b) -> p a b", b=shape[1])
            elif len(shape) == 3:
                v = v.rearrange("p (a b c) -> p a b c", b=shape[1], c=shape[2])
            return v

        def split_area(name, at, *shape):
            assert at + int(np.prod(shape)) <= WORDS
            return nc.alloc_sbuf_tensor_at(name, [P, *shape], F32R, offset=arena + 4 * at)

        def plain_area(name, at, *shape):
            assert at + int(np.prod(shape)) <= WORDS
            return nc.alloc_sbuf_tensor_at(name, [P, *shape], F32, offset=arena + 4 * at).ap()

        AT_X, AT_H, AT_W, AT_WORK, AT_CONST = 0, 8192, 16384, 24576, 46336
        X = area(AT_X, NT, D)
        H = area(AT_H, KT, SEQ)
        ring = [area(AT_W, 8, 512), area(AT_W + 4096, 8, 512)]
        masks = area(AT_CONST, MASKS, P)
        ident, ones = masks[:, 2 * LEVELS + 2, :], masks[:, 2 * LEVELS + 3, :]
        at = AT_CONST + MASKS * P
        gain = area(at, D)
        shift = area(at + D, D)
        at += 2 * D
        ssum = area(at, NT)
        rstd = area(at + 8, NT)
        mean = area(at + 16, NT)
        at += 32
        sgu_vg = area(at, SG, P)
        sgu_og = area(at + 512, SG, P)
        at += 1024
        sgu_bt = area(at, SG)
        conv_taps = area(at + 4, 12, CONV_K)
        gdn_gain = area(at + 64, HD)
        dt_row = area(at + 128, 16)
        alog_row = area(at + 144, 16)
        rs_arg, rs_root, rs_y, rs_t = (area(at + 160 + 128 * n, 128) for n in range(4))
        assert at + 672 <= WORDS

        QKV = area(AT_WORK, NT, 3 * GW)
        Z = area(AT_X, NT, GW)
        SU = area(AT_X + 4096, NT, GW)
        SV = area(AT_WORK + 12288, NT, GW)
        O = SV
        TMP = AT_WORK + 16384
        raw = [area(TMP + 1028 * b, 1028) for b in range(2)]
        cv = [area(TMP + 2056 + 1024 * b, SEQ) for b in range(2)]
        GT = TMP + 4104
        wgate = area(GT, KT, 32)
        graw = area(GT + 256, NT, 32)
        gdec = area(GT + 512, NT, 16)
        gbeta = area(GT + 640, NT, 16)
        gt1 = area(GT + 768, NT, 16)
        gt2 = area(GT + 896, NT, 16)
        assert GT + 1024 <= AT_CONST
        sgu_w = area(TMP, SG, P)
        sq = area(TMP + 512, 1024)
        vst = area(TMP + 1536, 16)
        Lm, Tm, Um, Cm = ([area(AT_W + 1024 * (2 * n + d), HEADS, P) for d in range(2)] for n in range(4))
        gd = AT_X + 4096
        Qt, DTm = ([area(gd + 1024 * (2 * n + d), HEADS, P) for d in range(2)] for n in range(2))
        Rm = Qt
        KTr, QTr, QdT = ([area(AT_H + 512 * (2 * n + d), 4, P) for d in range(2)] for n in range(3))
        KQ = [area(TMP + 1024 * d, 2 * HEADS, HD) for d in range(2)]
        vnew = [x[:, HEADS:, :] for x in KQ]
        kS, Kdec = ([area(TMP + 2048 + 512 * (2 * n + d), HEADS, HD) for d in range(2)] for n in range(2))
        S = [area(TMP + 4096 + 256 * d, 4, HD) for d in range(2)]
        gd = AT_CONST + MASKS * P
        Vb = [area(gd + 512 * d, HEADS, HD) for d in range(2)]
        exin = [area(gd + 1024 + 64 * d, 3, HEADS) for d in range(2)]
        ex = [area(gd + 1152 + 64 * d, 3, HEADS) for d in range(2)]
        bege = [area(gd + 1280 + 64 * d, HEADS) for d in range(2)]
        egl = [area(gd + 1408 + 64 * d, 4) for d in range(2)]
        gnow = [area(gd + 1536 + 64 * d, HEADS) for d in range(2)]

        def batch(x, h):
            return x[:, h:HEADS:2]

        def half(x, head):
            lo = HD * (head % 2)
            return x[lo:lo + HD, head // 2, :]

        def level_columns(x, lv, d):
            width = 1 << lv
            return x.rearrange("p k (n a b) -> p k n a b", a=2, b=width)[:, :, :, d, :]

        mixT = H
        xin = area(AT_WORK, NT, D)
        Hs = [split_area(f"H_{n}", AT_H + 8192 * q, KT, SEQ) for q, n in enumerate(("hi", "lo"))]
        ffs = [split_area(f"ff_{n}", AT_WORK + 4096 * q, 4, SEQ) for q, n in enumerate(("hi", "lo"))]
        ws = [[split_area(f"w{b}_{n}", AT_WORK + 8192 + 4096 * b + 2048 * q, 2048) for q, n in enumerate(("hi", "lo"))]
              for b in range(2)]
        wraw = [plain_area(f"wraw{b}", AT_WORK + 16384 + 2048 * b, 2048) for b in range(2)]
        fft = [plain_area(f"fft{b}", AT_WORK + 20480 + 512 * b, 512) for b in range(2)]
        xn = area(AT_WORK + 8192, NT, D)

        BZ = area(AT_WORK, WT, SEQ)
        U = area(AT_WORK + 4096, NT, W2)
        YA = area(AT_WORK + 4096, WT, SEQ)
        M = area(AT_WORK + 8192, KT, SEQ)
        gT = area(AT_WORK + 8192, WT, SEQ)
        T2 = AT_WORK + 16384
        hc_slab = [area(AT_W + 1024 * b, KT, P) for b in range(2)]
        zp = area(AT_W + 2048, WT, 10 * P)
        h_now = area(AT_W + 7168, SEQ)
        wo_first = (area(T2 + 2048, 6, 512), area(AT_CONST + MASKS * P + 2 * D + 32, 2, 512))
        b_slab = area(AT_WORK + 12288, KT, W2)
        d_row = area(T2 + 2560, W2)
        u_row = area(T2 + 3072, W2)
        sig = [area(T2 + 512 * b, 512) for b in range(4)]
        hids = [split_area(f"hid_{n}", AT_WORK + 2048 * q, 2, SEQ) for q, n in enumerate(("hi", "lo"))]
        ws2 = [[split_area(f"v{b}_{n}", AT_WORK + 4096 + 4096 * b + 2048 * q, 2048) for q, n in enumerate(("hi", "lo"))]
               for b in range(3)]
        wraw2 = [plain_area(f"vraw{b}", AT_WORK + 16384 + 2048 * b, 2048) for b in range(3)]
        hg = [plain_area(f"hg{b}", AT_WORK + 16384 + 6144 + 512 * b, 512) for b in range(2)]
        assert AT_WORK + 16384 + 6144 + 1024 <= AT_CONST + 2 * LEVELS * P
        at2 = AT_CONST
        bias_col = area(at2, 28)
        glu_col = area(at2 + 28, WT)
        taps2 = area(at2 + 32, WT, 3)
        bias_now = area(at2 + 44, 2, 2)
        hc_bias = area(at2 + 48, 2)
        at2 += 64

        def small(n):
            return area(at2 + 32 * n, SSM_G, parts=SSM_P)
        (s_lr, s_li, s_dt, s_x, s_k, s_r, s_e, s_mag, s_th, s_sin, s_cos, s_half, s_den, s_nr, s_fr, s_fi,
         s_phi, s_r8, s_t1, s_t2) = (small(n) for n in range(20))
        at2 += 640
        pw_re = area(at2, 9, SSM_G, parts=SSM_P)
        pw_im = area(at2 + 288, 9, SSM_G, parts=SSM_P)
        assert at2 + 576 <= AT_CONST + 2 * LEVELS * P
        sm = AT_WORK
        b_re, b_im, c_re, c_im = (area(sm + 512 * n, SSM_G, SSM_C, parts=SSM_P) for n in range(4))
        bb_re, bb_im = (area(sm + 2048 + 512 * n, SSM_G, SSM_C, parts=SSM_P) for n in range(2))
        rv_re, rv_im = (area(sm + 3072 + 256 * n, SUB, SSM_G, parts=SSM_P) for n in range(2))
        bst = area(sm + 3584, 2, 192, parts=SSM_P)
        iota = area(sm + 3968, P, parts=SSM_P)
        sm = AT_WORK + 8192
        wt_re, wt_im = (area(sm + 512 * n, GE, SUB * SSM_C, parts=SSM_P) for n in range(2))
        v_re, v_im = (area(sm + 1024 + 576 * n, GE, 9 * SSM_C, parts=SSM_P) for n in range(2))
        kall = area(sm + 2176, GE, P, parts=SSM_C)
        toep = area(sm + 2688, GE, P)
        wl_re, wl_im = (area(sm + 3200 + 256 * n, GE, SSM_P) for n in range(2))
        e_re, e_im = (area(sm + 3712 + 512 * n, GE, P, parts=SSM_P) for n in range(2))
        r8 = area(sm + 4736, GE, P, parts=SSM_P)
        d_re, d_im = (area(sm + 5248 + 512 * n, GE, P, parts=SSM_P) for n in range(2))
        uT = area(sm + 6272, GE, P)
        Uq = area(sm + 6784, GE, P)
        not_first = area(sm + 7296, GE, P, parts=SSM_P)
        tt = [area(T2 + 576 * n, 576, parts=SSM_P) for n in range(2)]
        tt4 = [area(T2 + 576 * n, GE, P, parts=SSM_P) for n in range(2)]
        s_re, s_im = wt_re, wt_im
        yt = area(T2 + 1152, GE, P)

        b2_in = sem("b2_in")
        ssm_in = sem("ssm_in")
        ssm_sin = sem("ssm_sin")
        ssm_own = sem("ssm_own")
        ssm_pre = sem("ssm_pre")
        ssm_w = sem("ssm_w")
        ssm_u = sem("ssm_u")
        ssm_angle = sem("ssm_angle")
        ssm_trig = sem("ssm_trig")
        ssm_state = sem("ssm_state")
        toep_in = sem("toep_in")
        mrg_in = [sem(f"mrg_in{b}") for b in range(2)]
        wo_in = sem("wo_in")
        hc_in = [sem(f"hc_in{b}") for b in range(2)]
        hc_bias_set = sem("hc_bias_set")
        conv2_done = sem("conv2_done")
        sig_done = sem("sig_done")
        ln_sum = sem("ln_sum")
        ln_mean = sem("ln_mean")
        ln_sq = sem("ln_sq")
        ln_scaled = sem("ln_scaled")
        ln_rows = sem("ln_rows")
        merged_rows = sem("merged_rows")
        ln_mean2 = sem("ln_mean2")
        bias_set = sem("bias_set")

        full = [sem(f"full{b}") for b in range(BANKS)]
        drained = [sem(f"drained{b}") for b in range(BANKS)]
        consts_in = sem("consts_in")
        x_in = sem("x_in")
        slab_in = [sem(f"slab_in{b}") for b in range(2)]
        gain_in = sem("gain_in")
        wgate_in = sem("wgate_in")
        sguw_in = sem("sguw_in")
        dve_step = sem("dve_step")
        act_step = sem("act_step")
        norm_sums = sem("norm_sums")
        norm_rows = sem("norm_rows")
        root_ask = sem("root_ask")
        root_done = sem("root_done")
        conv_done = sem("conv_done")
        silu_done = sem("silu_done")
        pads_set = sem("pads_set")
        gate_in = sem("gate_in")
        gate_out = sem("gate_out")
        sgu_v = sem("sgu_v")
        sgu_o = sem("sgu_o")
        gdn_ready = sem("gdn_ready")
        gdn_exin = sem("gdn_exin")
        gdn_ex = sem("gdn_ex")
        gdn_stage = sem("gdn_stage")
        gdn_go = sem("gdn_go")
        gdn_rexp = sem("gdn_rexp")
        gdn_din = sem("gdn_din")
        gdn_dexp = sem("gdn_dexp")
        gdn_vk = sem("gdn_vk")
        gdn_t0 = sem("gdn_t0")
        gdn_c = sem("gdn_c")
        gdn_qd = sem("gdn_qd")
        gdn_step = sem("gdn_step")
        gdn_over = sem("gdn_over")
        mix_rows = sem("mix_rows")
        xin_in = sem("xin_in")
        relu_done = sem("relu_done")
        square_done = sem("square_done")
        raw_in = [sem(f"raw_in{b}") for b in range(2)]
        raw2_in = [sem(f"raw2_in{b}") for b in range(3)]
        w_hi = sem("w_hi")
        w_lo = sem("w_lo")
        v_hi = sem("v_hi")
        v_lo = sem("v_lo")
        feat_hi = sem("feat_hi")
        ff_hi = sem("ff_hi")
        hid_f = sem("hid_f")
        hid_hi = sem("hid_hi")
        out_done = sem("out_done")

        block = ctx.enter_context(nc.Block())

        def where(start, k, i=None, per=0):
            g = start + k
            use = g // BANKS
            return g % BANKS, (use if i is None else i * (per // BANKS) + use)

        def wait_full(eng, start, k, i=None, per=0):
            b, use = where(start, k, i, per)
            eng.wait_ge(full[b], use + 1)
            return b

        def wait_drained(eng, start, k, i=None, per=0):
            b, use = where(start, k, i, per)
            eng.wait_ge(drained[b], use + 1)

        def wait_bank(eng, start, k, i=None, per=0):
            b, use = where(start, k, i, per)
            if i is not None or use > 0:
                eng.wait_ge(drained[b], use)
            return b

        HI_LO = ((0, 0), (0, 1), (1, 0))

        FF_SLAB_END = (3, 7, 15, 23)

        def ff_slab_done(eng, q, i):
            start = G_FF if q >= 0 else G_FF - FF_ROUND
            if isinstance(i, int):
                if q >= 0 or i > 0:
                    wait_full(eng, start + i * FF_ROUND, FF_SLAB_END[q])
            else:
                wait_full(eng, start, FF_SLAB_END[q], i, FF_ROUND)

        def at_round(start, i, per):
            return (start + i * per, {}) if isinstance(i, int) else (start, dict(i=i, per=per))

        def rounds(eng, count, body):
            with eng.Fori(0, count - 1) as i:
                body(i, False)
            body(count - 1, True)

        def strided_view(hview):
            return hview.rearrange("p k (c j) -> p k c j", j=8)

        last_mrg = G_MRG + (MRG_ROUNDS - 1) * MRG_ROUND
        last_f2 = G_F2 + (F2_ROUNDS - 1) * F2_ROUND
        w_in, w_out, w_ff1, w_ff2 = A["w_in"], A["w_out"], A["w_ff1"], A["w_ff2"]
        Z0 = 3 * GW
        SU0 = 4 * GW + 4 * HEADS
        slab_cols = [0, 512, 1024, SU0 + GW, SU0, Z0]
        slab_last = [(G_QKV, 13), (G_QKV, 29), (G_QKV, 45), (G_ROWS, 7), (G_ROWS, 15), (G_Z, 7),
                     (G_WOUT, 7), (G_WOUT, 15)]
        def dense_at(ct):
            return 2 * ct if ct == 0 else 4 * ct - 2
        def turn_at(ct):
            return 4 * ct + 4 if ct < 11 else 46

        @block.sync
        def _(sp):
            xv = A["x"].rearrange("(p j) d -> p j d", j=NT)
            for h in range(2):
                sp.dma_start(X[:, 4 * h:4 * h + 4, :], xv[:, 4 * h:4 * h + 4, :]).then_inc(x_in, 16)
            sp.dma_start(gain, A["norm_mix"].partition_broadcast(P)).then_inc(gain_in, 16)
            sp.dma_start(masks, consts).then_inc(consts_in, 16)
            sp.dma_start(conv_taps, A["conv_wT"].rearrange("(t p) k -> p t k", p=P)).then_inc(consts_in, 16)
            sp.dma_start(sgu_vg, A["sgu_v_norm"].partition_broadcast(P)).then_inc(consts_in, 16)
            sp.dma_start(sgu_og, A["sgu_out_norm"].partition_broadcast(P)).then_inc(consts_in, 16)
            sp.dma_start(sgu_bt, A["sgu_bT"]).then_inc(consts_in, 16)
            sp.dma_start(gdn_gain, A["gdn_norm"].partition_broadcast(P)).then_inc(consts_in, 16)
            sp.dma_start(dt_row[:, 0:8], A["dt_bias_fwd"].partition_broadcast(P)).then_inc(consts_in, 16)
            sp.dma_start(dt_row[:, 8:16], A["dt_bias_bwd"].partition_broadcast(P)).then_inc(consts_in, 16)
            sp.dma_start(alog_row[:, 0:8], A["a_log_fwd"].partition_broadcast(P)).then_inc(consts_in, 16)
            sp.dma_start(alog_row[:, 8:16], A["a_log_bwd"].partition_broadcast(P)).then_inc(consts_in, 16)
            sp.dma_start(wgate, w_in[:, 4 * GW:4 * GW + 32].rearrange("(k p) n -> p k n", p=P)).then_inc(wgate_in, 16)
            for n, c0 in enumerate(slab_cols):
                if n >= 2:
                    wait_full(sp, *slab_last[n - 2])
                sp.dma_start(ring[n % 2], w_in[:, c0:c0 + 512].rearrange("(k p) n -> p k n", p=P)
                             ).then_inc(slab_in[n % 2], 16)
                if n == 4:
                    wait_drained(sp, G_QKV, 47)
                    sp.dma_start(sgu_w, A["sgu_wT"].rearrange("g s t -> s g t")).then_inc(sguw_in, 16)
            sp.wait_ge(gdn_over, 1)
            for h in range(2):
                sp.dma_start(xin[:, 4 * h:4 * h + 4, :], xv[:, 4 * h:4 * h + 4, :]).then_inc(xin_in, 16)
            for h in range(2):
                sp.dma_start(ring[h], w_out[:, 512 * h:512 * h + 512].rearrange("(k p) n -> p k n", p=P)
                             ).then_inc(slab_in[h], 16)
            wait_full(sp, G_NORM1, 15)
            sp.dma_start(gain, A["norm_ffn"].partition_broadcast(P)).then_inc(gain_in, 16)
            w1v = w_ff1.rearrange("(k p) (r n) -> p k r n", p=P, n=256)
            w2v = w_ff2.rearrange("(r k p) n -> p r k n", k=4, p=P)

            def ff_load(q, i):
                row = bass.ds(i, 1)
                dst = wraw[q % 2]
                if q < 2:
                    src = w1v[:, :, bass.ds(i * 2 + q, 1), :]
                    dst = dst.rearrange("p (k n) -> p k n", n=256)
                else:
                    src = w2v[:, row, :, 512 * (q - 2):512 * (q - 2) + 512]
                    dst = dst.rearrange("p (k n) -> p k n", n=512)
                sp.dma_start(dst, src).then_inc(raw_in[q % 2], 16)

            def ff_loads(i, last):
                for q in range(4):
                    sp.wait_ge(w_lo, i * 4 + q + 1)
                    if q < 2:
                        ff_load(q + 2, i)
                    elif not last:
                        ff_load(q - 2, i + 1)

            wait_full(sp, G_WOUT, 15)
            ff_load(0, 0)
            ff_load(1, 0)
            rounds(sp, FF_ROUNDS, ff_loads)
            wait_full(sp, G_NORM2, 15)
            sp.dma_start(gain, A["norm_final"].partition_broadcast(P)).then_inc(gain_in, 16)
            last_ff = G_FF + (FF_ROUNDS - 1) * FF_ROUND
            wi2 = A["w_in_2"].rearrange("(k p) n -> p k n", p=P)
            wait_full(sp, last_ff, 7)
            sp.dma_start(ring[0], wi2[:, :, 0:512]).then_inc(slab_in[0], 16)
            sp.dma_start(bias_col, A["bias_col"]).then_inc(b2_in, 16)
            sp.dma_start(glu_col, A["glu_col"]).then_inc(b2_in, 16)
            sp.dma_start(taps2, A["conv_taps_2"].rearrange("p (t k) -> p t k", k=3)).then_inc(b2_in, 16)
            wait_full(sp, last_ff, 23)
            sp.dma_start(s_lr, A["lam_re"]).then_inc(ssm_in, 16)
            sp.dma_start(s_li, A["lam_im"]).then_inc(ssm_in, 16)
            sp.dma_start(s_x, A["log_dt"].partition_broadcast(SSM_P)).then_inc(ssm_in, 16)
            for dst, name in ((b_re, "b_re"), (b_im, "b_im"), (c_re, "c_re"), (c_im, "c_im")):
                sp.dma_start(dst, A[name]).then_inc(ssm_in, 16)
            sp.dma_start(iota, A["counts"].partition_broadcast(SSM_P)).then_inc(ssm_in, 16)
            sp.dma_start(d_row, A["ssm_d"].partition_broadcast(P)).then_inc(ssm_in, 16)
            sp.dma_start(u_row, A["b_in"].rearrange("(a n) -> a n", a=1)[0, 0:W2].partition_broadcast(P)
                         ).then_inc(ssm_in, 16)
            sp.wait_ge(norm_rows, 24)
            sp.dma_start(gain, A["ln1_g"].partition_broadcast(P)).then_inc(gain_in, 16)
            sp.dma_start(shift, A["ln1_b"].partition_broadcast(P)).then_inc(gain_in, 16)
            wait_full(sp, G_U, 7)
            for r in range(2):
                sp.dma_start(hc_slab[r], wi2[:, :, 512 * (r + 1):512 * (r + 1) + P]).then_inc(hc_in[r], 16)

            def ssm_moves(i, last):
                for r in range(2):
                    start, at = at_round(G_SSM + SSM_STEP * r, i, SSM_ROUND)
                    wait_full(sp, start, S_HC + 1, **at)
                    if not last:
                        sp.dma_start(hc_slab[r], wi2[:, :, bass.ds(i * P + (512 * (r + 1) + P), P)]
                                     ).then_inc(hc_in[r], 16)
                    wait_drained(sp, start, S_KALL, **at)
                    for lag in range(SUB):
                        rows = slice(SSM_C * lag, SSM_C * (lag + 1))
                        sp.dma_start(toep[rows, :, SSM_C * lag:P], kall[:, :, 0:P - SSM_C * lag]).then_inc(toep_in, 16)
            rounds(sp, SSM_ROUNDS // 2, ssm_moves)
            last_ssm = G_YT - SSM_STEP
            sp.dma_start(ring[0][:, 0:4, :], A["glu_w"].rearrange("(k p) n -> p k n", p=P)).then_inc(slab_in[0], 16)
            for g in range(GE):
                wait_drained(sp, last_ssm, S_Y + g)
            sp.dma_start(b_slab, wi2[:, :, 1536:2048]).then_inc(slab_in[1], 16)
            sp.wait_ge(conv2_done, 1)
            wsv = A["w_ssm_out"].rearrange("(k p) (n c) -> p k n c", p=P, c=4)
            wcv = A["w_conv_out"].rearrange("(k p) (n c) -> p k n c", p=P, c=4)
            wov = A["w_o"].rearrange("(k p) n -> p k n", p=P)
            sp.dma_start(wo_first[0], wov[:, 0:6, 0:512]).then_inc(wo_in, 16)
            sp.dma_start(wo_first[1], wov[:, 6:8, 0:512]).then_inc(wo_in, 16)
            with sp.Fori(0, MRG_ROUNDS) as i:
                for ft in range(2):
                    wait_full(sp, G_MRG - MRG_ROUND, 8 * ft + 5, i, MRG_ROUND)
                    for n in range(2):
                        c0 = P * ft + 256 * n
                        sp.dma_start(ring[1][:, :, c0:c0 + P], wi2[:, :, bass.ds(i * 256 + (2048 + 1024 * n + P * ft), P)]
                                     ).then_inc(mrg_in[ft], 16)
                    wait_full(sp, G_MRG - MRG_ROUND, 8 * ft + 7, i, MRG_ROUND)
                    for n, src in enumerate((wsv, wcv)):
                        c0 = P * ft + 256 * n
                        sp.dma_start(ring[0][:, 0:4, c0:c0 + P].rearrange("p k (n c) -> p k n c", c=4),
                                     src[:, :, bass.ds(i * 64 + 32 * ft, 32), :]).then_inc(mrg_in[ft], 16)
            last_mrg = G_MRG + (MRG_ROUNDS - 1) * MRG_ROUND
            wait_full(sp, last_mrg, 13)
            sp.dma_start(ring[1], wov[:, :, 512:1024]).then_inc(slab_in[1], 16)
            wgv = A["w_gate"].rearrange("(k p) (r n) -> p k r n", p=P, n=P)
            wuv = A["w_up"].rearrange("(k p) (r n) -> p k r n", p=P, n=P)
            wdv = A["w_down"].rearrange("(r k p) n -> p r k n", k=2, p=P)

            def f2_load(q, i):
                if q < 2:
                    dst = wraw2[q].rearrange("p (k n) -> p k n", n=256)
                    for n, src in enumerate((wgv, wuv)):
                        sp.dma_start(dst[:, :, P * n:P * n + P], src[:, :, bass.ds(i * 2 + q, 1), :]
                                     ).then_inc(raw2_in[q], 16)
                else:
                    sp.dma_start(wraw2[2].rearrange("p (k n) -> p k n", n=D), wdv[:, bass.ds(i, 1), :, :]
                                 ).then_inc(raw2_in[2], 16)

            def f2_loads(i, last):
                for q in range(3):
                    sp.wait_ge(v_lo, i * 3 + q + 1)
                    if not last:
                        f2_load(q, i + 1)

            sp.wait_ge(merged_rows, 8 + 4 * MRG_ROUNDS)
            f2_load(0, 0)
            wait_full(sp, G_WO, 7)
            f2_load(1, 0)
            f2_load(2, 0)
            rounds(sp, F2_ROUNDS, f2_loads)
            sp.wait_ge(ln_rows, 8)
            sp.dma_start(gain, A["ln2_g"].partition_broadcast(P)).then_inc(gain_in, 16)
            sp.dma_start(shift, A["ln2_b"].partition_broadcast(P)).then_inc(gain_in, 16)
            ov = out.rearrange("(p j) d -> p j d", j=NT)
            for j in range(NT):
                sp.wait_ge(ln_rows, 8 + j + 1)
                sp.dma_start(ov[:, j, :], X[:, j, :]).then_inc(out_done, 16)
            sp.wait_ge(out_done, 16 * NT)

        @block.tensor
        def _(pe):
            def turn(dst, src):
                return nc.tensor.transpose(dst, src, ident)

            def rows_to_features(start, src):
                for j in range(NT):
                    pe.wait_ge(norm_rows, norm_base[0] + j + 1)
                    for h in range(2):
                        b = wait_bank(pe, start, 2 * j + h)
                        for q in range(4):
                            k = 4 * h + q
                            mm = turn(ps[:, b, q * P:(q + 1) * P], src[:, j, k * P:(k + 1) * P])
                        mm.then_inc(full[b], 1)
                norm_base[0] += NT

            norm_base = [0]
            pe.wait_ge(consts_in, 16 * 10)
            rows_to_features(G_NORM1, xn)

            wait_drained(pe, G_NORM1, 14)
            wait_drained(pe, G_NORM1, 15)
            for b in range(6):
                wait_drained(pe, G_NORM1, 8 + b)

            def feature_tile(slot, ft, start, k0, kts=KT, src=H):
                for h in range(2):
                    b = wait_bank(pe, start, k0 + h)
                    for k in range(kts):
                        mm = nc.tensor.matmul(ps[:, b, :], ring[slot][:, k, ft * P:(ft + 1) * P],
                                              src[:, k, h * 512:h * 512 + 512], start=(k == 0), stop=(k == kts - 1))
                    mm.then_inc(full[b], 1)

            for ct in range(13):
                if ct < 12:
                    n = ct // 4
                    if ct % 4 == 0:
                        pe.wait_ge(slab_in[n % 2], 16 * (n // 2 + 1))
                    feature_tile(n % 2, ct % 4, G_QKV, dense_at(ct))
                if ct >= 1:
                    pe.wait_ge(silu_done, ct)
                    for h in range(2):
                        b = wait_bank(pe, G_QKV, turn_at(ct - 1) + h)
                        for q in range(4):
                            t = 4 * h + q
                            mm = turn(ps[:, b, q * P:(q + 1) * P], cv[(ct - 1) % 2][:, t * P:(t + 1) * P])
                        mm.then_inc(full[b], 1)

            def row_tiles(slot, start, k0, kts=KT, src=H):
                for t in range(NT):
                    b = wait_bank(pe, start, k0 + t)
                    for k in range(kts):
                        mm = nc.tensor.matmul(ps[:, b, :], src[:, k, t * P:(t + 1) * P], ring[slot][:, k, :],
                                              start=(k == 0), stop=(k == kts - 1))
                    mm.then_inc(full[b], 1)

            for n in range(3, 5):
                pe.wait_ge(slab_in[n % 2], 16 * (n // 2 + 1))
                row_tiles(n % 2, G_ROWS, 8 * (n - 3))
            pe.wait_ge(wgate_in, 16)
            b = wait_bank(pe, G_ROWS, 16)
            for t in range(NT):
                for k in range(KT):
                    mm = nc.tensor.matmul(ps[:, b, t * 32:(t + 1) * 32], H[:, k, t * P:(t + 1) * P], wgate[:, k, :],
                                          start=(k == 0), stop=(k == KT - 1))
            mm.then_inc(full[b], 1)

            pe.wait_ge(sguw_in, 16)
            for t in range(NT):
                pe.wait_ge(sgu_v, t + 1)
                b = wait_bank(pe, G_SGU, t)
                for g in range(SG):
                    mm = nc.tensor.matmul(ps[:, b, g * P:(g + 1) * P], sgu_w[:, g, :], SV[:, t, g * P:(g + 1) * P],
                                          start=True, stop=True)
                mm.then_inc(full[b], 1)
            pe.wait_ge(slab_in[1], 16 * 3)
            row_tiles(1, G_Z, 0)
            for t in range(NT):
                pe.wait_ge(sgu_o, t + 1)
                b = wait_bank(pe, G_SGT, t)
                for g in range(SG):
                    mm = turn(ps[:, b, g * P:(g + 1) * P], SU[:, t, g * P:(g + 1) * P])
                mm.then_inc(full[b], 1)

            pe.wait_ge(gdn_ready, 1)
            with pe.Fori(0, NT) as i:
                both, batches = range(2), [(d, h) for d in range(2) for h in range(2)]

                def bank(*key):
                    return wait_bank(pe, G_GDN, GDN_AT[key], i, GDN_ROUND)

                def ready(*key):
                    wait_drained(pe, G_GDN, GDN_AT[key], i, GDN_ROUND)

                def four(key, h, lhs, rhs, width=P):
                    b = bank(*key)
                    for q in range(4):
                        mm = nc.tensor.matmul(ps[:, b, q * width:(q + 1) * width], lhs(2 * q + h), rhs(2 * q + h),
                                              start=True, stop=True)
                    mm.then_inc(full[b], 1)

                for d in both:
                    tile = i if d == 0 else i * -1 + 7
                    b = bank("sums", d)
                    gt = gdec[:, bass.ds(tile, 1), 8 * d:8 * d + 8]
                    nc.tensor.matmul(ps[:, b, 0:8], masks[:, 2 * LEVELS + d, :], gt, start=True, stop=True)
                    nc.tensor.matmul(ps[:, b, 8:16], ones, gt, start=True, stop=True).then_inc(full[b], 1)
                for d, h in batches:
                    pe.wait_ge(gdn_go, i * 2 + d + 1)
                    four(("rows", d, h), h, lambda x: gnow[d][:, x:x + 1].broadcast_to([P, P]),
                         lambda x: masks[:, 2 * LEVELS + d, :])
                for n, name in enumerate(("keys", "queries")):
                    for d in both:
                        pe.wait_ge(gdn_stage, i * 2 + d + 1)
                        b = bank(name, d)
                        for q in range(4):
                            at = 8 * n + 2 * q
                            mm = turn(ps[:, b, q * P:(q + 1) * P], KQ[d][:, at:at + 2, :])
                        mm.then_inc(full[b], 1)
                for name, source, rhs in (("kk", "keys", KTr), ("kq", "queries", QTr)):
                    for d, h in batches:
                        ready(source, d)
                        four((name, d, h), h, lambda x: half(KTr[d], x), lambda x: half(rhs[d], x))
                for d, h in batches:
                    pe.wait_ge(gdn_t0, i * 4 + 2 * d + h + 1)
                    b = bank("U", 0, d, h)
                    for q in range(4):
                        mm = turn(ps[:, b, q * P:(q + 1) * P], Tm[d][:, 2 * q + h, :])
                    mm.then_inc(full[b], 1)
                for lv in range(1, LEVELS):
                    for d, h in batches:
                        pe.wait_ge(gdn_c, i * 24 + 4 * (lv - 1) + 2 * d + h + 1)
                        ready("U", lv - 1, d, h)
                        four(("Q", lv, d, h), h, lambda x: Cm[d][:, x, :], lambda x: Um[d][:, x, :])
                    if lv == LEVELS - 1:
                        for d, h in batches:
                            ready("Q", lv, d, h)
                            cols = level_columns(Qt[d], lv, 1 - d)
                            four(("U", lv, d, h), h, lambda x: Tm[d][:, x, :], lambda x: cols[:, x, :, :], HD)
                        continue
                    for d, h in batches:
                        ready("Q", lv, d, h)
                        cols = level_columns(Tm[d], lv, d)
                        four(("T", lv, d, h), h, lambda x: Qt[d][:, x, :], lambda x: cols[:, x, :, :], HD)
                    for d, h in batches:
                        ready("T", lv, d, h)
                        b = bank("U", lv, d, h)
                        for q in range(4):
                            mm = turn(ps[:, b, q * P:(q + 1) * P], Tm[d][:, 2 * q + h, :])
                        mm.then_inc(full[b], 1)
                    if lv == 1:
                        for d, h in batches:
                            wait_drained(pe, G_GDN - GDN_ROUND, GDN_AT[("kv", d)], i, GDN_ROUND)
                            four(("kS", d, h), h, lambda x: half(KTr[d], x), lambda x: half(S[d], x), HD)
                for d in both:
                    pe.wait_ge(gdn_vk, i * 2 + d + 1)
                for d, h in batches:
                    ready("U", LEVELS - 1, d, h)
                    four(("v", d, h), h, lambda x: Um[d][:, x, :], lambda x: Vb[d][:, x, :], HD)
                for d, h in batches:
                    pe.wait_ge(gdn_qd, i * 2 + d + 1)
                    ready("v", d, h)
                    b = bank("o", d, h)
                    for q in range(4):
                        x = 2 * q + h
                        nc.tensor.matmul(ps[:, b, q * HD:(q + 1) * HD], half(QdT[d], x), half(S[d], x),
                                         start=True, stop=False)
                        mm = nc.tensor.matmul(ps[:, b, q * HD:(q + 1) * HD], DTm[d][:, x, :], vnew[d][:, x, :],
                                              start=False, stop=True)
                    mm.then_inc(full[b], 1)
                for d in both:
                    b = bank("kv", d)
                    for x in range(HEADS):
                        lo = HD * (x % 2)
                        mm = nc.tensor.matmul(ps[lo:lo + HD, b, (x // 2) * HD:(x // 2 + 1) * HD], Kdec[d][:, x, :],
                                              vnew[d][:, x, :], start=True, stop=True)
                    mm.then_inc(full[b], 1)

            for t in range(NT):
                pe.wait_ge(mix_rows, t + 1)
                b = wait_bank(pe, G_MIXT, t)
                for q in range(4):
                    mm = turn(ps[:, b, q * P:(q + 1) * P], O[:, t, q * P:(q + 1) * P])
                mm.then_inc(full[b], 1)
            for t in range(NT):
                wait_drained(pe, G_MIXT, t)
            for n in range(2):
                pe.wait_ge(slab_in[n], 16 * 4)
                row_tiles(n, G_WOUT, 8 * n, src=mixT)

            rows_to_features(G_NORM2, xn)
            for k in range(8, 16):
                wait_drained(pe, G_NORM2, k)
            def split_product(out_ap, stationary, moving, kts):
                for k in range(kts):
                    for n, (a, c) in enumerate(HI_LO):
                        mm = nc.tensor.matmul(out_ap, stationary(a, k), moving(c, k), start=(k == 0 and n == 0),
                                              stop=(k == kts - 1 and n == 2))
                return mm

            def ff_round(i, last):
                start, at = at_round(G_FF, i, FF_ROUND)
                for ft in range(4):
                    if ft % 2 == 0:
                        pe.wait_ge(w_lo, i * 4 + ft // 2 + 1)
                    wv = [w.ap().rearrange("p (k n) -> p k n", n=256) for w in ws[ft // 2]]
                    for h in range(2):
                        b = wait_bank(pe, start, 2 * ft + h, **at)
                        cols = slice((ft % 2) * P, (ft % 2) * P + P)
                        split_product(ps[:, b, :], lambda a, k: wv[a][:, k, cols],
                                      lambda a, k: Hs[a][:, k, h * 512:h * 512 + 512], KT).then_inc(full[b], 1)
                for h in range(2):
                    pe.wait_ge(w_lo, i * 4 + 2 + h + 1)
                    wv = [w.ap().rearrange("p (k n) -> p k n", n=512) for w in ws[h]]
                    for t in range(NT):
                        if h == 0 and t % 4 == 0:
                            for k in range(t // 4, 8, 2):
                                wait_drained(pe, start, k, **at)
                        b = wait_bank(pe, start, 8 + 8 * h + t, **at)
                        split_product(ps[:, b, :], lambda a, k: ffs[a][:, k, t * P:(t + 1) * P],
                                      lambda a, k: wv[a][:, k, :], 4).then_inc(full[b], 1)
            rounds(pe, FF_ROUNDS, ff_round)
            rows_to_features(G_NORM3, X)
            for k in range(8, 16):
                wait_drained(pe, G_NORM3, k)

            def product(start, k0, out_ap, terms, i=None, per=0):
                b = wait_bank(pe, start, k0, i, per)
                for n, (lhs, rhs) in enumerate(terms):
                    mm = nc.tensor.matmul(out_ap(b), lhs, rhs, start=(n == 0), stop=(n == len(terms) - 1))
                mm.then_inc(full[b], 1)

            pe.wait_ge(slab_in[0], 16 * 5)
            row_tiles(0, G_U, 0)
            pe.wait_ge(ssm_pre, 1)

            def ssm_step(i, r):
                def bank(k):
                    return wait_bank(pe, G_SSM, SSM_STEP * r + k, i, SSM_ROUND)

                def ready(k):
                    wait_drained(pe, G_SSM, SSM_STEP * r + k, i, SSM_ROUND)

                pe.wait_ge(hc_in[r], i * 16 + 16)
                for h in range(2):
                    b = bank(S_HC + h)
                    for k in range(KT):
                        mm = nc.tensor.matmul(ps[:, b, :], hc_slab[r][:, k, :], H[:, k, h * 512:h * 512 + 512],
                                              start=(k == 0), stop=(k == KT - 1))
                    mm.then_inc(full[b], 1)
                pe.wait_ge(ssm_w, i * 2 + r + 1)
                for n, src in enumerate((wt_re, wt_im)):
                    b = bank(S_WT + n)
                    for g in range(GE):
                        mm = nc.tensor.matmul(ps[:, b, g * SSM_P:(g + 1) * SSM_P], src[:, g, :],
                                              ident[0:SSM_P, 0:SSM_P], start=True, stop=True)
                    mm.then_inc(full[b], 1)
                b = bank(S_KALL)
                for g in range(GE):
                    nc.tensor.matmul(ps[:, b, g * P:(g + 1) * P], bst[:, 0, SSM_C * g:SSM_C * g + P], v_re[:, g, 0:P],
                                     start=True, stop=False)
                    mm = nc.tensor.matmul(ps[:, b, g * P:(g + 1) * P], bst[:, 1, SSM_C * g:SSM_C * g + P], v_im[:, g, 0:P],
                                          start=False, stop=True)
                mm.then_inc(full[b], 1)
                pe.wait_ge(ssm_u, i * 2 + r + 1)
                b = bank(S_UT)
                for g in range(GE):
                    mm = turn(ps[:, b, g * P:(g + 1) * P], Uq[:, g, :])
                mm.then_inc(full[b], 1)
                for n, wl in enumerate((wl_re, wl_im)):
                    ready(S_WT + n)
                    ready(S_UT)
                    b = bank(S_W + n)
                    for g in range(GE):
                        mm = nc.tensor.matmul(ps[0:SSM_P, b, g * P:(g + 1) * P], wl[:, g, :], uT[:, g, :],
                                              start=True, stop=True)
                    mm.then_inc(full[b], 1)
                pe.wait_ge(toep_in, i * (32 * SUB) + (16 * SUB * (r + 1) + 16))
                pe.wait_ge(ssm_state, i * 2 + r + 1)
                for g in range(GE):
                    b = bank(S_Y + g)
                    o = ps[:, b, 0:P]
                    nc.tensor.matmul(o, uT[:, g, :], toep[:, g, :], start=True, stop=False)
                    nc.tensor.matmul(o, d_re[:, g, :], v_re[:, g, SSM_C:SSM_C + P], start=False, stop=False)
                    mm = nc.tensor.matmul(o, d_im[:, g, :], v_im[:, g, SSM_C:SSM_C + P], start=False, stop=True)
                    mm.then_inc(full[b], 1)
            with pe.Fori(0, SSM_ROUNDS // 2) as i:
                for r in range(2):
                    ssm_step(i, r)
            for g in range(GE):
                wait_drained(pe, G_YT - SSM_STEP, S_Y + g)
            for j in range(NT):
                b = wait_bank(pe, G_YT, j)
                for q in range(4):
                    mm = turn(ps[:, b, q * P:(q + 1) * P], U[:, j, q * P:(q + 1) * P])
                mm.then_inc(full[b], 1)
            pe.wait_ge(slab_in[0], 16 * 6)
            for j in range(NT):
                wait_drained(pe, G_YT, j)
            for ft in range(4):
                feature_tile(0, ft, G_GLU, 2 * ft, kts=4, src=gT)
            pe.wait_ge(slab_in[1], 16 * 5)
            for ft in range(WT):
                for h in range(2):
                    product(G_B, 2 * ft + h, lambda b: ps[:, b, :],
                            [(b_slab[:, k, ft * P:ft * P + P], H[:, k, h * 512:h * 512 + 512]) for k in range(KT)])
            for k in range(8):
                wait_drained(pe, G_GLU, k)
            for k in range(8):
                wait_drained(pe, G_B, k)
            with pe.Fori(0, MRG_ROUNDS) as i:
                for ft in range(2):
                    pe.wait_ge(mrg_in[ft], i * 64 + 64)
                    for h in range(2):
                        hc = slice(512 * h, 512 * h + 512)
                        k0 = 4 * (2 * ft + h)
                        ca = slice(ft * P, ft * P + P)
                        cb = slice(256 + ft * P, 256 + ft * P + P)
                        for n, (slot, cols, src, kts) in enumerate(((1, ca, H, 8), (1, cb, H, 8),
                                                                    (0, ca, YA, 4), (0, cb, BZ, 4))):
                            product(G_MRG, k0 + n, lambda b: ps[:, b, :],
                                    [(ring[slot][:, k, cols], src[:, k, hc]) for k in range(kts)], i, MRG_ROUND)
            for k in range(3, 16, 4):
                wait_drained(pe, last_mrg, k)
            pe.wait_ge(merged_rows, 8 + 4 * MRG_ROUNDS)
            pe.wait_ge(wo_in, 32)
            for t in range(NT):
                product(G_WO, t, lambda b: ps[:, b, :],
                        [(M[:, k, t * P:(t + 1) * P], wo_first[k // 6][:, k % 6, :]) for k in range(KT)])
            pe.wait_ge(slab_in[1], 16 * 6)
            row_tiles(1, G_WO, 8, src=M)

            def ln_rows_to_features(start):
                for j in range(NT):
                    pe.wait_ge(ln_rows, j + 1)
                    for h in range(2):
                        b = wait_bank(pe, start, 2 * j + h)
                        for q in range(4):
                            k = 4 * h + q
                            mm = turn(ps[:, b, q * P:(q + 1) * P], X[:, j, k * P:(k + 1) * P])
                        mm.then_inc(full[b], 1)
            ln_rows_to_features(G_LN1)
            for k in range(8, 16):
                wait_drained(pe, G_LN1, k)
            def f2_round(i, last):
                start, at = at_round(G_F2, i, F2_ROUND)
                for ft in range(2):
                    pe.wait_ge(v_lo, i * 3 + ft + 1)
                    wv = [w.ap().rearrange("p (k n) -> p k n", n=256) for w in ws2[ft]]
                    for h in range(2):
                        for n in range(2):
                            b = wait_bank(pe, start, 4 * ft + 2 * h + n, **at)
                            split_product(ps[:, b, :], lambda a, k: wv[a][:, k, P * n:P * n + P],
                                          lambda a, k: Hs[a][:, k, 512 * h:512 * h + 512], KT).then_inc(full[b], 1)
                pe.wait_ge(v_lo, i * 3 + 3)
                wv = [w.ap().rearrange("p (k n) -> p k n", n=D) for w in ws2[2]]
                for t in range(NT):
                    if t % 4 == 0:
                        for k in range(1 + t // 2, 8, 4):
                            wait_drained(pe, start, k, **at)
                    for h in range(2):
                        b = wait_bank(pe, start, 8 + 2 * t + h, **at)
                        split_product(ps[:, b, :], lambda a, k: hids[a][:, k, t * P:(t + 1) * P],
                                      lambda a, k: wv[a][:, k, 512 * h:512 * h + 512], 2).then_inc(full[b], 1)
            rounds(pe, F2_ROUNDS, f2_round)

        @block.scalar
        def _(act):
            steps = [0]

            def then(ins):
                ins.then_inc(act_step, 1)
                steps[0] += 1
                act.wait_ge(act_step, steps[0])

            def square_sums(src, waits, junk=None):
                junk = xn if junk is None else junk
                for j in range(NT):
                    waits(j)
                    nc.scalar.activation(junk[:, j, :], src[:, j, :], ACT.Square,
                                         accum_out=ssum[:, j:j + 1]).then_inc(norm_sums, 1)

            asked = [0]

            def root(n):
                asked[0] += 1
                act.wait_ge(root_ask, asked[0])
                nc.scalar.activation(rs_root[:, 0:n], rs_arg[:, 0:n], ACT.Sqrt).then_inc(root_done, 1)

            def copy_features(start, dst_of):
                for j in range(NT):
                    for h in range(2):
                        b = wait_full(act, start, 2 * j + h)
                        nc.scalar.copy(dst_of(j, h), ps[:, b, :].rearrange("p (k c) -> p k c", c=P)
                                       ).then_inc(drained[b], 1)

            def natural(j, h):
                return H[:, 4 * h:4 * h + 4, :].rearrange("p k (c j) -> p k c j", j=8)[:, :, :, j]

            def strided(j, h):
                return H[:, 4 * h:4 * h + 4, j * P:(j + 1) * P]

            square_sums(X, lambda j: act.wait_ge(x_in, 32))
            root(NT)
            copy_features(G_NORM1, natural)

            act.wait_ge(pads_set, 1)
            def raw_half(ct, h):
                if ct < 12:
                    if ct >= 2 and h == 0:
                        act.wait_ge(conv_done, ct - 1)
                    b = wait_full(act, G_QKV, dense_at(ct) + h)
                    nc.scalar.copy(raw[ct % 2][:, 2 + 512 * h:514 + 512 * h], ps[:, b, :]).then_inc(drained[b], 1)

            for ct in range(13):
                raw_half(ct, 0)
                if ct >= 1:
                    act.wait_ge(conv_done, ct)
                    nc.scalar.activation(cv[(ct - 1) % 2], cv[(ct - 1) % 2], ACT.Silu).then_inc(silu_done, 1)
                raw_half(ct, 1)
                if ct >= 1:
                    c = ct - 1
                    for h in range(2):
                        b = wait_full(act, G_QKV, turn_at(c) + h)
                        nc.scalar.copy(QKV[:, 4 * h:4 * h + 4, c * P:(c + 1) * P],
                                       ps[:, b, :].rearrange("p (t c) -> p t c", c=P)).then_inc(drained[b], 1)
            root(128)

            def activated_rows(start, k0, dst, fn):
                for t in range(NT):
                    b = wait_full(act, start, k0 + t)
                    nc.scalar.activation(dst[:, t, :], ps[:, b, :], fn).then_inc(drained[b], 1)

            activated_rows(G_ROWS, 0, SV, ACT.Gelu)
            root(NT * SG)
            activated_rows(G_ROWS, 8, SU, ACT.Gelu)
            act.wait_ge(gate_in, 1)
            nc.scalar.activation(gbeta, graw[:, :, 0:16], ACT.Sigmoid).then_inc(gate_out, 1)
            nc.scalar.activation(alog_row, alog_row, ACT.Exp).then_inc(gate_out, 1)
            then(nc.scalar.activation(gt1, gt1, ACT.Exp))
            nc.scalar.activation(gt1, gt1, ACT.Ln, bias=1.0).then_inc(gate_out, 1)
            root(NT * SG)
            activated_rows(G_Z, 0, Z, ACT.Silu)
            for t in range(NT):
                b = wait_full(act, G_SGT, t)
                nc.scalar.copy(mixT[:, 4:8, :].rearrange("p k (j c) -> p k j c", j=8)[:, :, :, 16 * t:16 * t + 16],
                               ps[:, b, :].rearrange("p (k c j) -> p k j c", c=16, j=8)).then_inc(drained[b], 1)

            with act.Fori(0, NT) as i:
                both, batches = range(2), [(d, h) for d in range(2) for h in range(2)]

                def arrived(*key):
                    return wait_full(act, G_GDN, GDN_AT[key], i, GDN_ROUND)

                def drain(key, dst):
                    b = arrived(*key)
                    nc.scalar.copy(dst, ps[:, b, 0:dst.shape[1] * dst.shape[2]]
                                   .rearrange("p (k c) -> p k c", c=dst.shape[2])).then_inc(drained[b], 1)

                for d in both:
                    tile = i if d == 0 else i * -1 + 7
                    act.wait_ge(gdn_go, i * 2 + d + 1)
                    row = QKV[:, bass.ds(tile, 1), :]
                    nc.scalar.copy(KQ[d][:, 0:HEADS, :], row[:, :, GW:2 * GW].rearrange("p t (h e) -> p (t h) e", e=HD))
                    nc.scalar.copy(KQ[d][:, HEADS:, :], row[:, :, 0:GW].rearrange("p t (h e) -> p (t h) e", e=HD)
                                   ).then_inc(gdn_stage, 1)
                for d in both:
                    act.wait_ge(gdn_exin, i * 2 + d + 1)
                    nc.scalar.activation(ex[d], exin[d], ACT.Exp).then_inc(gdn_ex, 1)
                for d, h in batches:
                    b = arrived("rows", d, h)
                    lo = HD * h
                    nc.scalar.activation(QdT[d][lo:lo + HD], ps[lo:lo + HD, b, :].rearrange("p (k c) -> p k c", c=P),
                                         ACT.Exp).then_inc(gdn_rexp, 1)
                for name, dst in (("keys", KTr), ("queries", QTr)):
                    for d in both:
                        drain((name, d), dst[d])
                for d, h in batches:
                    act.wait_ge(gdn_din, i * 4 + 2 * d + h + 1)
                    nc.scalar.activation(batch(Cm[d], h), batch(Cm[d], h), ACT.Exp)
                    nc.scalar.activation(batch(DTm[d], h), batch(DTm[d], h), ACT.Exp).then_inc(gdn_dexp, 1)
                for d, h in batches:
                    drain(("U", 0, d, h), batch(Um[d], h))
                for lv in range(1, LEVELS):
                    for name, dst in (("Q", Qt), ("U", Um)):
                        if (name, lv) == ("U", LEVELS - 1):
                            break
                        for d, h in batches:
                            drain((name, lv, d, h), batch(dst[d], h))
                for d, h in batches:
                    drain(("v", d, h), batch(vnew[d], h))

            root(NT * HEADS)
            for t in range(NT):
                b = wait_full(act, G_MIXT, t)
                nc.scalar.copy(mixT[:, 0:4, :].rearrange("p k (j c) -> p k j c", j=8)[:, :, :, 16 * t:16 * t + 16],
                               ps[:, b, :].rearrange("p (k c j) -> p k j c", c=16, j=8)).then_inc(drained[b], 1)

            def after_wout(j):
                wait_drained(act, G_WOUT, 8 + j)
            square_sums(X, after_wout)
            root(NT)
            def round_features(start, count):
                for j in range(NT):
                    for h in range(2):
                        b = wait_full(act, start, 2 * j + h)
                        nc.scalar.copy(Hs[0][:, 4 * h:4 * h + 4, j * P:(j + 1) * P],
                                       ps[:, b, :].rearrange("p (k c) -> p k c", c=P)).then_inc(feat_hi, 1)
            def round_slab(q, i):
                act.wait_ge(raw_in[q % 2], i * 32 + 16 * (q // 2 + 1))
                ff_slab_done(act, q - 2, i)
                nc.scalar.copy(ws[q % 2][0].ap(), wraw[q % 2]).then_inc(w_hi, 1)
            round_features(G_NORM2, 0)
            round_slab(0, 0)
            def ff_round(i, last):
                start, at = at_round(G_FF, i, FF_ROUND)
                for k in range(8):
                    b = wait_full(act, start, k, **at)
                    if isinstance(i, int) or k >= 2:
                        wait_drained(act, start, k - 2, **at)
                    else:
                        wait_drained(act, start - FF_ROUND, 6 + k, **at)
                    nc.scalar.activation(fft[k % 2], ps[:, b, :], ACT.Relu).then_inc(relu_done, 1)
                    act.wait_ge(relu_done, i * 8 + k + 1)
                    nc.scalar.activation(fft[k % 2], fft[k % 2], ACT.Square).then_inc(square_done, 1)
                    if k in (0, 4):
                        round_slab(1 + k // 4, i)
                for h in range(2):
                    wait_full(act, start, 8 + 8 * h, **at)
                    if h == 0:
                        round_slab(3, i)
                    elif not last:
                        round_slab(0, i + 1)
            rounds(act, FF_ROUNDS, ff_round)
            last_ff = G_FF + (FF_ROUNDS - 1) * FF_ROUND

            def after_ff(j):
                for h in range(2):
                    wait_drained(act, last_ff, 8 + 8 * h + j)
            square_sums(X, after_ff, junk=area(AT_H, NT, D))
            root(NT)
            copy_features(G_NORM3, strided)

            act.wait_ge(ssm_angle, 1)
            nc.scalar.activation(s_sin, s_th, ACT.Sin)
            nc.scalar.activation(s_half, s_th, ACT.Sin, scale=0.5).then_inc(ssm_sin, 1)
            act.wait_ge(b2_in, 48)

            def ssm_step(i, r):
                n = i * 2 + r

                def drain(k, dst, parts, width):
                    b = wait_full(act, G_SSM, SSM_STEP * r + k, i, SSM_ROUND)
                    nc.scalar.copy(dst, ps[0:parts, b, 0:GE * width].rearrange("p (k c) -> p k c", c=width)
                                   ).then_inc(drained[b], 1)
                act.wait_ge(ssm_angle, n + 2)
                nc.scalar.activation(e_im, tt4[0], ACT.Sin)
                nc.scalar.activation(e_re, tt4[0], ACT.Sin, scale=0.5).then_inc(ssm_trig, 1)
                if r == 0:
                    for h in range(2):
                        b = wait_full(act, G_SSM, S_HC + h, i, SSM_ROUND)
                        nc.scalar.activation(h_now[:, 512 * h:512 * h + 512], ps[:, b, :], ACT.Identity,
                                             bias=hc_bias[:, 0:1]).then_inc(drained[b], 1)
                drain(S_WT, wl_re, P, SSM_P)
                drain(S_WT + 1, wl_im, P, SSM_P)
                act.wait_ge(toep_in, i * (32 * SUB) + (16 * SUB * r + 16))
                drain(S_KALL, kall, SSM_C, P)
                drain(S_UT, uT, P, P)

            with act.Fori(0, SSM_ROUNDS // 2) as i:
                for h in range(2):
                    wait_drained(act, G_SSM - SSM_STEP, S_HC + h, i, SSM_ROUND)
                nc.scalar.copy(hc_bias[:, 0:1], bias_col[:, bass.ds(i, 1)])
                nc.scalar.copy(hc_bias[:, 1:2], bias_col[:, bass.ds(i + 4, 1)]).then_inc(hc_bias_set, 1)
                act.wait_ge(hc_bias_set, i + 1)
                for r in range(2):
                    ssm_step(i, r)
            for j in range(NT):
                b = wait_full(act, G_YT, j)
                nc.scalar.activation(gT[:, :, j * P:(j + 1) * P], ps[:, b, :].rearrange("p (k c) -> p k c", c=P),
                                     ACT.Gelu_apprx_tanh).then_inc(drained[b], 1)
            for k in range(8):
                b = wait_full(act, G_GLU, k)
                if k >= 4:
                    wait_drained(act, G_GLU, k - 4)
                nc.scalar.activation(sig[k % 4], ps[:, b, :], ACT.Sigmoid, bias=glu_col[:, k // 2:k // 2 + 1]
                                     ).then_inc(sig_done, 1)
            with act.Fori(0, MRG_ROUNDS) as i:
                wait_drained(act, G_MRG - MRG_ROUND, 13, i, MRG_ROUND)
                nc.scalar.copy(bias_now[:, 0, :], bias_col[:, bass.ds(i * 2 + 12, 2)])
                nc.scalar.copy(bias_now[:, 1, :], bias_col[:, bass.ds(i * 2 + 20, 2)]).then_inc(bias_set, 1)
                act.wait_ge(bias_set, i + 1)
                for ft in range(2):
                    for h in range(2):
                        k0 = 4 * (2 * ft + h)
                        r = 2 * ft + h
                        act.wait_ge(merged_rows, i * 4 + r + 7)
                        for n in range(2):
                            b = wait_full(act, G_MRG, k0 + n, i, MRG_ROUND)
                            nc.scalar.activation(sig[2 * (r % 2) + n], ps[:, b, :], ACT.Sigmoid,
                                                 bias=bias_now[:, n, ft:ft + 1]
                                                 ).then_inc(drained[b], 1)

            def layer_sums(waits, count):
                junk = area(AT_H, NT, D)
                for j in range(NT + 1):
                    if j < NT:
                        waits(j)
                        nc.scalar.activation(junk[:, j, :], X[:, j, :], ACT.Copy, accum_out=ssum[:, j:j + 1]
                                             ).then_inc(ln_sum, 1)
                    if j > 0:
                        act.wait_ge(ln_mean, (count - 1) * NT + j)
                        nc.scalar.activation(junk[:, j - 1, :], X[:, j - 1, :], ACT.Square, bias=mean[:, j - 1:j],
                                             accum_out=rstd[:, j - 1:j]).then_inc(ln_sq, 1)
                root(NT)
                act.wait_ge(ln_sq, count * NT)
                act.wait_ge(ln_mean2, count)
                for j in range(NT):
                    nc.scalar.activation(xn[:, j, :], X[:, j, :], ACT.Identity, bias=ssum[:, j:j + 1],
                                         scale=rs_y[:, j:j + 1]).then_inc(ln_scaled, 1)

            def round_slab2(q, i):
                act.wait_ge(raw2_in[q], i * (32 if q < 2 else 16) + (32 if q < 2 else 16))
                nc.scalar.copy(ws2[q][0].ap(), wraw2[q]).then_inc(v_hi, 1)

            for k in (14, 15):
                wait_full(act, last_mrg, k)
            round_slab2(0, 0)
            layer_sums(lambda j: wait_drained(act, G_WO, 8 + j), 1)
            round_features(G_LN1, 1)
            act.wait_ge(ln_rows, NT)
            for q in (1, 2):
                round_slab2(q, 0)

            def f2_round(i, last):
                start, at = at_round(G_F2, i, F2_ROUND)
                for q in range(4):
                    b = wait_full(act, start, 2 * q, **at)
                    if q >= 2:
                        wait_drained(act, start, 2 * q - 3, **at)
                    else:
                        wait_drained(act, start - F2_ROUND, 5 + 2 * q, **at)
                    nc.scalar.activation(hg[q % 2], ps[:, b, :], ACT.Silu).then_inc(drained[b], 1)
                    act.wait_ge(hid_f, i * 4 + q + 1)
                    nc.scalar.copy(hids[0][:, q // 2, 512 * (q % 2):512 * (q % 2) + 512], hg[q % 2]).then_inc(hid_hi, 1)
                if not last:
                    for q in range(3):
                        wait_full(act, start, (3, 7, 23)[q], **at)
                        round_slab2(q, i + 1)
            rounds(act, F2_ROUNDS, f2_round)

            def after_f2(j):
                for h in range(2):
                    wait_drained(act, last_f2, 8 + 2 * j + h)
            layer_sums(after_f2, 2)

        @block.vector
        def _(dve):
            V = nc.vector
            steps = [0]

            def then(ins):
                ins.then_inc(dve_step, 1)
                steps[0] += 1
                dve.wait_ge(dve_step, steps[0])

            asked = [0]

            def inverse_root(n, factor=1.0):
                asked[0] += 1
                arg, y, t = rs_arg[:, 0:n], rs_y[:, 0:n], rs_t[:, 0:n]
                dve.wait_ge(root_ask, asked[0])
                dve.wait_ge(root_done, asked[0])
                then(V.reciprocal(y, rs_root[:, 0:n]))
                then(V.tensor_tensor(t, y, y, ALU.mult))
                then(V.tensor_tensor(t, t, arg, ALU.mult))
                then(V.tensor_scalar(t, t, -0.5, 1.5, ALU.mult, ALU.add))
                then(V.tensor_tensor(y, y, t, ALU.mult))

            def rms_rows(src, dst, count):
                dve.wait_ge(gain_in, 16 * count)
                dve.wait_ge(norm_sums, count * NT)
                V.tensor_scalar(rs_arg[:, 0:NT], ssum, 1.0 / D, EPS, ALU.mult, ALU.add).then_inc(root_ask, 1)
                inverse_root(NT)
                for j in range(NT):
                    V.scalar_tensor_tensor(dst[:, j, :], src[:, j, :], rs_y[:, j:j + 1], gain,
                                           ALU.mult, ALU.mult).then_inc(norm_rows, 1)

            rms_rows(X, xn, 1)

            for b in range(2):
                V.memset(raw[b][:, 0:2], 0.0)
                pad = V.memset(raw[b][:, 1026:1028], 0.0)
            pad.then_inc(pads_set, 1)
            dve.wait_ge(pads_set, 1)
            dve.wait_ge(consts_in, 16 * 10)
            for ct in range(12):
                for h in range(2):
                    wait_drained(dve, G_QKV, dense_at(ct) + h)
                if ct >= 2:
                    wait_full(dve, G_QKV, turn_at(ct - 2) + 1)
                r, c = raw[ct % 2], cv[ct % 2]
                then(V.tensor_scalar(c, r[:, 0:SEQ], conv_taps[:, ct, 0:1], None, ALU.mult))
                for k in range(1, CONV_K):
                    ins = V.scalar_tensor_tensor(c, r[:, k:k + SEQ], conv_taps[:, ct, k:k + 1], c, ALU.mult, ALU.add)
                    if k < CONV_K - 1:
                        then(ins)
                ins.then_inc(conv_done, 1)

            s3 = sq.rearrange("p (h e) -> p h e", e=HD)
            for ct in range(8):
                for h in range(2):
                    wait_drained(dve, G_QKV, turn_at(ct) + h)
            wait_full(dve, G_QKV, 47)
            for t in range(NT):
                qk = QKV[:, t, 0:2 * GW].rearrange("p (h e) -> p h e", e=HD)
                then(V.tensor_tensor(s3, qk, qk, ALU.mult))
                then(V.tensor_reduce(vst[:, 0:16], s3, AX_X, ALU.add))
                ins = V.tensor_scalar(rs_arg[:, 16 * t:16 * t + 16], vst[:, 0:16], EPS, None, ALU.add)
            ins.then_inc(root_ask, 1)
            inverse_root(128)
            y3 = rs_y.rearrange("p (t h) -> p t h", h=16)
            then(V.tensor_scalar(y3[:, :, 0:8], y3[:, :, 0:8], HD ** -0.5, None, ALU.mult))
            for t in range(NT):
                qk = QKV[:, t, 0:2 * GW].rearrange("p (h e) -> p h e", e=HD)
                V.tensor_tensor(qk, qk, y3[:, t, :].unsqueeze(2).broadcast_to([P, 16, HD]), ALU.mult)

            def heads_of(rows, width):
                return rows.rearrange("p (g c) -> p g c", c=width)

            def group_sums(t, rows, width, count, scratch):
                r3 = heads_of(rows, width)
                then(V.tensor_tensor(scratch, r3, r3, ALU.mult))
                then(V.tensor_reduce(vst[:, 0:count], scratch, AX_X, ALU.add))
                return V.tensor_scalar(rs_arg[:, count * t:count * t + count], vst[:, 0:count], 1.0 / width, EPS,
                                       ALU.mult, ALU.add)

            def group_scale(t, rows, width, count):
                return V.tensor_tensor(heads_of(rows, width), heads_of(rows, width),
                                       rs_y[:, count * t:count * t + count].unsqueeze(2)
                                       .broadcast_to([P, count, width]), ALU.mult)

            sq4 = sq[:, 0:512].rearrange("p (g c) -> p g c", c=P)
            for t in range(NT):
                wait_drained(dve, G_ROWS, t)
                ins = group_sums(t, SV[:, t, :], P, SG, sq4)
            ins.then_inc(root_ask, 1)
            inverse_root(NT * SG)
            for t in range(NT):
                then(group_scale(t, SV[:, t, :], P, SG))
                V.tensor_tensor(heads_of(SV[:, t, :], P), heads_of(SV[:, t, :], P), sgu_vg, ALU.mult
                                ).then_inc(sgu_v, 1)
            b = wait_full(dve, G_ROWS, 16)
            gv = ps[:, b, 0:256].rearrange("p (t n) -> p t n", n=32)
            then(V.tensor_copy(graw, gv))
            then(V.tensor_tensor(gt2, graw[:, :, 16:32], dt_row.unsqueeze(1).broadcast_to([P, NT, 16]), ALU.add))
            then(V.tensor_scalar(gt1, gt2, -1.0, None, ALU.mult))
            then(V.tensor_tensor(gt1, gt1, gt2, ALU.min))
            V.tensor_copy(graw[:, 0:1, 0:1], graw[:, 0:1, 0:1]).then_inc(gate_in, 1)
            dve.wait_ge(gate_out, 3)
            then(V.scalar_tensor_tensor(gt2, gt2, 0.0, gt1, ALU.max, ALU.add))
            then(V.tensor_tensor(gt2, gt2, alog_row.unsqueeze(1).broadcast_to([P, NT, 16]), ALU.mult))
            then(V.tensor_scalar(gdec, gt2, -1.0, None, ALU.mult))
            V.tensor_copy(graw[:, 0:1, 0:1], graw[:, 0:1, 0:1]).then_inc(drained[b], 1)

            for t in range(NT):
                b = wait_full(dve, G_SGU, t)
                wait_drained(dve, G_ROWS, 8 + t)
                V.tensor_tensor(sq4, heads_of(ps[:, b, :], P), sgu_bt.unsqueeze(2).broadcast_to([P, SG, P]), ALU.add
                                ).then_inc(drained[b], 1)
                wait_drained(dve, G_SGU, t)
                u4 = heads_of(SU[:, t, :], P)
                then(V.tensor_tensor(u4, sq4, u4, ALU.mult))
                ins = group_sums(t, SU[:, t, :], P, SG, sq4)
            ins.then_inc(root_ask, 1)
            inverse_root(NT * SG)
            for t in range(NT):
                then(group_scale(t, SU[:, t, :], P, SG))
                V.tensor_tensor(heads_of(SU[:, t, :], P), heads_of(SU[:, t, :], P), sgu_og, ALU.mult
                                ).then_inc(sgu_o, 1)

            V.memset(SV.rearrange("p t c -> p (t c)"), 0.0)
            wait_full(dve, G_SGT, 7)
            V.memset(S[0].rearrange("p a b -> p (a b)"), 0.0)
            ins = V.memset(S[1].rearrange("p a b -> p (a b)"), 0.0)
            ins.then_inc(gdn_ready, 1)
            dve.wait_ge(gdn_ready, 1)

            with dve.Fori(0, NT) as i:
                own = [0]
                both, batches = range(2), [(d, h) for d in range(2) for h in range(2)]
                tris = [masks[:, 2 * LEVELS + d, :] for d in both]
                tiles = [i, i * -1 + 7]

                def chain(ins):
                    ins.then_inc(gdn_step, 1)
                    own[0] += 1
                    dve.wait_ge(gdn_step, i * GDN_OWN + own[0])

                def arrived(*key):
                    return wait_full(dve, G_GDN, GDN_AT[key], i, GDN_ROUND)

                def ready(*key):
                    wait_drained(dve, G_GDN, GDN_AT[key], i, GDN_ROUND)

                def view(b, c=P, n=4):
                    return ps[:, b, 0:n * c].rearrange("p (k c) -> p k c", c=c)

                def per_head(col, n=HEADS, width=HD):
                    return col.unsqueeze(2).broadcast_to([P, n, width])

                def level_mask(d, lv):
                    return masks[:, LEVELS * d + lv, :].unsqueeze(1).broadcast_to([P, 4, P])

                def rows_of(d, c0):
                    return QKV[:, bass.ds(tiles[d], 1), c0:c0 + GW].rearrange("p t (h e) -> p (t h) e", e=HD)

                def gates_of(x, d):
                    return x[:, bass.ds(tiles[d], 1), 8 * d:8 * d + 8].rearrange("p t h -> p (t h)")

                for d in both:
                    V.tensor_scalar(gnow[d], gates_of(gdec, d), 1.0, None, ALU.mult)
                    V.tensor_scalar(bege[d], gates_of(gbeta, d), 1.0, None, ALU.mult).then_inc(gdn_go, 1)
                for d in both:
                    b = arrived("sums", d)
                    V.tensor_copy(exin[d][:, 0:2, :], ps[:, b, 0:16].rearrange("p (a h) -> p a h", h=8)
                                  ).then_inc(drained[b], 1)
                    ready("sums", d)
                    V.tensor_tensor(exin[d][:, 2, :], exin[d][:, 1, :], exin[d][:, 0, :], ALU.subtract
                                    ).then_inc(gdn_exin, 1)
                dve.wait_ge(gdn_go, i * 2 + 2)
                for d, h in batches:
                    dve.wait_ge(gdn_rexp, i * 4 + 2 * d + h + 1)
                    b = arrived("rows", d, h)
                    hs = slice(h, HEADS, 2)
                    V.tensor_tensor(Rm[d][:, hs, :], view(b), per_head(exin[d][:, 0, hs], 4, P), ALU.subtract
                                    ).then_inc(drained[b], 1)
                    ready("rows", d, h)
                    V.tensor_scalar(Cm[d][:, hs, :], Rm[d][:, hs, :], -1.0, 0.0, ALU.mult, ALU.min)
                    V.tensor_scalar(DTm[d][:, hs, :], Rm[d][:, hs, :], 0.0, None, ALU.min).then_inc(gdn_din, 1)
                for d, h in batches:
                    hs = slice(h, HEADS, 2)
                    b = arrived("kk", d, h)
                    dve.wait_ge(gdn_dexp, i * 4 + 2 * d + h + 1)
                    V.tensor_tensor(Lm[d][:, hs, :], view(b), Cm[d][:, hs, :], ALU.mult).then_inc(drained[b], 1)
                    ready("kk", d, h)
                    chain(V.tensor_tensor(Lm[d][:, hs, :], Lm[d][:, hs, :], per_head(bege[d][:, hs], 4, P), ALU.mult))
                    chain(V.tensor_tensor(Tm[d][:, hs, :], Lm[d][:, hs, :], level_mask(d, 0), ALU.mult))
                    V.tensor_tensor(Tm[d][:, hs, :], ident.unsqueeze(1).broadcast_to([P, 4, P]), Tm[d][:, hs, :],
                                    ALU.subtract).then_inc(gdn_t0, 1)

                def cut(lv, d, h):
                    hs = slice(h, HEADS, 2)
                    V.tensor_tensor(Cm[d][:, hs, :], Lm[d][:, hs, :], level_mask(d, lv), ALU.mult).then_inc(gdn_c, 1)

                for d, h in batches:
                    cut(1, d, h)
                for d, h in batches:
                    hs = slice(h, HEADS, 2)
                    b = arrived("kq", d, h)
                    V.tensor_tensor(DTm[d][:, hs, :], view(b), DTm[d][:, hs, :], ALU.mult).then_inc(drained[b], 1)

                def between(lv):
                    if lv == 1:
                        for d in both:
                            V.tensor_tensor(Vb[d], rows_of(d, 2 * GW), per_head(bege[d]), ALU.mult)
                            dve.wait_ge(gdn_ex, i * 2 + d + 1)
                            chain(V.tensor_tensor(exin[d][:, 0, :], ex[d][:, 0, :], bege[d], ALU.mult))
                        for d, h in batches:
                            hs = slice(h, HEADS, 2)
                            b = arrived("kS", d, h)
                            V.tensor_tensor(kS[d][:, hs, :], view(b, HD), per_head(exin[d][:, 0, hs], 4), ALU.mult
                                            ).then_inc(drained[b], 1)
                    if lv == 2:
                        for d in both:
                            V.tensor_tensor(Kdec[d], rows_of(d, GW), per_head(ex[d][:, 2, :]), ALU.mult)
                        for d in both:
                            for h in range(2):
                                ready("kS", d, h)
                            V.tensor_tensor(Vb[d], Vb[d], kS[d], ALU.subtract).then_inc(gdn_vk, 1)
                    if lv == 3:
                        for d in both:
                            ready("kq", d, 1)
                            ready("kq", d, 0)
                            V.tensor_tensor(QdT[d], QdT[d], QTr[d], ALU.mult)
                            V.tensor_tensor(DTm[d], DTm[d], tris[d].unsqueeze(1).broadcast_to([P, HEADS, P]),
                                            ALU.mult).then_inc(gdn_qd, 1)
                    if lv == 4:
                        for d in both:
                            for x in range(2):
                                lo = HD * x
                                ins = V.tensor_copy(egl[d][lo:lo + HD, :], ex[d][lo:lo + HD, 1, :]
                                                    .rearrange("p (m a) -> p m a", a=2)[:, :, x])
                            chain(ins)

                for d in both:
                    ready("queries", d)
                for lv in range(1, LEVELS - 1):
                    for d, h in batches:
                        hs = slice(h, HEADS, 2)
                        b = arrived("T", lv, d, h)
                        cols = level_columns(Tm[d], lv, d)[:, hs, :, :]
                        V.tensor_tensor(cols, cols, ps[:, b, 0:4 * HD].rearrange("p (k n b) -> p k n b", k=4, b=1 << lv),
                                        ALU.subtract).then_inc(drained[b], 1)
                        cut(lv + 1, d, h)
                    between(lv)
                lv = LEVELS - 1
                for d, h in batches:
                    b = arrived("U", lv, d, h)
                    cols = level_columns(Um[d], lv, 1 - d)[:, slice(h, HEADS, 2), :, :]
                    V.tensor_tensor(cols, cols, ps[:, b, 0:4 * HD].rearrange("p (k n b) -> p k n b", k=4, b=1 << lv),
                                    ALU.subtract).then_inc(drained[b], 1)
                for d in both:
                    for h in range(2):
                        b = arrived("o", d, h)
                        orow = batch(O[:, bass.ds(tiles[d], 1), :].rearrange("p t (h e) -> p (t h) e", e=HD), h)
                        V.tensor_tensor(orow, orow, view(b, HD), ALU.add).then_inc(drained[b], 1)
                    chain(V.tensor_tensor(S[d], S[d], per_head(egl[d], 4), ALU.mult))
                for d in both:
                    b = arrived("kv", d)
                    V.tensor_tensor(S[d], S[d], view(b, HD), ALU.add).then_inc(drained[b], 1)
                assert own[0] == GDN_OWN, own[0]

            for d in range(2):
                for key in (("o", d, 0), ("o", d, 1), ("kv", d)):
                    wait_drained(dve, G_GDN + (NT - 1) * GDN_ROUND, GDN_AT[key])
            V.memset(vst, 0.0).then_inc(gdn_over, 1)
            dve.wait_ge(gdn_over, 1)
            sq8 = heads_of(sq[:, 0:512], HD)
            for t in range(NT):
                ins = group_sums(t, O[:, t, :], HD, HEADS, sq8)
            ins.then_inc(root_ask, 1)
            inverse_root(NT * HEADS)
            for t in range(NT):
                o3 = heads_of(O[:, t, :], HD)
                then(group_scale(t, O[:, t, :], HD, HEADS))
                then(V.tensor_tensor(o3, o3, gdn_gain.unsqueeze(1).broadcast_to([P, HEADS, HD]), ALU.mult))
                V.tensor_tensor(O[:, t, :], O[:, t, :], Z[:, t, :], ALU.mult).then_inc(mix_rows, 1)

            dve.wait_ge(xin_in, 32)
            for h in range(2):
                for t in range(NT):
                    b = wait_full(dve, G_WOUT, 8 * h + t)
                    V.tensor_tensor(X[:, t, 512 * h:512 * h + 512], xin[:, t, 512 * h:512 * h + 512], ps[:, b, :],
                                    ALU.add).then_inc(drained[b], 1)
            for t in range(NT):
                for h in range(2):
                    wait_drained(dve, G_WOUT, 8 * h + t)
            rms_rows(X, xn, 2)

            def rest_features(start, count):
                for j in range(NT):
                    for h in range(2):
                        dve.wait_ge(feat_hi, 16 * count + 2 * j + h + 1)
                        b = wait_full(dve, start, 2 * j + h)
                        part = (slice(None), slice(4 * h, 4 * h + 4), slice(j * P, (j + 1) * P))
                        V.tensor_tensor(Hs[1][part], ps[:, b, :].rearrange("p (k c) -> p k c", c=P),
                                        Hs[0][part].bitcast(F32), ALU.subtract).then_inc(drained[b], 1)

            def rest_slab(q, i):
                dve.wait_ge(w_hi, i * 4 + q + 1)
                V.tensor_tensor(ws[q % 2][1].ap(), wraw[q % 2], ws[q % 2][0].ap().bitcast(F32), ALU.subtract
                                ).then_inc(w_lo, 1)
            rest_features(G_NORM2, 0)
            rest_slab(0, 0)
            def ff_round(i, last):
                start, at = at_round(G_FF, i, FF_ROUND)
                for k in range(8):
                    dve.wait_ge(square_done, i * 8 + k + 1)
                    part = (slice(None), k // 2, slice((k % 2) * 512, (k % 2) * 512 + 512))
                    V.tensor_copy(ffs[0][part], fft[k % 2]).then_inc(ff_hi, 1)
                    dve.wait_ge(ff_hi, i * 8 + k + 1)
                    V.tensor_tensor(ffs[1][part], fft[k % 2], ffs[0][part].bitcast(F32), ALU.subtract
                                    ).then_inc(drained[where(start, k)[0]], 1)
                    if k in (0, 4):
                        rest_slab(1 + k // 4, i)
                for h in range(2):
                    for t in range(NT):
                        b = wait_full(dve, start, 8 + 8 * h + t, **at)
                        xs = X[:, t, 512 * h:512 * h + 512]
                        V.tensor_tensor(xs, xs, ps[:, b, :], ALU.add).then_inc(drained[b], 1)
                        if t == 0 and h == 0:
                            rest_slab(3, i)
                        elif t == 0 and not last:
                            rest_slab(0, i + 1)
            rounds(dve, FF_ROUNDS, ff_round)
            for k in range(8, 24):
                wait_drained(dve, G_FF + (FF_ROUNDS - 1) * FF_ROUND, k)
            rms_rows(X, X, 3)

            dve.wait_ge(ssm_in, 16 * 10)
            mul, add, sub = ALU.mult, ALU.add, ALU.subtract

            def tt2(out, a, b, op):
                then(V.tensor_tensor(out, a, b, op))

            def ts2(out, a, x, op0, y=None, op1=None):
                if op1 is None:
                    then(V.tensor_scalar(out, a, x, None, op0))
                else:
                    then(V.tensor_scalar(out, a, x, y, op0, op1))

            def exp_to(out, x):
                ts2(s_k, x, 1.0 / float(np.log(2.0)), mul, -1e6, ALU.max)
                ts2(s_k, s_k, ROUNDER, add)
                ts2(s_k, s_k, ROUNDER, sub)
                then(V.scalar_tensor_tensor(s_r, s_k, -LN2_HI, x, mul, add))
                then(V.scalar_tensor_tensor(s_r, s_k, -LN2_LO, s_r, mul, add))
                ts2(s_r, s_r, -1.0, ALU.max, 1.0, ALU.min)
                ts2(s_e, s_r, 1.0 / 5040, mul, 1.0 / 720, add)
                for c in (1.0 / 120, 1.0 / 24, 1.0 / 6, 0.5, 1.0, 1.0):
                    tt2(s_e, s_e, s_r, mul)
                    ts2(s_e, s_e, c, add)
                ts2(s_k, s_k, -127.0, ALU.max, 128.0, ALU.min)
                ts2(s_k, s_k, 127.0, add, 8388608.0, mul)
                then(V.tensor_copy(s_t1.bitcast(mybir.dt.int32), s_k))
                tt2(out, s_e, s_t1, mul)

            def reduce_angle(out, x, k, clamp_out=None):
                ts2(k, x, 1.0 / TWO_PI, mul, ROUNDER, add)
                ts2(k, k, ROUNDER, sub)
                then(V.scalar_tensor_tensor(out, k, -TWO_PI_HI, x, mul, add))
                then(V.scalar_tensor_tensor(out, k, -TWO_PI_LO, out, mul, add))
                return V.tensor_scalar(out, out, PI_IN, -PI_IN, ALU.min, ALU.max)

            exp_to(s_dt, s_x)
            tt2(s_x, s_lr, s_dt, mul)
            exp_to(s_mag, s_x)
            ts2(s_x, s_x, 8.0, mul)
            exp_to(s_r8, s_x)
            tt2(s_x, s_li, s_dt, mul)
            reduce_angle(s_th, s_x, s_k).then_inc(ssm_angle, 1)
            dve.wait_ge(ssm_sin, 1)
            tt2(s_cos, s_half, s_half, mul)
            ts2(s_cos, s_cos, -2.0, mul, 1.0, add)
            V.memset(pw_re[:, 0, :], 1.0)
            V.memset(pw_im[:, 0, :], 0.0)
            tt2(pw_re[:, 1, :], s_mag, s_cos, mul)
            tt2(pw_im[:, 1, :], s_mag, s_sin, mul)

            def power_rows(first, count, by):
                lo, hi = slice(1, 1 + count), slice(first, first + count)
                xr = pw_re[:, by, :].unsqueeze(1).broadcast_to([SSM_P, count, SSM_G])
                xi = pw_im[:, by, :].unsqueeze(1).broadcast_to([SSM_P, count, SSM_G])
                n = count * SSM_G
                t0, t1 = (tt[q][:, 0:n].rearrange("p (a b) -> p a b", b=SSM_G) for q in range(2))
                tt2(t0, pw_re[:, lo, :], xr, mul)
                tt2(t1, pw_im[:, lo, :], xi, mul)
                tt2(pw_re[:, hi, :], t0, t1, sub)
                tt2(t0, pw_re[:, lo, :], xi, mul)
                tt2(t1, pw_im[:, lo, :], xr, mul)
                tt2(pw_im[:, hi, :], t0, t1, add)

            power_rows(2, 1, 1)
            power_rows(3, 2, 2)
            power_rows(5, 4, 4)
            for j in range(SUB):
                then(V.tensor_copy(rv_re[:, j, :], pw_re[:, SUB - 1 - j, :]))
                then(V.tensor_copy(rv_im[:, j, :], pw_im[:, SUB - 1 - j, :]))
            ts2(s_x, s_th, 8.0, mul)
            then(reduce_angle(s_phi, s_x, s_k))
            tt2(s_den, s_lr, s_lr, mul)
            tt2(s_t1, s_li, s_li, mul)
            tt2(s_den, s_den, s_t1, add)
            then(V.reciprocal(s_den, s_den))
            ts2(s_nr, pw_re[:, 1, :], 1.0, sub)
            tt2(s_t1, s_nr, s_lr, mul)
            tt2(s_t2, pw_im[:, 1, :], s_li, mul)
            tt2(s_fr, s_t1, s_t2, add)
            tt2(s_fr, s_fr, s_den, mul)
            tt2(s_t1, pw_im[:, 1, :], s_lr, mul)
            tt2(s_t2, s_nr, s_li, mul)
            tt2(s_fi, s_t1, s_t2, sub)
            tt2(s_fi, s_fi, s_den, mul)
            t0, t1 = (tt[q][:, 0:512].rearrange("p (a b) -> p a b", b=SSM_C) for q in range(2))
            fr = s_fr.unsqueeze(2).broadcast_to([SSM_P, SSM_G, SSM_C])
            fi = s_fi.unsqueeze(2).broadcast_to([SSM_P, SSM_G, SSM_C])
            tt2(t0, b_re, fr, mul)
            tt2(t1, b_im, fi, mul)
            tt2(bb_re, t0, t1, sub)
            tt2(t0, b_im, fr, mul)
            tt2(t1, b_re, fi, mul)
            tt2(bb_im, t0, t1, add)
            V.memset(bst.rearrange("p a b -> p (a b)"), 0.0)
            V.memset(toep.rearrange("p a b -> p (a b)"), 0.0).then_inc(toep_in, 16)
            then(V.memset(not_first.rearrange("p a b -> p (a b)"), 1.0))
            then(V.memset(not_first[:, :, 0], 0.0))
            then(V.memset(d_re[:, :, 0], 0.0))
            then(V.memset(d_im[:, :, 0], 0.0))
            for j in range(NT):
                b = wait_full(dve, G_U, j)
                V.tensor_tensor(U[:, j, :], ps[:, b, :], u_row, add).then_inc(drained[b], 1)
            for j in range(NT):
                wait_drained(dve, G_U, j)
            V.memset(zp[:, :, 0:2 * P], 0.0)
            V.memset(s_t1, 0.0).then_inc(ssm_pre, 1)
            dve.wait_ge(ssm_pre, 1)
            dve.wait_ge(b2_in, 48)

            def ssm_step(i, r, own):
                n0 = i * 2 + r

                def chain(ins):
                    ins.then_inc(ssm_own, 1)
                    own[0] += 1
                    dve.wait_ge(ssm_own, i * SSM_OWN + own[0])

                def complex_product(out_re, out_im, a, b, t, conj=False, last_im=None):
                    (ar, ai), (br, bi) = a, b
                    V.tensor_tensor(t[0], ar, br, mul)
                    chain(V.tensor_tensor(t[1], ai, bi, mul))
                    chain(V.tensor_tensor(out_re, t[0], t[1], add if conj else sub))
                    V.tensor_tensor(t[0], ar, bi, mul)
                    chain(V.tensor_tensor(t[1], ai, br, mul))
                    return V.tensor_tensor(out_im, t[0], t[1], sub if conj else add)

                gs = bass.ds(n0 * GE, GE)

                def groups(x):
                    return x[:, :, gs].rearrange("p j g -> p g j")

                def lags(x, n):
                    return groups(x).unsqueeze(3).broadcast_to([SSM_P, GE, n, SSM_C])

                def chans(x, n):
                    return x[:, gs, :].unsqueeze(2).broadcast_to([SSM_P, GE, n, SSM_C])

                def split(x):
                    return x.rearrange("p g (j c) -> p g j c", c=SSM_C)

                def scratch(n):
                    return [tt[q][:, 0:GE * n * SSM_C].rearrange("p (g j c) -> p g j c", j=n, c=SSM_C)
                            for q in range(2)]

                chain(V.tensor_tensor(tt4[0], s_phi[:, gs].unsqueeze(2).broadcast_to([SSM_P, GE, P]),
                                      iota.unsqueeze(1).broadcast_to([SSM_P, GE, P]), mul))
                x, k = tt[0][:, 0:512], tt[1][:, 0:512]
                chain(V.tensor_scalar(k, x, 1.0 / TWO_PI, ROUNDER, mul, add))
                chain(V.tensor_scalar(k, k, ROUNDER, None, sub))
                chain(V.scalar_tensor_tensor(x, k, -TWO_PI_HI, x, mul, add))
                chain(V.scalar_tensor_tensor(x, k, -TWO_PI_LO, x, mul, add))
                V.tensor_scalar(x, x, PI_IN, -PI_IN, ALU.min, ALU.max).then_inc(ssm_angle, 1)
                V.tensor_tensor(r8, s_r8[:, gs].unsqueeze(2).broadcast_to([SSM_P, GE, P]), not_first, mul)
                Uv = U[:, :, bass.ds(n0 * (GE * SSM_C), GE * SSM_C)].rearrange("p j (g c) -> p g j c", c=SSM_C)
                Uqv = Uq.rearrange("p g (j c) -> p g j c", c=SSM_C)
                for g in range(GE):
                    ins = V.tensor_scalar(Uqv[:, g, :, :], Uv[:, g, :, :], 1.0, None, mul)
                ins.then_inc(ssm_u, 1)
                dve.wait_ge(ssm_u, n0 + 1)
                dve.wait_ge(ssm_trig, n0 + 1)
                chain(V.tensor_tensor(e_re, e_re, e_re, mul))
                chain(V.tensor_scalar(e_re, e_re, -2.0, 1.0, mul, add))
                t = scratch(9)
                chain(complex_product(split(v_re), split(v_im), (chans(c_re, 9), chans(c_im, 9)),
                                      (lags(pw_re, 9), lags(pw_im, 9)), t))
                chain(V.tensor_scalar(v_im, v_im, -1.0, None, mul))
                for n, x in enumerate((bb_re, bb_im)):
                    chain(V.tensor_scalar(bst[:, n, 0:GE * SSM_C].rearrange("p (g c) -> p g c", c=SSM_C), x[:, gs, :],
                                          1.0, None, mul))
                t = scratch(8)
                complex_product(split(wt_re), split(wt_im), (chans(bb_re, 8), chans(bb_im, 8)),
                                (lags(rv_re, 8), lags(rv_im, 8)), t).then_inc(ssm_w, 1)
                dve.wait_ge(ssm_w, n0 + 1)
                if r == 1:
                    dve.wait_ge(hc_bias_set, i + 1)
                    for h in range(2):
                        wait_drained(dve, G_SSM, S_HC + h, i, SSM_ROUND)
                        b = wait_full(dve, G_SSM, SSM_STEP + S_HC + h, i, SSM_ROUND)
                        V.scalar_tensor_tensor(zp[:, bass.ds(i, 1), 2 * P + 512 * h:2 * P + 512 * h + 512]
                                               .rearrange("p a b -> p (a b)"), ps[:, b, :], hc_bias[:, 1:2],
                                               h_now[:, 512 * h:512 * h + 512], add, mul).then_inc(drained[b], 1)
                w = []
                for n in range(2):
                    b = wait_full(dve, G_SSM, SSM_STEP * r + S_W + n, i, SSM_ROUND)
                    w.append(ps[0:SSM_P, b, :].rearrange("p (g c) -> p g c", c=P)[:, :, 0:P - 1])
                er, ei = e_re[:, :, 1:P], e_im[:, :, 1:P]
                t = [tt4[0][:, :, 1:P], tt4[1][:, :, 1:P]]
                dr, di = d_re[:, :, 1:P], d_im[:, :, 1:P]
                V.tensor_tensor(t[0], er, w[0], mul)
                chain(V.tensor_tensor(t[1], ei, w[1], mul))
                chain(V.tensor_tensor(dr, t[0], t[1], add))
                b1 = where(G_SSM, SSM_STEP * r + S_W + 1)[0]
                b0 = where(G_SSM, SSM_STEP * r + S_W)[0]
                V.tensor_tensor(t[0], er, w[1], mul).then_inc(drained[b1], 1)
                V.tensor_tensor(t[1], ei, w[0], mul).then_inc(drained[b0], 1)
                wait_drained(dve, G_SSM, SSM_STEP * r + S_W + 1, i, SSM_ROUND)
                wait_drained(dve, G_SSM, SSM_STEP * r + S_W, i, SSM_ROUND)
                chain(V.tensor_tensor(di, t[0], t[1], sub))

                def flat(x):
                    return x.rearrange("p a b -> p (a b)")
                V.tensor_tensor_scan(flat(s_re), flat(r8), flat(d_re), 0.0, mul, add)
                chain(V.tensor_tensor_scan(flat(s_im), flat(r8), flat(d_im), 0.0, mul, add))
                complex_product(d_re, d_im, (e_re, e_im), (s_re, s_im), tt4).then_inc(ssm_state, 1)
                dve.wait_ge(ssm_state, n0 + 1)
                dv = d_row[:, bass.ds(n0 * (GE * SSM_C), GE * SSM_C)].rearrange("p (g c) -> p g c", c=SSM_C)
                ytv = yt.rearrange("p g (j c) -> p g j c", c=SSM_C)
                chain(V.tensor_tensor(ytv, Uqv, dv.unsqueeze(2).broadcast_to([P, GE, SUB, SSM_C]), mul))
                for g in range(GE):
                    b = wait_full(dve, G_SSM, SSM_STEP * r + S_Y + g, i, SSM_ROUND)
                    chain(V.tensor_tensor(yt[:, g, :], yt[:, g, :], ps[:, b, 0:P], add))
                    V.tensor_scalar(Uv[:, g, :, :], ytv[:, g, :, :], 1.0, None, mul).then_inc(drained[b], 1)
                for g in range(GE):
                    wait_drained(dve, G_SSM, SSM_STEP * r + S_Y + g, i, SSM_ROUND)

            with dve.Fori(0, SSM_ROUNDS // 2) as i:
                own = [0]
                for r in range(2):
                    ssm_step(i, r, own)
                assert own[0] == SSM_OWN, own[0]

            for ft in range(WT):
                z = zp[:, ft, :]
                then(V.tensor_copy(z[:, 1:P], z[:, 8 * P:9 * P - 1]))
                then(V.tensor_copy(z[:, P + 1:2 * P], z[:, 9 * P:10 * P - 1]))
                o = BZ[:, ft, :]
                then(V.tensor_scalar(o, z[:, 0:SEQ], taps2[:, ft, 0:1], None, mul))
                then(V.scalar_tensor_tensor(o, z[:, P:P + SEQ], taps2[:, ft, 1:2], o, mul, add))
                ins = V.scalar_tensor_tensor(o, z[:, 2 * P:2 * P + SEQ], taps2[:, ft, 2:3], o, mul, add)
                if ft < WT - 1:
                    then(ins)
            ins.then_inc(conv2_done, 1)
            dve.wait_ge(conv2_done, 1)
            for k in range(8):
                dve.wait_ge(sig_done, k + 1)
                hs = slice(512 * (k % 2), 512 * (k % 2) + 512)
                if k == 0:
                    wait_full(dve, G_YT, 7)
                b = where(G_GLU, k)[0]
                V.tensor_tensor(YA[:, k // 2, hs], gT[:, k // 2, hs], sig[k % 4], mul).then_inc(drained[b], 1)
            for k in range(8):
                b = wait_full(dve, G_B, k)
                o = BZ[:, k // 2, 512 * (k % 2):512 * (k % 2) + 512]
                V.scalar_tensor_tensor(o, ps[:, b, :], bias_col[:, 8 + k // 2:9 + k // 2], o, add, mul
                                       ).then_inc(drained[b], 1)
            then(V.memset(s_t1, 0.0))
            for k in range(8):
                wait_drained(dve, G_GLU, k)
            V.memset(s_t2, 0.0).then_inc(merged_rows, 8)
            with dve.Fori(0, MRG_ROUNDS) as i:
                for ft in range(2):
                    for h in range(2):
                        r = 2 * ft + h
                        k0 = 4 * r
                        s0, s1 = sig[2 * (r % 2)], sig[2 * (r % 2) + 1]
                        for n, x in enumerate((s0, s1)):
                            wait_drained(dve, G_MRG, k0 + n, i, MRG_ROUND)
                            b = wait_full(dve, G_MRG, k0 + 2 + n, i, MRG_ROUND)
                            V.tensor_tensor(x, x, ps[:, b, :], mul).then_inc(drained[b], 1)
                        for n in range(2):
                            wait_drained(dve, G_MRG, k0 + 2 + n, i, MRG_ROUND)
                        V.tensor_tensor(M[:, bass.ds(i * 2 + ft, 1), 512 * h:512 * h + 512].rearrange("p a b -> p (a b)"),
                                        s0, s1, add).then_inc(merged_rows, 1)
            def row_mean(j, count):
                dve.wait_ge(ln_sum, (count - 1) * NT + j + 1)
                V.tensor_scalar(mean[:, j:j + 1], ssum[:, j:j + 1], -1.0 / D, None, mul).then_inc(ln_mean, 1)

            for h in range(2):
                for t in range(NT):
                    b = wait_full(dve, G_WO, 8 * h + t)
                    xs = X[:, t, 512 * h:512 * h + 512]
                    V.scalar_tensor_tensor(xs, xs, ALPHA, ps[:, b, :], mul, add).then_inc(drained[b], 1)
                    if h == 1 and t > 0:
                        row_mean(t - 1, 1)
            row_mean(NT - 1, 1)

            def layer_rows(count):
                dve.wait_ge(ln_sq, count * NT)
                V.tensor_scalar(rs_arg[:, 0:NT], rstd, 1.0 / D, LN_EPS, mul, add).then_inc(root_ask, 1)
                inverse_root(NT)
                V.tensor_tensor(ssum, mean, rs_y[:, 0:NT], mul).then_inc(ln_mean2, 1)
                dve.wait_ge(gain_in, 16 * (3 + 2 * count))
                for j in range(NT):
                    dve.wait_ge(ln_scaled, (count - 1) * NT + j + 1)
                    then(V.tensor_tensor(X[:, j, :], xn[:, j, :], gain, mul))
                    V.tensor_tensor(X[:, j, :], X[:, j, :], shift, add).then_inc(ln_rows, 1)

            def rest_slab2(q, i):
                dve.wait_ge(v_hi, i * 3 + q + 1)
                V.tensor_tensor(ws2[q][1].ap(), wraw2[q], ws2[q][0].ap().bitcast(F32), sub).then_inc(v_lo, 1)

            rest_slab2(0, 0)
            layer_rows(1)
            rest_features(G_LN1, 1)
            for q in (1, 2):
                rest_slab2(q, 0)
            dve.wait_ge(ln_rows, 8)
            for j in range(NT):
                wait_full(dve, G_LN1, 2 * j + 1)
                ins = V.tensor_scalar(X[:, j, :], X[:, j, :], ALPHA, None, mul)
            then(ins)

            def f2_round(i, last):
                start, at = at_round(G_F2, i, F2_ROUND)
                for q in range(4):
                    wait_drained(dve, start, 2 * q, **at)
                    b = wait_full(dve, start, 2 * q + 1, **at)
                    V.tensor_tensor(hg[q % 2], hg[q % 2], ps[:, b, :], mul).then_inc(hid_f, 1)
                    dve.wait_ge(hid_hi, i * 4 + q + 1)
                    part = (slice(None), q // 2, slice(512 * (q % 2), 512 * (q % 2) + 512))
                    V.tensor_tensor(hids[1][part], hg[q % 2], hids[0][part].bitcast(F32), sub).then_inc(drained[b], 1)
                for t in range(NT):
                    if not last and t == 1:
                        for q in range(2):
                            rest_slab2(q, i + 1)
                    for h in range(2):
                        b = wait_full(dve, start, 8 + 2 * t + h, **at)
                        xs = X[:, t, 512 * h:512 * h + 512]
                        V.tensor_tensor(xs, xs, ps[:, b, :], add).then_inc(drained[b], 1)
                    if last and t > 0:
                        row_mean(t - 1, 2)
                if last:
                    row_mean(NT - 1, 2)
                else:
                    rest_slab2(2, i + 1)
            rounds(dve, F2_ROUNDS, f2_round)
            for k in range(8, 24):
                wait_drained(dve, last_f2, k)
            layer_rows(2)


GDN_OWN = 14
SSM_OWN = 58
PI_IN = 3.1415925


def kernel(**inputs):
    import numpy as _np
    import concourse.bacc as _bacc
    from concourse import mybir as _mybir
    from concourse.bass_utils import run_bass_kernel_spmd as _run

    def c(a):
        return _np.ascontiguousarray(a)

    arrays = {n: c(inputs[n][0]) for n in ("x", "norm_mix", "w_in", "a_log_fwd", "dt_bias_fwd", "a_log_bwd",
                                           "dt_bias_bwd", "gdn_norm", "sgu_v_norm", "sgu_out_norm", "w_out",
                                           "norm_ffn", "w_ff1", "w_ff2")}
    arrays["norm_final"] = c(inputs["norm_final"])
    arrays["conv_wT"] = c(inputs["conv_w"][0].T)
    arrays["sgu_bT"] = c(inputs["sgu_b"][0].T)
    arrays["sgu_wT"] = c(_np.swapaxes(inputs["sgu_w"][0], 1, 2))
    arrays["shape_constants"] = shape_constants()
    for n in ("w_in", "glu_w", "w_ssm_out", "w_conv_out", "w_o", "ln1_g", "ln1_b", "w_gate", "w_up", "w_down",
              "ln2_g", "ln2_b", "ssm_d"):
        arrays[n if n != "w_in" else "w_in_2"] = c(inputs[n + "_2"][0])
    b_in = inputs["b_in_2"][0]
    arrays["b_in"] = c(b_in)
    arrays["bias_col"] = c(b_in[W2:].reshape(-1, P).T)
    arrays["glu_col"] = c(inputs["glu_b_2"][0].reshape(-1, P).T)
    arrays["conv_taps_2"] = c(inputs["conv_w_2"][0].T.reshape(WT, P, 3).transpose(1, 0, 2).reshape(P, WT * 3))
    arrays["lam_re"] = c(inputs["ssm_lambda_re_2"][0].T)
    arrays["lam_im"] = c(inputs["ssm_lambda_im_2"][0].T)
    arrays["log_dt"] = c(inputs["ssm_log_dt_2"][0])
    arrays["b_re"] = c(inputs["ssm_b_re_2"][0].transpose(1, 0, 2))
    arrays["b_im"] = c(inputs["ssm_b_im_2"][0].transpose(1, 0, 2))
    arrays["c_re"] = c(inputs["ssm_c_re_2"][0].transpose(2, 0, 1))
    arrays["c_im"] = c(inputs["ssm_c_im_2"][0].transpose(2, 0, 1))
    arrays["counts"] = _np.arange(P, dtype=_np.float32)

    nc = _bacc.Bacc("TRN2", target_bir_lowering=False, num_devices=1)
    A = {n: nc.dram_tensor(f"in_{n}", a.shape, _mybir.dt.from_np(a.dtype), kind="ExternalInput").ap()
         for n, a in arrays.items()}
    out = nc.dram_tensor("out_x", (SEQ, D), F32, kind="ExternalOutput").ap()
    build(nc, A, out, A["shape_constants"])
    r = _run(nc, [{f"in_{n}": a for n, a in arrays.items()}], core_ids=[0])
    return r.results[0]["out_x"].reshape(1, SEQ, D)
```
